# Optimizing a Trainium2 kernel written in Bass

```python
import math
import jax
import jax.numpy as jnp
from jax import lax
import numpy as np

D_MODEL = 1024
BATCH = 1
SEQ = 256
DEPTH = 2

PLE_DIM = 256
NORM_EPS = 1e-6
MASK_VALUE = -1e30

SWA_Q_HEADS = 8
SWA_KV_HEADS = 2
SWA_HEAD_DIM = 64
SWA_WINDOW = 128
ROT_DIM = SWA_HEAD_DIM // 4
ROPE_THETA = 500000.0

GLA_HEADS = 4
GLA_DK = 64
GLA_DV = 128
GLA_GATE_RANK = 16
GLA_GATE_NORM = 16.0
GLA_CHUNK = 64

GDN_HEADS = 4
GDN_DK = 128
GDN_DV = 128
GDN_CONV = 4
GDN_CHUNK = 64

N_BRANCH = 3

N_GROUPS = 4
EXPERTS_PER_GROUP = 8
N_EXPERTS = N_GROUPS * EXPERTS_PER_GROUP
EXPERT_FF = 512
TOP_K = 2
MOE_BLOCK = 128

SWA_Q = SWA_Q_HEADS * SWA_HEAD_DIM
SWA_KV = SWA_KV_HEADS * SWA_HEAD_DIM
GLA_K = GLA_HEADS * GLA_DK
GLA_V = GLA_HEADS * GLA_DV
GDN_K = GDN_HEADS * GDN_DK
GDN_V = GDN_HEADS * GDN_DV
GDN_QKV = 2 * GDN_K + GDN_V
IN_SPLITS = (SWA_Q, SWA_KV, SWA_KV,
             GLA_K, GLA_K, GLA_V, GLA_GATE_RANK, GLA_V,
             GDN_QKV, GDN_HEADS, GDN_HEADS, GDN_V,
             N_BRANCH * D_MODEL)
IN_DIM = sum(IN_SPLITS)
IN_OFFSETS = tuple(int(o) for o in np.cumsum(IN_SPLITS)[:-1])

kernel_name = 'hybrid_swa_gla_gdn_hmoe_ple'

def rmsnorm(x, g):
    xf = x.astype(jnp.float32)
    y = xf * lax.rsqrt(jnp.mean(xf * xf, axis=-1, keepdims=True) + NORM_EPS)
    return (y * g.astype(jnp.float32)).astype(x.dtype)

def l2norm(x):
    return x * lax.rsqrt(jnp.sum(x * x, axis=-1, keepdims=True) + NORM_EPS)

def rope_tables(positions):
    inv_freq = 1.0 / (ROPE_THETA ** (jnp.arange(0, ROT_DIM, 2, dtype=jnp.float32) / ROT_DIM))
    ang = positions.astype(jnp.float32)[..., None] * inv_freq
    return jnp.cos(ang)[:, :, None, :], jnp.sin(ang)[:, :, None, :]

def apply_partial_rope(x, cos, sin):
    half = ROT_DIM // 2
    x1 = x[..., :half].astype(jnp.float32)
    x2 = x[..., half:ROT_DIM].astype(jnp.float32)
    rot = jnp.concatenate([x1 * cos - x2 * sin, x2 * cos + x1 * sin], axis=-1).astype(x.dtype)
    return jnp.concatenate([rot, x[..., ROT_DIM:]], axis=-1)

def to_chunks(t, c):
    b, s = t.shape[0], t.shape[1]
    return jnp.moveaxis(t.reshape(b, s // c, c, *t.shape[2:]), 3, 1)

def from_chunks(t):
    b, h, nc, c, d = t.shape
    return jnp.moveaxis(t, 1, 3).reshape(b, nc * c, h, d)

def sliding_window_sink_attention(q, k, v, sinks):
    B, S, HQ, HD = q.shape
    HKV = k.shape[2]
    GQ = HQ // HKV
    W = SWA_WINDOW
    nb = S // W
    qb = q.reshape(B, nb, W, HKV, GQ, HD)

    def with_prev(t):
        tb = t.reshape(B, nb, W, HKV, HD)
        prev = jnp.concatenate([jnp.zeros_like(tb[:, :1]), tb[:, :-1]], axis=1)
        return jnp.concatenate([prev, tb], axis=2)

    kc, vc = with_prev(k), with_prev(v)
    s = jnp.einsum('bnqhgd,bnkhd->bnhgqk', qb, kc).astype(jnp.float32) * (HD ** -0.5)
    qi = jnp.arange(W)[:, None]
    kj = jnp.arange(2 * W)[None, :]
    band = (kj > qi) & (kj <= qi + W)
    not_first = jnp.arange(nb)[:, None, None] > 0
    mask = band[None] & (not_first | (kj >= W)[None])
    s = jnp.where(mask[None, :, None, None], s, MASK_VALUE)
    sink = sinks.astype(jnp.float32).reshape(1, 1, HKV, GQ, 1, 1)
    m = jnp.maximum(jnp.max(s, axis=-1, keepdims=True), sink)
    e = jnp.exp(s - m)
    prob = e / (jnp.sum(e, axis=-1, keepdims=True) + jnp.exp(sink - m))
    o = jnp.einsum('bnhgqk,bnkhd->bnqhgd', prob.astype(v.dtype), vc)
    return o.reshape(B, S, HQ * HD).astype(q.dtype)

def gla_attention(q, k, v, log_a):
    B, S, H, DK = q.shape
    DV = v.shape[-1]
    C = GLA_CHUNK
    q = to_chunks(q.astype(jnp.float32) * (DK ** -0.5), C)
    k = to_chunks(k.astype(jnp.float32), C)
    v = to_chunks(v.astype(jnp.float32), C)
    b = jnp.cumsum(to_chunks(log_a.astype(jnp.float32), C), axis=3)
    qe = q * jnp.exp(b)
    ke = k * jnp.exp(-b)
    causal = jnp.tril(jnp.ones((C, C), dtype=bool))
    att = jnp.where(causal, jnp.einsum('bhncd,bhnsd->bhncs', qe, ke), 0.0)
    o = jnp.einsum('bhncs,bhnse->bhnce', att, v)
    b_last = b[:, :, :, -1:]
    du = jnp.einsum('bhnsd,bhnse->bhnde', k * jnp.exp(b_last - b), v)
    decay = jnp.exp(b_last[:, :, :, 0])

    def step(state, inp):
        d, u = inp
        return d[..., None] * state + u, state

    s0 = jnp.zeros((B, H, DK, DV), jnp.float32)
    _, s_prev = lax.scan(step, s0, (jnp.moveaxis(decay, 2, 0), jnp.moveaxis(du, 2, 0)))
    o = o + jnp.einsum('bhncd,nbhde->bhnce', qe, s_prev)
    return from_chunks(o)

def gated_delta_rule(q, k, v, beta, g):
    B, S, H, DK = q.shape
    DV = v.shape[-1]
    C = GDN_CHUNK
    q = to_chunks(l2norm(q.astype(jnp.float32)) * (DK ** -0.5), C)
    k = to_chunks(l2norm(k.astype(jnp.float32)), C)
    v = to_chunks(v.astype(jnp.float32), C)
    beta = to_chunks(beta, C)
    G = jnp.cumsum(to_chunks(g, C), axis=-1)
    causal = jnp.tril(jnp.ones((C, C), dtype=bool))
    strict = jnp.tril(jnp.ones((C, C), dtype=bool), k=-1)
    diff = G[..., :, None] - G[..., None, :]
    decay = jnp.where(causal, jnp.exp(jnp.where(causal, diff, 0.0)), 0.0)
    kk = jnp.einsum('bhncd,bhnsd->bhncs', k, k)
    tmat = jnp.eye(C, dtype=jnp.float32) + jnp.where(strict, beta[..., None] * kk * decay, 0.0)
    rhs = jnp.concatenate([v * beta[..., None], k * (beta * jnp.exp(G))[..., None]], axis=-1)
    sol = lax.linalg.triangular_solve(tmat, rhs, left_side=True, lower=True, unit_diagonal=True)
    u, w = sol[..., :DV], sol[..., DV:]
    att = jnp.einsum('bhncd,bhnsd->bhncs', q, k) * decay
    q_dec = q * jnp.exp(G)[..., None]
    G_last = G[..., -1:]
    k_dec = k * jnp.exp(G_last - G)[..., None]
    chunk_decay = jnp.exp(G_last[..., 0])

    def step(state, inp):
        u_c, w_c, q_c, k_c, a_c, d_c = inp
        v_new = u_c - jnp.einsum('bhcd,bhde->bhce', w_c, state)
        o_c = jnp.einsum('bhcd,bhde->bhce', q_c, state) + jnp.einsum('bhcs,bhse->bhce', a_c, v_new)
        state = d_c[..., None, None] * state + jnp.einsum('bhcd,bhce->bhde', k_c, v_new)
        return state, o_c

    xs = (jnp.moveaxis(u, 2, 0), jnp.moveaxis(w, 2, 0), jnp.moveaxis(q_dec, 2, 0),
          jnp.moveaxis(k_dec, 2, 0), jnp.moveaxis(att, 2, 0), jnp.moveaxis(chunk_decay, 2, 0))
    s0 = jnp.zeros((B, H, DK, DV), jnp.float32)
    _, o = lax.scan(step, s0, xs)
    return from_chunks(jnp.moveaxis(o, 0, 2))

def gated_head_norm(o, g, r):
    B, S = o.shape[0], o.shape[1]
    on = rmsnorm(o, g).reshape(B, S, -1)
    return (on * jax.nn.silu(r.astype(jnp.float32))).astype(r.dtype)

def causal_depthwise_conv(x, w):
    return lax.conv_general_dilated(x, w[:, None, :], window_strides=(1,),
                                    padding=[(w.shape[0] - 1, 0)],
                                    dimension_numbers=('NWC', 'WIO', 'NWC'),
                                    feature_group_count=x.shape[-1])

def hierarchical_moe(h, w_coarse, b_coarse, w_fine, b_fine, w_gate_e, w_up_e, w_down_e):
    B, S, D = h.shape
    N = B * S
    M = N * TOP_K
    hf = h.reshape(N, D)
    group_prob = jax.nn.softmax((hf @ w_coarse + b_coarse).astype(jnp.float32), axis=-1)
    g_prob, g_idx = lax.top_k(group_prob, 1)
    fine = (hf @ w_fine + b_fine).astype(jnp.float32).reshape(N, N_GROUPS, EXPERTS_PER_GROUP)
    fine = jnp.take_along_axis(fine, g_idx[:, :, None], axis=1)[:, 0]
    e_prob, e_local = lax.top_k(jax.nn.softmax(fine, axis=-1), TOP_K)
    weight = g_prob * e_prob / jnp.sum(e_prob, axis=-1, keepdims=True)
    expert = (g_idx * EXPERTS_PER_GROUP + e_local).reshape(M).astype(jnp.int32)
    token = jnp.repeat(jnp.arange(N, dtype=jnp.int32), TOP_K)
    order = jnp.argsort(expert)
    e_sorted = expert[order]
    counts = jax.ops.segment_sum(jnp.ones((M,), jnp.int32), expert, num_segments=N_EXPERTS)
    starts = jnp.cumsum(counts) - counts
    padded = (counts + MOE_BLOCK - 1) // MOE_BLOCK * MOE_BLOCK
    pad_end = jnp.cumsum(padded)
    pad_start = pad_end - padded
    slot_sorted = pad_start[e_sorted] + jnp.arange(M, dtype=jnp.int32) - starts[e_sorted]
    slot = jnp.zeros((M,), jnp.int32).at[order].set(slot_sorted)
    n_slots = M + N_EXPERTS * MOE_BLOCK
    n_blocks = n_slots // MOE_BLOCK
    slot_token = jnp.full((n_slots,), N, jnp.int32).at[slot].set(token)
    block_start = jnp.arange(n_blocks, dtype=jnp.int32) * MOE_BLOCK
    block_expert = jnp.minimum(jnp.searchsorted(pad_end, block_start, side='right'), N_EXPERTS - 1)
    h_pad = jnp.concatenate([hf, jnp.zeros((1, D), hf.dtype)], axis=0)

    def run_block(args):
        tok, e = args
        xb = h_pad[tok]
        return (jax.nn.silu(xb @ w_gate_e[e]) * (xb @ w_up_e[e])) @ w_down_e[e]

    y_slots = lax.map(run_block, (slot_token.reshape(n_blocks, MOE_BLOCK), block_expert))
    y = y_slots.reshape(n_slots, D)[slot].reshape(N, TOP_K, D)
    out = jnp.einsum('nk,nkd->nd', weight, y.astype(jnp.float32))
    return out.reshape(B, S, D).astype(h.dtype)

def hybrid_layer(x, p_i, cos, sin, attn_norm, w_in, q_norm, k_norm, sinks, gla_wa2, gla_ba, gla_norm,
                 gdn_conv, gdn_a_log, gdn_dt_bias, gdn_norm, w_br_a, w_br_b, w_br_c, w_o,
                 ffn_norm, w_coarse, b_coarse, w_fine, b_fine, w_gate_e, w_up_e, w_down_e,
                 ple_norm, w_ple_gate, w_ple):
    B, S, D = x.shape
    h = rmsnorm(x, attn_norm)
    (a_q, a_k, a_v, b_q, b_k, b_v, b_lr, b_r, c_qkv, c_beta, c_a, c_g,
     gate_logits) = jnp.split(h @ w_in, IN_OFFSETS, axis=-1)
    a_q = apply_partial_rope(rmsnorm(a_q.reshape(B, S, SWA_Q_HEADS, SWA_HEAD_DIM), q_norm), cos, sin)
    a_k = apply_partial_rope(rmsnorm(a_k.reshape(B, S, SWA_KV_HEADS, SWA_HEAD_DIM), k_norm), cos, sin)
    y_a = sliding_window_sink_attention(a_q, a_k, a_v.reshape(B, S, SWA_KV_HEADS, SWA_HEAD_DIM), sinks)
    log_a = jax.nn.log_sigmoid((b_lr @ gla_wa2 + gla_ba).astype(jnp.float32)) / GLA_GATE_NORM
    o_b = gla_attention(b_q.reshape(B, S, GLA_HEADS, GLA_DK), b_k.reshape(B, S, GLA_HEADS, GLA_DK),
                        b_v.reshape(B, S, GLA_HEADS, GLA_DV), log_a.reshape(B, S, GLA_HEADS, GLA_DK))
    y_b = gated_head_norm(o_b, gla_norm, b_r)
    c_qkv = jax.nn.silu(causal_depthwise_conv(c_qkv, gdn_conv))
    c_q, c_k, c_v = jnp.split(c_qkv, (GDN_K, 2 * GDN_K), axis=-1)
    beta = jax.nn.sigmoid(c_beta.astype(jnp.float32))
    g = -jnp.exp(gdn_a_log.astype(jnp.float32)) * jax.nn.softplus(c_a.astype(jnp.float32) + gdn_dt_bias.astype(jnp.float32))
    o_c = gated_delta_rule(c_q.reshape(B, S, GDN_HEADS, GDN_DK), c_k.reshape(B, S, GDN_HEADS, GDN_DK),
                           c_v.reshape(B, S, GDN_HEADS, GDN_DV), beta, g)
    y_c = gated_head_norm(o_c, gdn_norm, c_g)
    gates = jax.nn.sigmoid(gate_logits.reshape(B, S, N_BRANCH, D))
    merged = (gates[:, :, 0] * (y_a @ w_br_a) + gates[:, :, 1] * (y_b @ w_br_b)
              + gates[:, :, 2] * (y_c @ w_br_c))
    x = x + merged @ w_o
    x = x + hierarchical_moe(rmsnorm(x, ffn_norm), w_coarse, b_coarse, w_fine, b_fine,
                             w_gate_e, w_up_e, w_down_e)
    x = x + jax.nn.sigmoid(rmsnorm(x, ple_norm) @ w_ple_gate) * (p_i @ w_ple)
    return x

def setup_inputs(seed: int = 0) -> dict:
    key = jax.random.key(seed)
    ks = iter(jax.random.split(key, 40))
    L = DEPTH

    def nrm(shape, scale):
        return jax.random.normal(next(ks), shape, jnp.float32) * scale

    def gain(shape):
        return 1.0 + nrm(shape, 0.02)

    x = nrm((BATCH, SEQ, D_MODEL), 1.0)
    p = nrm((L, BATCH, SEQ, PLE_DIM), 1.0)
    offset = jax.random.randint(next(ks), (BATCH, 1), 0, 1024, dtype=jnp.int32)
    positions = offset + jnp.arange(SEQ, dtype=jnp.int32)[None, :]
    attn_norm = gain((L, D_MODEL))
    w_in = nrm((L, D_MODEL, IN_DIM), D_MODEL ** -0.5)
    q_norm = gain((L, SWA_HEAD_DIM))
    k_norm = gain((L, SWA_HEAD_DIM))
    sinks = nrm((L, SWA_Q_HEADS), 1.0)
    gla_wa2 = nrm((L, GLA_GATE_RANK, GLA_K), GLA_GATE_RANK ** -0.5)
    gla_ba = nrm((L, GLA_K), 0.1)
    gla_norm = gain((L, GLA_DV))
    gdn_conv = nrm((L, GDN_CONV, GDN_QKV), GDN_CONV ** -0.5)
    gdn_a_log = jnp.log(jax.random.uniform(next(ks), (L, GDN_HEADS), jnp.float32, 1.0, 16.0))
    dt = jnp.exp(jax.random.uniform(next(ks), (L, GDN_HEADS), jnp.float32, math.log(1e-3), math.log(1e-1)))
    gdn_dt_bias = dt + jnp.log(-jnp.expm1(-dt))
    gdn_norm = gain((L, GDN_DV))
    w_br_a = nrm((L, SWA_Q, D_MODEL), SWA_Q ** -0.5)
    w_br_b = nrm((L, GLA_V, D_MODEL), GLA_V ** -0.5)
    w_br_c = nrm((L, GDN_V, D_MODEL), GDN_V ** -0.5)
    w_o = nrm((L, D_MODEL, D_MODEL), D_MODEL ** -0.5)
    ffn_norm = gain((L, D_MODEL))
    w_coarse = nrm((L, D_MODEL, N_GROUPS), D_MODEL ** -0.5)
    b_coarse = nrm((L, N_GROUPS), 0.01)
    w_fine = nrm((L, D_MODEL, N_EXPERTS), D_MODEL ** -0.5)
    b_fine = nrm((L, N_EXPERTS), 0.01)
    w_gate_e = nrm((L, N_EXPERTS, D_MODEL, EXPERT_FF), D_MODEL ** -0.5)
    w_up_e = nrm((L, N_EXPERTS, D_MODEL, EXPERT_FF), D_MODEL ** -0.5)
    w_down_e = nrm((L, N_EXPERTS, EXPERT_FF, D_MODEL), EXPERT_FF ** -0.5)
    ple_norm = gain((L, D_MODEL))
    w_ple_gate = nrm((L, D_MODEL, D_MODEL), D_MODEL ** -0.5)
    w_ple = nrm((L, PLE_DIM, D_MODEL), PLE_DIM ** -0.5)
    return {'x': x, 'p': p, 'positions': positions, 'attn_norm': attn_norm, 'w_in': w_in,
            'q_norm': q_norm, 'k_norm': k_norm, 'sinks': sinks, 'gla_wa2': gla_wa2, 'gla_ba': gla_ba,
            'gla_norm': gla_norm, 'gdn_conv': gdn_conv, 'gdn_a_log': gdn_a_log,
            'gdn_dt_bias': gdn_dt_bias, 'gdn_norm': gdn_norm, 'w_br_a': w_br_a, 'w_br_b': w_br_b,
            'w_br_c': w_br_c, 'w_o': w_o, 'ffn_norm': ffn_norm, 'w_coarse': w_coarse,
            'b_coarse': b_coarse, 'w_fine': w_fine, 'b_fine': b_fine, 'w_gate_e': w_gate_e,
            'w_up_e': w_up_e, 'w_down_e': w_down_e, 'ple_norm': ple_norm,
            'w_ple_gate': w_ple_gate, 'w_ple': w_ple}

def reference(x, p, positions, attn_norm, w_in, q_norm, k_norm, sinks, gla_wa2, gla_ba, gla_norm,
              gdn_conv, gdn_a_log, gdn_dt_bias, gdn_norm, w_br_a, w_br_b, w_br_c, w_o,
              ffn_norm, w_coarse, b_coarse, w_fine, b_fine, w_gate_e, w_up_e, w_down_e,
              ple_norm, w_ple_gate, w_ple):
    cos, sin = rope_tables(positions)
    for i in range(DEPTH):
        x = hybrid_layer(x, p[i], cos, sin, attn_norm[i], w_in[i], q_norm[i], k_norm[i], sinks[i],
                         gla_wa2[i], gla_ba[i], gla_norm[i], gdn_conv[i], gdn_a_log[i],
                         gdn_dt_bias[i], gdn_norm[i], w_br_a[i], w_br_b[i], w_br_c[i], w_o[i],
                         ffn_norm[i], w_coarse[i], b_coarse[i], w_fine[i], b_fine[i],
                         w_gate_e[i], w_up_e[i], w_down_e[i], ple_norm[i], w_ple_gate[i], w_ple[i])
    return x


_drawn_inputs = setup_inputs


def setup_inputs(seed=0):
    import zlib

    import numpy as np

    out = dict(_drawn_inputs(seed))
    spreads = {}
    factors = {'q_norm': 8.0,
     'k_norm': 4.049,
     'sinks': 18.903,
     'gla_norm': 3.288,
     'gdn_norm': 3.915,
     'b_coarse': 49.044,
     'b_fine': 5.104,
     'ple_norm': 26.396}
    for name, (base, spread) in spreads.items():
        noise = np.random.default_rng([zlib.crc32(name.encode()), seed]).standard_normal(out[name].shape)
        drawn = base * np.exp(spread * noise) if base else spread * noise
        out[name] = jnp.asarray(drawn.astype(out[name].dtype))
    for name, factor in factors.items():
        out[name] = (out[name] * factor).astype(out[name].dtype)
    return out
```

```python
from contextlib import ExitStack

import numpy as np
import concourse.bass as bass
from concourse import mybir

F32 = mybir.dt.float32
I32 = mybir.dt.int32
ALU = mybir.AluOpType
ACT = mybir.ActivationFunctionType
AX = mybir.AxisListType

P = 128
D = 1024
SEQ = 256
T = SEQ // P
KT = D // P
EPS = 1e-6
BIG = 1e30
HEADS_A, KV_A, HD_A = 8, 2, 64
QK_A = (HEADS_A + KV_A) * HD_A
ROT = HD_A // 4
HALF = ROT // 2
H = 4
DK_B = 64
CHUNK = 64
RANK = 16
E = 32
GROUPS = 4
PER_GROUP = E // GROUPS
PAIRS = E // 2
FF = 512
FT = FF // P
CAP = 64
ROUNDS_MAX = 32
ROUNDS_LIMIT = PAIRS + 2 * SEQ // (CAP + 1)
PLE = 256
SLOT = 8 * 520

C_AQ, C_AK, C_BQ, C_BK, C_BV, C_LR, C_BR = 0, 512, 768, 1024, 1280, 1792, 1808
C_CQKV, C_BETA, C_CG, C_GATE = 2320, 3856, 3864, 4376

STATIC = [
    ("w_in", C_CQKV, 512), ("w_in", C_CQKV + 512, 512), ("w_in", C_CQKV + 1024, 512),
    ("w_in", C_BETA, 520), ("w_in", C_BV + 256, 272), ("w_in", C_BR, 512),
    ("w_in", C_AK, 512), ("w_in", C_BK, 512), ("w_in", C_AQ, 512),
    ("w_in", C_GATE + 2048, 512), ("w_br_c", 0, 1024), ("w_in", C_GATE + 2560, 512),
    ("w_in", C_GATE + 1024, 512), ("w_br_b", 0, 1024), ("w_in", C_GATE + 1536, 512),
    ("w_in", C_GATE, 512), ("w_br_a", 0, 1024), ("w_in", C_GATE + 512, 512),
    ("w_o", 0, 512), ("w_o", 512, 512), ("w_router", 0, 36),
    ("w_ple_gate", 0, 512), ("w_ple_gate", 512, 512), ("w_ple", 0, 1024),
]
(J_CQ, J_CK, J_CV, J_CG, J_BVT, J_BR, J_AKV, J_BK, J_AQ, J_GC0, J_WC, J_GC1, J_GB0, J_WB, J_GB1,
 J_GA0, J_WA, J_GA1, J_WO0, J_WO1, J_ROUTER, J_PG0, J_PG1, J_PLE) = range(24)
BEFORE_MOE = J_ROUTER + 1
NS = len(STATIC)

_s = np.arange(P)[:, None]
_c = np.arange(P)[None, :]
_same = _s // CHUNK == _c // CHUNK
LEVELS = 6


def _tables():
    t = {}
    t["ident"] = _s == _c
    t["causal"] = (_s <= _c) & _same
    t["after"] = (_s > _c) & _same
    t["chunk0"] = np.broadcast_to(_s < CHUNK, (P, P))
    t["chunk1"] = np.broadcast_to(_s >= CHUNK, (P, P))
    t["not_causal_big"] = np.where((_s <= _c) & _same, 0.0, BIG)
    for l in range(LEVELS):
        b = 1 << l
        t[f"level{l}"] = (_s // (2 * b) == _c // (2 * b)) & (_s // b % 2 == 0) & (_c // b % 2 == 1)
    t["ones"] = np.ones((P, P))
    t["before"] = _s < _c
    t["swa0"] = np.where(_c <= _s, 0.0, -BIG)
    k = np.arange(2 * P)[None, :]
    t["swa1"] = np.where((k > _s) & (k <= _s + P), 0.0, -BIG)
    t["pair_diag"] = (_s // DK_B) == (k // P)
    t["iota64"] = np.broadcast_to(np.arange(CAP), (P, CAP))
    t["iota32"] = np.broadcast_to(np.arange(ROUNDS_MAX), (P, ROUNDS_MAX))
    t["desc32"] = np.broadcast_to(E - np.arange(E), (P, E))
    t["desc4"] = np.broadcast_to(GROUPS - np.arange(GROUPS), (P, GROUPS))
    inv = (1.0 / (np.float32(500000.0) ** (np.arange(0, ROT, 2, dtype=np.float32) / np.float32(ROT))))
    t["inv_freq"] = np.broadcast_to(inv.astype(np.float32), (P, HALF))
    t["eps"] = np.full((P, 1), EPS)
    t["eps4"] = np.full((P, 1), 4 * EPS)
    t["one"] = np.ones((P, 1))
    at, off, parts = {}, 0, []
    for name, a in t.items():
        at[name] = (off, a.shape[1])
        off += a.shape[1]
        parts.append(np.asarray(a, np.float32))
    return at, np.concatenate(parts, 1)


TABLE_AT, TABLES = _tables()

ROWS = {"qk_gain": QK_A, "gla_norm": 128, "gdn_norm": 128, "sinks": HEADS_A, "dt_bias": H, "a_log": H,
        "b_router": 36}
ROW_AT, _o = {}, 0
for _n, _w in ROWS.items():
    ROW_AT[_n] = (_o, _w)
    _o += _w
ROW_N = _o
COLS = {"attn_norm": KT, "ffn_norm": KT, "ple_norm": KT, "conv": 48}
COL_AT, _o = {}, 0
for _n, _w in COLS.items():
    COL_AT[_n] = (_o, _w)
    _o += _w
COL_N = _o


class Signal:

    def __init__(self, sem, per):
        self.sem, self.per = sem, per

    def at(self, layer, k):
        return layer * self.per + k


def build(nc, a):
    with ExitStack() as ctx:
        _build(nc, a, ctx)


def _build(nc, a, ctx):
    L_N = a["x_layers"]

    def sb(name, shape, dt=F32):
        return ctx.enter_context(nc.sbuf_tensor(name, shape, dt))

    def signal(name, per=1):
        return Signal(ctx.enter_context(nc.semaphore(name)), per)

    ring = sb("ring", [P, 6, SLOT])
    tab = sb("tab", [P, TABLES.shape[1]])
    rows = sb("rows", [P, ROW_N])
    cols = sb("cols", [P, COL_N])
    wa2 = sb("wa2", [RANK + 1, 256])
    blrT = sb("blrT", [RANK + 1, SEQ])
    x = sb("x", [P, T, D])
    h = sb("h", [P, T, D])
    hT = sb("hT", [P, KT, SEQ])
    cossin = sb("cossin", [P, 2, T, HALF])
    posi = sb("posi", [P, T], I32)
    small = sb("small", [P, 512])
    big_a = sb("big_a", [P, 14848])
    ps = ctx.enter_context(nc.psum_tensor("ps", [P, 8, 512], F32))

    class Arena:
        def __init__(self, ap):
            self.ap, self.off, self.size = ap, 0, ap.shape[1]

        def take(self, *dims, at=None):
            n = int(np.prod(dims))
            off = self.off if at is None else at
            if at is None:
                self.off += n
            assert off + n <= self.size, (off + n, self.size)
            v = self.ap[:, off:off + n]
            if len(dims) == 2:
                return v.rearrange("p (a b) -> p a b", a=dims[0])
            if len(dims) == 3:
                return v.rearrange("p (a b c) -> p a b c", a=dims[0], b=dims[1])
            return v

    A = Arena(big_a[:, :])
    scratch = Arena(ring[:, 3:6, :].rearrange("p s n -> p (s n)"))

    def table(name):
        o, n = TABLE_AT[name]
        return tab[:, o:o + n]

    def row(name):
        o, n = ROW_AT[name]
        return rows[:, o:o + n]

    def col(name):
        o, n = COL_AT[name]
        return cols[:, o:o + n]

    ident = table("ident")
    causal, after = table("causal"), table("after")

    ct = A.take(T, 1536)
    kT_c = A.take(4, SEQ)
    kbT_c = A.take(4, SEQ)
    qT_c = A.take(4, SEQ)
    qdT_c = A.take(4, SEQ)
    cg = A.take(T, 512)
    br = A.take(T, 512)
    bt = A.take(T, 1024)
    aq = A.take(T, 768)
    yT = A.take(4, SEQ)
    tmpA = A.take(T, 512)
    tmpk = scratch.take(T, 512)
    kg = scratch.take(T, 512)
    kd = scratch.take(T, 512)
    decT = scratch.take(T, 4, P)
    AT = scratch.take(T, 4, P)
    lower = scratch.take(T, 4, P)
    X = scratch.take(T, 4, P)
    XT = scratch.take(T, 4, P)
    Pm = scratch.take(T, 4, P)
    attG = scratch.take(T, 4, P)
    vnew = scratch.take(T, 512)
    Sc = scratch.take(4, P)
    conv_y = scratch.take(4, SEQ, at=3 * 1024)
    conv_e = scratch.take(4, SEQ, at=4 * 1024)
    wT, u = kbT_c, qT_c.rearrange("p h c -> p (h c)").rearrange("p (t n) -> p t n", t=T)
    la = scratch.take(T, 256, at=3 * 1024)
    zab = scratch.take(T, 256, at=3 * 1024 + 512)
    h_flat = h.rearrange("p t d -> p (t d)")

    def in_h(i):
        return h_flat[:, 512 * i:512 * (i + 1)].rearrange("p (t n) -> p t n", t=T)
    eb, enb, ea = in_h(0), in_h(1), in_h(2)
    qe, ke, kdb = eb, enb, ea
    Sb = scratch.take(3, 2, 256, at=4 * 1024)
    dum = scratch.take(2, 256, at=4 * 1024 + 1536)
    qeT = scratch.take(2, SEQ, at=6 * 1024)
    keT = scratch.take(2, SEQ, at=6 * 1024 + 512)
    attB = scratch.take(T, 4, P, at=8 * 1024)
    y_of = [scratch.take(T, 512, at=at) for at in (0, 7 * 1024, 0)]
    sq_of = [scratch.take(T, 512, at=at) for at in (1024, 2 * 1024)]
    merged = scratch.take(T, D, at=9 * 1024)
    kswap = scratch.take(T, P, at=11 * 1024)
    kTa = scratch.take(SEQ, at=11 * 1024 + 256)
    kTb = scratch.take(SEQ, at=11 * 1024 + 512)
    scores = A.take(HEADS_A, 3 * P, at=0)
    pT = A.take(24, P, at=3072)
    qT_a = qdT_c
    M = Arena(big_a[:, :])
    sel = M.take(T, 2, CAP)
    selw = M.take(T, 2, CAP)
    selwT = M.take(SEQ)
    xgT = M.take(KT, P)
    sig = M.take(FF)
    act_h = M.take(FF)
    hgT = M.take(FT, P)
    ye = M.take(D)
    lg = M.take(T, 36)
    oh_g = M.take(T, GROUPS)
    msk_g = M.take(T, GROUPS)
    fm = M.take(T, E)
    tmpe = M.take(T, E)
    oh1 = M.take(T, E)
    oh2 = M.take(T, E)
    wts = M.take(T, E)
    chosen = M.take(T, E)
    posm = M.take(T, E)
    counts = M.take(E)
    rounds = M.take(PAIRS)
    rtmp = M.take(PAIRS)
    cum = M.take(PAIRS)
    cmp3 = M.take(ROUNDS_MAX, PAIRS)
    pair_f = M.take(ROUNDS_MAX)
    off_f = M.take(ROUNDS_MAX)
    row_f = M.take(64)
    pin = M.take(T, PLE)
    pinT = M.take(2, SEQ)
    gtmp = M.take(T, 512)
    tbl = sb("tbl", [1, L_N * 64], I32)
    base_f = sb("base_f", [P, 1])

    so = [0]

    def sm(*dims):
        n = int(np.prod(dims))
        v = small[:, so[0]:so[0] + n]
        so[0] += n
        assert so[0] <= 512
        if len(dims) == 2:
            return v.rearrange("p (a b) -> p a b", a=dims[0])
        if len(dims) == 3:
            return v.rearrange("p (a b c) -> p a b c", a=dims[0], b=dims[1])
        return v

    ss = sm(T)
    rstd = sm(T)
    ba = sm(T, 8)
    beta = sm(T, H)
    gdec = sm(T, H)
    gabs = sm(T, H)
    nea = sm(H)
    expG = sm(T, 4, H)
    negG = sm(T, H)
    betaG = sm(T, H)
    ssq = sm(T, 8)
    decB = sm(2, T, 2)
    ssa = sm(T, 10)
    mx = sm(T, HEADS_A)
    den = sm(T, HEADS_A)
    esink = sm(T, HEADS_A)
    ra = [sm(T, 10, HALF) for _ in range(1)][0]
    so2 = sb("rope_tmp", [P, 3, T, 10, HALF])
    sso = sm(T, H)
    gmx = sm(T)
    m1 = sm(T)
    m2 = sm(T)
    gsum = sm(T)
    e2 = sm(T)
    w1 = sm(T)
    w2 = sm(T)
    pk = sm(T)

    s_tab = signal("tables_loaded")
    s_x0 = signal("x_loaded")
    s_par = signal("params_loaded", 3)
    s_par_used = signal("params_used")
    s_pin = signal("ple_input_loaded")
    s_slot = [signal(f"slot{i}_loaded") for i in range(6)]
    s_static_used = signal("static_chunk_used", NS)
    s_trig = signal("trig_args_ready")
    s_trigd = signal("trig_done")
    s_zero = signal("zeros_ready")
    s_ss = signal("square_sums_ready", 3)
    s_h = signal("h_normed", 3 * T)
    s_hTp = signal("h_transposed", 3 * 4)
    s_hT = signal("hT_ready", 3 * 4)
    s_conv_y = signal("conv_out_ready", 3)
    s_conv_e = signal("conv_exp_ready", 3)
    s_conv_s = signal("conv_silu_ready", 3)
    s_ct_p = signal("conv_transposed", 3)
    s_ct = signal("ct_ready", 3)
    s_pj_dve = signal("output_gate_taken", 2)
    s_pj_act = signal("projection_taken", 4)
    s_gexp = signal("gate_exp_ready", 2)
    s_nsq = signal("head_squares_ready")
    s_nr = signal("head_rstd_ready")
    s_beta_e = signal("beta_exp_ready", 3)
    s_g = signal("g_ready", 4)
    s_G_p = signal("G_summed")
    s_G = signal("G_exps_ready", 2)
    s_Gr_p = signal("G_rows_ready", T)
    s_dm = signal("decay_args_ready", T)
    s_dec = signal("decay_ready", T)
    s_kqn = signal("k_q_normed")
    s_kb = signal("k_beta_ready")
    s_trc_p = signal("c_transposed", 4)
    s_trc = signal("c_transposed_taken", 4)
    s_qd = signal("q_decayed")
    s_kd = signal("k_decayed")
    s_A_p = signal("kk_products", T)
    s_A = signal("AT_ready", T)
    s_at_p = signal("qk_products", T)
    s_at = signal("attG_ready", T)
    s_lv = signal("level_blocks_ready", LEVELS * T)
    s_P_p = signal("level_P", LEVELS * T)
    s_P = signal("level_P_taken", LEVELS * T)
    s_D_p = signal("level_D", LEVELS * T)
    s_X = signal("inverse_updated", LEVELS * T)
    s_wu_p = signal("w_u_products", T)
    s_wu = signal("w_u_ready", T)
    s_ws = signal("w_state", 3)
    s_vn = signal("v_new_ready", 4)
    s_ds = signal("state_product", 3)
    s_S = signal("state_ready", 3)
    s_oc = signal("o_products", 2 * T)
    s_ot = signal("o_taken", 4)
    s_on = signal("o_norm_args", 2)
    s_onr = signal("o_norm_ready", 2)
    s_y = signal("y_ready", 3)
    s_yT_p = signal("y_transposed", 3)
    s_yT = signal("yT_ready", 3)
    s_gt_p = signal("gate_products", 9)
    s_gt_e = signal("gate_exps", 12)
    s_mg = signal("merge_added", 12)
    s_z = signal("z_ready", 2)
    s_la = signal("log_a_exp", 2)
    s_lar = signal("log_a_ready")
    s_b_p = signal("b_summed")
    s_b = signal("b_exps_ready")
    s_qke = signal("gla_operands_ready")
    s_trb_p = signal("gla_transposed")
    s_trb = signal("gla_transposed_taken")
    s_ab_p = signal("gla_products", T)
    s_ab = signal("gla_att_ready", T)
    s_du_p = signal("gla_state_products", 3)
    s_Sb = signal("gla_states_ready", 3)
    s_asq = signal("swa_squares_ready")
    s_ar = signal("swa_rstd_ready")
    s_ak = signal("swa_roped")
    s_tra_p = signal("swa_transposed")
    s_tra = signal("swa_transposed_taken")
    s_sc_p = signal("scores_products", T)
    s_sc = signal("scores_masked", T)
    s_sx = signal("scores_centered")
    s_pe = signal("probs_ready")
    s_pt_p = signal("probs_transposed", 6)
    s_pt = signal("probs_taken", 6)
    s_pv = signal("pv_products", T)
    s_mT_p = signal("merged_transposed", 4)
    s_mT = signal("merged_taken", 4)
    s_wo = signal("wo_products", 2)
    s_x = signal("x_updated", 2)
    s_rt = signal("router_exp_args", 2)
    s_rte = signal("router_exps", 2)
    s_ch = signal("chosen_ready")
    s_pos_p = signal("positions_summed")
    s_tbl = signal("rounds_planned")
    s_init = signal("moe_zeroed")
    s_sel = signal("selection_ready")
    s_selw = signal("weighted_selection_ready")
    s_ga = signal("gathered")
    s_xg = signal("gathered_taken")
    s_gate = signal("gate_done")
    s_up = signal("up_done")
    s_down = signal("down_done")
    s_sig = signal("silu_tanh_ready")
    s_act = signal("act_ready")
    s_swT_p = signal("weighted_selection_transposed")
    s_swT = signal("weighted_selection_taken")
    s_hg_p = signal("act_transposed")
    s_hg = signal("act_taken")
    s_ye = signal("expert_out_taken")
    s_scat = signal("scattered")
    s_acc = signal("moe_done")
    s_pl_p = signal("ple_transposed")
    s_pl = signal("ple_taken")
    s_pg_p = signal("ple_products", 3)
    s_pg_e = signal("ple_exps", 4)
    s_pg = signal("ple_added", 4)
    s_out = signal("out_stored")

    def plan(eng, L, at, lo, hi):
        return eng.value_load(tbl[0:1, bass.ds(L * 64 + at, 1)], min_val=lo, max_val=hi)

    block = ctx.enter_context(nc.Block())

    def slot_view(j):
        name, c0, n = STATIC[j]
        kt = {"w_br_a": 4, "w_br_b": 4, "w_br_c": 4, "w_ple": 2}.get(name, KT)
        return ring[:, j % 3, 0:kt * n].rearrange("p (k n) -> p k n", k=kt)

    def chunk_used(L, j):
        return L * NS + 3 + j + 1

    def slot_loaded(L, j):
        return 16 * (L * (NS // 3 + PAIRS) + j // 3 + 1 + (PAIRS if j >= BEFORE_MOE else 0))

    def pair_loaded(L, c, pair):
        if c < 3:
            return 16 * (L * (NS // 3 + PAIRS) + BEFORE_MOE // 3 + pair + 1)
        return 16 * (L * PAIRS + pair + 1)

    @block.sync
    def _(sp):
        sp.dma_start(tab[:, :], a["tables"]).then_inc(s_tab.sem, 16)
        sp.dma_start(posi[:, :], a["positions"].rearrange("(t p) -> p t", p=P),
                     allow_slow_non_contiguous=True).then_inc(s_tab.sem, 16)
        sp.dma_start(x[:, :, :], a["x"].rearrange("(t p) d -> p t d", p=P)).then_inc(s_x0.sem, 16)
        moe = {"w_gate_e": a["w_gate_e"].rearrange("l e (p k) n -> (l e) p (k n)", k=KT),
               "w_up_e": a["w_up_e"].rearrange("l e (p k) n -> (l e) p (k n)", k=KT),
               "w_down_e": a["w_down_e"].rearrange("l e (p k) n -> (l e) p (k n)", k=FT)}

        def one(ap, i):
            return ap[bass.ds(i, 1)]

        with sp.Fori(0, L_N) as L:
            sp.wait_ge(s_par_used.sem, s_par_used.at(L, 1))
            sp.dma_start(cols[:, :], one(a["cols"], L).rearrange("l p n -> (l p) n")).then_inc(s_par.sem, 16)
            sp.dma_start(rows[:, :], one(a["rows"], L).rearrange("l n -> (l n)").partition_broadcast(P)
                         ).then_inc(s_par.sem, 16)
            sp.dma_start(wa2[:, :], one(a["wa2"], L).rearrange("l k n -> (l k) n")).then_inc(s_par.sem, 16)

            def load_static(j):
                name, c0, n = STATIC[j]
                kt = slot_view(j).shape[1]
                src = one(a[name], L)[:, :, c0:c0 + n].rearrange("l (p k) n -> (l p) k n", k=kt)
                sp.dma_start(slot_view(j), src).then_inc(s_slot[j % 3].sem, 16)

            for j in range(BEFORE_MOE):
                if j != J_AQ:
                    sp.wait_ge(s_static_used.sem, chunk_used(L, j - 2 if j == J_BK else j - 3))
                load_static(j)

            def load_pair(i, c):
                name = ("w_gate_e", "w_up_e", "w_down_e")[c // 2]
                src = one(moe[name], L * E + 2 * i + c % 2).rearrange("l p n -> (l p) n")
                sp.dma_start(ring[:, c, 0:4096], src).then_inc(s_slot[c].sem, 16)

            for c in range(3):
                sp.wait_ge(s_static_used.sem, chunk_used(L, BEFORE_MOE + c - 3))
                load_pair(0, c)
            sp.wait_ge(s_mT.sem, s_mT.at(L, 4))
            for c in range(3, 6):
                load_pair(0, c)
            sp.wait_ge(s_tbl.sem, L + 1)
            total = plan(sp, L, ROUNDS_MAX + PAIRS - 1, 1, 4096)
            with sp.Fori(1, PAIRS) as i:
                done = plan(sp, L, ROUNDS_MAX - 1 + i, 1, 4096)
                for s, c in ((s_gate, 0), (s_gate, 1), (s_up, 2), (s_up, 3), (s_down, 4), (s_down, 5)):
                    if c % 2 == 0:
                        sp.wait_ge(s.sem, done)
                    load_pair(i, c)
            sp.wait_ge(s_gate.sem, total)
            load_static(J_PG0)
            load_static(J_PG1)
            sp.wait_ge(s_up.sem, total)
            load_static(J_PLE)
        for t in range(T):
            sp.wait_ge(s_pg.sem, 4 * L_N + (3 if t == 0 else 4))
            sp.dma_start(a["out"].rearrange("(t p) d -> p t d", p=P)[:, t, :], x[:, t, :]).then_inc(s_out.sem, 16)
        sp.wait_ge(s_out.sem, 16 * T)

    @block.gpsimd
    def _(pool):
        pool.memset(blrT[:, :], 1.0).then_inc(s_zero.sem, 1)
        with pool.Fori(0, L_N) as L:
            for l in range(LEVELS):
                for t in range(T):
                    if l == 0:
                        pool.wait_ge(s_A.sem, s_A.at(L, t + 1))
                    else:
                        pool.wait_ge(s_P_p.sem, s_P_p.at(L, 2 * (l - 1) + t + 1))
                    pool.tensor_tensor(lower[:, t], AT[:, t],
                                       table(f"level{l}").unsqueeze(1).broadcast_to([P, 4, P]),
                                       ALU.mult).then_inc(s_lv.sem, 1)
            pool.wait_ge(s_tbl.sem, L + 1)
            pool.dma_start(pin, a["p"][bass.ds(L, 1)].rearrange("l (t p) n -> p (l t) n", p=P)
                           ).then_inc(s_pin.sem, 16)
            pool.memset(ye, 0.0)
            pool.memset(selwT, 0.0).then_inc(s_init.sem, 1)

    @block.tensor
    def _(pe):
        mm = nc.tensor.matmul
        tr = nc.tensor.transpose
        for c in range(3):
            pe.sem_inc(s_static_used.sem, 1)
        pe.sem_inc(s_swT_p.sem, 1)
        pe.wait_ge(s_tab.sem, 32)
        with pe.Fori(0, L_N) as L:
            def transpose_h(n):
                for t in range(T):
                    pe.wait_ge(s_h.sem, s_h.at(L, n * T + t + 1))
                    for q in range(2):
                        for k in range(4):
                            last = tr(ps[:, 2 + 2 * t + q, k * P:(k + 1) * P], h[:, t, 4 * q + k:D:KT], ident)
                        last.then_inc(s_hTp.sem, 1)

            def token_major(j, t, bank, c0, n, at=0):
                w = slot_view(j)
                for k in range(w.shape[1]):
                    last = mm(ps[:, bank, at:at + n], hT[:, k, t * P:(t + 1) * P], w[:, k, c0:c0 + n],
                              start=(k == 0), stop=(k == w.shape[1] - 1))
                return last

            def need(j):
                pe.wait_ge(s_slot[j % 3].sem, slot_loaded(L, j))

            transpose_h(0)
            pe.wait_ge(s_hT.sem, s_hT.at(L, 4))

            def channel_group(g):
                need(J_CQ + g)
                w = slot_view(J_CQ + g)
                if g == 2:
                    pe.wait_ge(s_conv_y.sem, s_conv_y.at(L, 1))
                for m in range(4):
                    b = (0 if g % 2 == 0 else 6) + m // 2
                    for k in range(KT):
                        last = mm(ps[:, b, (m % 2) * SEQ:(m % 2 + 1) * SEQ], w[:, k, m * P:(m + 1) * P],
                                  hT[:, k, :], start=(k == 0), stop=(k == KT - 1))
                last.then_inc(s_static_used.sem, 1)

            def conv_transposes(g):
                pe.wait_ge(s_conv_s.sem, s_conv_s.at(L, g + 1))
                if g:
                    pe.wait_ge(s_ct.sem, s_ct.at(L, g))
                for t in range(T):
                    for m in range(4):
                        last = tr(ps[:, 2 + t, m * P:(m + 1) * P], conv_y[:, m, t * P:(t + 1) * P], ident)
                last.then_inc(s_ct_p.sem, 1)

            channel_group(0)
            channel_group(1)
            conv_transposes(0)
            channel_group(2)
            conv_transposes(1)
            need(J_CG)
            pe.wait_ge(s_conv_y.sem, s_conv_y.at(L, 2))
            for t in range(T):
                token_major(J_CG, t, 6, 0, 8, at=8 * t)
            for t in range(T):
                last = token_major(J_CG, t, 4 + t, 8, 512)
            last.then_inc(s_static_used.sem, 1)
            conv_transposes(2)
            need(J_BVT)
            pe.wait_ge(s_conv_y.sem, s_conv_y.at(L, 3))
            w = slot_view(J_BVT)
            for k in range(KT):
                mm(ps[0:RANK, 7, 0:SEQ], w[:, k, 256:256 + RANK], hT[:, k, :], start=(k == 0), stop=(k == KT - 1))
            for t in range(T):
                last = token_major(J_BVT, t, t, 0, 256)
            last.then_inc(s_static_used.sem, 1)
            need(J_BR)
            pe.wait_ge(s_pj_dve.sem, s_pj_dve.at(L, 1))
            for t in range(T):
                last = token_major(J_BR, t, 4 + t, 0, 512)
            last.then_inc(s_static_used.sem, 1)
            pe.wait_ge(s_g.sem, s_g.at(L, 3))
            for t in range(T):
                for i, m in enumerate((causal, after, table("chunk0"), table("chunk1"))):
                    last = mm(ps[:, 6, 64 + 16 * t + 4 * i:68 + 16 * t + 4 * i], m, gdec[:, t, :], start=True, stop=True)
            last.then_inc(s_G_p.sem, 1)
            pe.wait_ge(s_g.sem, s_g.at(L, 4))
            pe.wait_ge(s_ct.sem, s_ct.at(L, 3))
            gB = tmpA.rearrange("p t (h s) -> p t h s", h=H)
            for t in range(T):
                for hh in range(H):
                    last = mm(ps[:, 2 + t, hh * P:(hh + 1) * P], gB[:, t, hh, :], causal, start=True, stop=True)
                last.then_inc(s_Gr_p.sem, 1)

            def c_transposes(i, src, b, ready):
                ready()
                for t in range(T):
                    for hh in range(H):
                        last = tr(ps[:, b + t, hh * P:(hh + 1) * P], src[:, t, hh * P:(hh + 1) * P], ident)
                last.then_inc(s_trc_p.sem, 1)

            def k_ready():
                pe.wait_ge(s_kqn.sem, L + 1)
                pe.wait_ge(s_pj_act.sem, s_pj_act.at(L, 1))
                pe.wait_ge(s_G.sem, s_G.at(L, 2))
            need(J_AKV)
            pe.wait_ge(s_pj_act.sem, s_pj_act.at(L, 1))
            for t in range(T):
                last = token_major(J_AKV, t, t, 0, 512)
            last.then_inc(s_static_used.sem, 1)

            c_transposes(0, ct[:, :, 512:1024], 6, k_ready)

            def kb_ready():
                pe.wait_ge(s_kb.sem, L + 1)
                pe.wait_ge(s_pj_dve.sem, s_pj_dve.at(L, 2))
            c_transposes(1, tmpk, 4, kb_ready)

            def q_ready():
                pe.wait_ge(s_trc.sem, s_trc.at(L, 1))
            c_transposes(2, ct[:, :, 0:512], 6, q_ready)
            for t in range(T):
                pe.wait_ge(s_trc.sem, s_trc.at(L, 2))
                pe.wait_ge(s_dm.sem, s_dm.at(L, t + 1))
                for hh in range(H):
                    last = mm(ps[:, 2 + t, hh * P:(hh + 1) * P], kT_c[:, hh, t * P:(t + 1) * P],
                              kbT_c[:, hh, t * P:(t + 1) * P], start=True, stop=True)
                last.then_inc(s_A_p.sem, 1)
            for t in range(T):
                pe.wait_ge(s_trc.sem, s_trc.at(L, 3))
                for hh in range(H):
                    last = mm(ps[:, 4 + t, hh * P:(hh + 1) * P], kT_c[:, hh, t * P:(t + 1) * P],
                              qT_c[:, hh, t * P:(t + 1) * P], start=True, stop=True)
                last.then_inc(s_at_p.sem, 1)

            def qd_ready():
                pe.wait_ge(s_qd.sem, L + 1)
            c_transposes(3, ct[:, :, 0:512], 6, qd_ready)

            units = [(J_BK, 0), (J_BK, 1), (J_AQ, 0), (J_AQ, 1)]

            def unit(i):
                j, t = units[i]
                if t == 0:
                    need(j)
                    pe.wait_ge(s_pj_act.sem, s_pj_act.at(L, 2 + i // 2))
                last = token_major(j, t, t, 0, 512)
                if t == 1:
                    last.then_inc(s_static_used.sem, 1)

            def level(l):
                for t in range(T):
                    pe.wait_ge(s_lv.sem, s_lv.at(L, 2 * l + t + 1))
                    if l:
                        pe.wait_ge(s_X.sem, s_X.at(L, 2 * (l - 1) + t + 1))
                    for hh in range(H):
                        last = mm(ps[:, 2 + t, hh * P:(hh + 1) * P], lower[:, t, hh, :],
                                  X[:, t, hh, :] if l else ident, start=True, stop=True)
                    last.then_inc(s_P_p.sem, 1)
                for t in range(T):
                    pe.wait_ge(s_P.sem, s_P.at(L, 2 * l + t + 1))
                    if l == 0:
                        pe.wait_ge(s_at.sem, s_at.at(L, t + 1))
                        pe.wait_ge(s_trc.sem, s_trc.at(L, 4))
                    for hh in range(H):
                        last = mm(ps[:, 4 + t, hh * P:(hh + 1) * P], Pm[:, t, hh, :],
                                  XT[:, t, hh, :] if l else ident, start=True, stop=True)
                    if l < LEVELS - 1:
                        for hh in range(H):
                            last = mm(ps[:, 6 + t, hh * P:(hh + 1) * P], XT[:, t, hh, :] if l else ident,
                                      Pm[:, t, hh, :], start=True, stop=True)
                    last.then_inc(s_D_p.sem, 1)

            for l in range(LEVELS):
                level(l)
                if l < 4:
                    unit(l)
                elif l == 4:
                    pe.wait_ge(s_pj_act.sem, s_pj_act.at(L, 4))
                    for t in range(T):
                        last = mm(ps[:, 0, t * 256:(t + 1) * 256], blrT[:, t * P:(t + 1) * P], wa2[:, :],
                                  start=True, stop=True)
                    last.then_inc(s_z.sem, 1)
            for t in range(T):
                pe.wait_ge(s_X.sem, s_X.at(L, 2 * (LEVELS - 1) + t + 1))
                for hh in range(H):
                    mm(ps[:, 2 + t, hh * P:(hh + 1) * P], kg[:, t, hh * P:(hh + 1) * P], XT[:, t, hh, :],
                       start=True, stop=True)
                for hh in range(H):
                    last = mm(ps[:, 4 + t, hh * P:(hh + 1) * P], XT[:, t, hh, :],
                              ct[:, t, 1024 + hh * P:1024 + (hh + 1) * P], start=True, stop=True)
                last.then_inc(s_wu_p.sem, 1)
            def scan(n):
                t, r = n // 2, CHUNK * (n % 2)
                if n:
                    pe.wait_ge(s_S.sem, s_S.at(L, n))
                    m = CHUNK if r == 0 else P
                    for hh in range(H):
                        last = mm(ps[0:m, 6, hh * P:(hh + 1) * P], wT[:, hh, t * P:t * P + m], Sc[:, hh, :],
                                  start=True, stop=True)
                    last.then_inc(s_ws.sem, 1)
                if n == 0:
                    pe.wait_ge(s_wu.sem, s_wu.at(L, 2))
                if n:
                    for hh in range(H):
                        mm(ps[r:r + CHUNK, 2 + t, hh * P:(hh + 1) * P], qdT_c[:, hh, t * P + r:t * P + r + CHUNK],
                           Sc[:, hh, :], start=(hh == 0), stop=(hh == H - 1), skip_group_check=True)
                pe.wait_ge(s_vn.sem, s_vn.at(L, n + 1))
                if n < 3:
                    for hh in range(H):
                        last = mm(ps[:, 7, hh * P:(hh + 1) * P], kd[r:r + CHUNK, t, hh * P:(hh + 1) * P],
                                  vnew[r:r + CHUNK, t, hh * P:(hh + 1) * P], start=True, stop=True)
                    last.then_inc(s_ds.sem, 1)
                if r:
                    for half in range(2):
                        o = CHUNK * half
                        for hh in range(H):
                            last = mm(ps[o:o + CHUNK, 2 + t, hh * P:(hh + 1) * P], attG[:, t, hh, o:o + CHUNK],
                                      vnew[:, t, hh * P:(hh + 1) * P],
                                      start=(t == 0 and half == 0 and hh == 0), stop=(hh == H - 1), skip_group_check=True)
                    last.then_inc(s_oc.sem, 1)

            def gla_state_product(n):
                t, r = n // 2, CHUNK * (n % 2)
                b = 1 - n % 2
                if n == 2:
                    pe.wait_ge(s_Sb.sem, s_Sb.at(L, 1))
                for g in range(2):
                    last = mm(ps[:, b, g * 256:(g + 1) * 256], kdb[r:r + CHUNK, t, g * P:(g + 1) * P],
                              bt[r:r + CHUNK, t, 512 + g * 256:512 + (g + 1) * 256], start=True, stop=True)
                last.then_inc(s_du_p.sem, 1)

            scan(0)
            pe.wait_ge(s_lar.sem, L + 1)
            for t in range(T):
                mm(ps[:, 0, t * 256:(t + 1) * 256], causal, la[:, t, :], start=True, stop=True)
            for t in range(T):
                mm(ps[:, 1, t * 256:(t + 1) * 256], after, la[:, t, :], start=True, stop=True)
            for t in range(T):
                for g in range(2):
                    for n in range(2):
                        o = 4 * g + 2 * t + n
                        last = mm(ps[:, 4, o:o + 1], la[:, t, g * P:(g + 1) * P],
                                  table("chunk0" if n == 0 else "chunk1")[:, 0:1], start=True, stop=True)
            last.then_inc(s_b_p.sem, 1)
            scan(1)
            pe.wait_ge(s_qke.sem, L + 1)
            for i, src in enumerate((qe, ke)):
                for g in range(2):
                    for t in range(T):
                        last = tr(ps[:, 4 + i, (2 * g + t) * P:(2 * g + t + 1) * P], src[:, t, g * P:(g + 1) * P], ident)
            last.then_inc(s_trb_p.sem, 1)
            gla_state_product(0)
            scan(2)
            gla_state_product(1)
            pe.wait_ge(s_trb.sem, L + 1)
            for odd in range(2):
                for t in range(T):
                    for g in range(2):
                        r = DK_B * odd
                        last = mm(ps[:, 4 + odd, (2 * t + g) * P:(2 * t + g + 1) * P],
                                  keT[r:r + DK_B, g, t * P:(t + 1) * P], qeT[r:r + DK_B, g, t * P:(t + 1) * P],
                                  start=True, stop=True)
                last.then_inc(s_ab_p.sem, 1)
            gla_state_product(2)
            scan(3)
            for t in range(T):
                pe.wait_ge(s_ab.sem, s_ab.at(L, 2))
                for half in range(2):
                    r, n = CHUNK * half, 2 * t + half
                    if n:
                        pe.wait_ge(s_Sb.sem, s_Sb.at(L, n))
                    out = ps[r:r + CHUNK, 4 + t, :]
                    for hh in range(H):
                        last = mm(out[:, hh * P:(hh + 1) * P], attB[:, t, hh, r:r + CHUNK],
                                  bt[:, t, 512 + hh * P:512 + (hh + 1) * P], start=(hh == 0), stop=(n == 0),
                                  skip_group_check=True)
                    if n:
                        for g in range(2):
                            last = mm(out[:, g * 256:(g + 1) * 256], qeT[:, g, t * P + r:t * P + r + CHUNK],
                                      Sb[:, n - 1, g, :], start=False, stop=(g == 1), skip_group_check=True)
                last.then_inc(s_oc.sem, 1)

            def y_transposes(n):
                pe.wait_ge(s_y.sem, s_y.at(L, n + 1))
                for t in range(T):
                    for k in range(4):
                        last = tr(ps[:, 6 + t, k * P:(k + 1) * P], y_of[n][:, t, k:512:4], ident)
                last.then_inc(s_yT_p.sem, 1)

            def merge_gates(n, jg):
                need(jg)
                for t in range(T):
                    if n:
                        pe.wait_ge(s_mg.sem, s_mg.at(L, 4 * n + t - 1))
                    last = token_major(jg, t, t, 0, 512)
                last.then_inc(s_static_used.sem, 1)

            def branch_product(t, f, jg):
                w = slot_view(jg + 1)
                for k in range(4):
                    last = mm(ps[:, 2 + t, :], yT[:, k, t * P:(t + 1) * P], w[:, k, f * 512:(f + 1) * 512],
                              start=(k == 0), stop=(k == 3))
                return last

            def merge_first(n, jg):
                need(jg + 1)
                pe.wait_ge(s_yT.sem, s_yT.at(L, n + 1))
                for t in range(T):
                    branch_product(t, 0, jg).then_inc(s_gt_p.sem, 1)

            def merge_second(n, jg):
                need(jg + 2)
                pe.wait_ge(s_mg.sem, s_mg.at(L, 4 * n + 1))
                token_major(jg + 2, 0, 0, 0, 512)
                branch_product(0, 1, jg).then_inc(s_gt_p.sem, 1)
                pe.wait_ge(s_mg.sem, s_mg.at(L, 4 * n + 2))
                branch_product(1, 1, jg).then_inc(s_static_used.sem, 1)
                token_major(jg + 2, 1, 1, 0, 512).then_inc(s_static_used.sem, 1)

            merge_gates(0, J_GC0)
            y_transposes(0)
            merge_first(0, J_GC0)
            merge_second(0, J_GC0)
            pe.wait_ge(s_ak.sem, L + 1)
            pe.wait_ge(s_ot.sem, s_ot.at(L, 4))
            for t in range(T):
                for g in range(4):
                    tr(ps[:, 4 + t, g * P:(g + 1) * P], aq[:, t, g * P:(g + 1) * P], ident)
                tr(ps[:, 6, t * P:(t + 1) * P], aq[:, t, 512:640], ident)
                last = tr(ps[:, 6, 256 + t * P:256 + (t + 1) * P], kswap[:, t, :], ident)
            last.then_inc(s_tra_p.sem, 1)
            merge_gates(1, J_GB0)

            def score(hh, t, out):
                r = HD_A * (hh % 2)
                kv = hh // (HEADS_A // KV_A)
                keys = (kTa if kv == hh % 2 else kTb)[r:r + HD_A, 0:P * (t + 1)]
                return mm(out, qT_a[r:r + HD_A, hh // 2, t * P:(t + 1) * P], keys, start=True, stop=True)
            pe.wait_ge(s_tra.sem, L + 1)
            for hh in range(HEADS_A):
                last = score(hh, 0, ps[:, 4 + hh % 2, (hh // 2) * P:(hh // 2 + 1) * P])
            last.then_inc(s_sc_p.sem, 1)
            y_transposes(1)
            merge_first(1, J_GB0)
            pe.wait_ge(s_sc.sem, s_sc.at(L, 1))
            for hh in range(HEADS_A):
                b = (6, 4)[hh % 2] + hh // 4
                last = score(hh, 1, ps[:, b, (hh // 2 % 2) * SEQ:(hh // 2 % 2 + 1) * SEQ])
            last.then_inc(s_sc_p.sem, 1)
            merge_second(1, J_GB0)
            merge_gates(2, J_GA0)
            pe.wait_ge(s_pe.sem, L + 1)
            for i in range(6):
                if i >= 4:
                    pe.wait_ge(s_pt.sem, s_pt.at(L, i - 3))
                for k in range(4):
                    hh, b = divmod(4 * i + k, 3)
                    last = tr(ps[:, 4 + i % 4, k * P:(k + 1) * P], scores[:, hh, b * P:(b + 1) * P], ident)
                last.then_inc(s_pt_p.sem, 1)
            pe.wait_ge(s_pt.sem, s_pt.at(L, 6))
            for t in range(T):
                for hh in range(HEADS_A):
                    out = ps[:, 4 + 2 * t + hh // 4, (hh % 4) * P:(hh % 4 + 1) * P]
                    for kb in range(t + 1):
                        last = mm(out, pT[:, 3 * hh + (kb + 1 if t else 0), :], aq[:, kb, 640:768],
                                  start=(kb == 0), stop=(kb == t))
                last.then_inc(s_pv.sem, 1)
            y_transposes(2)
            merge_first(2, J_GA0)
            merge_second(2, J_GA0)
            pe.wait_ge(s_mg.sem, s_mg.at(L, 12))
            for t in range(T):
                for q in range(2):
                    for k in range(4):
                        last = tr(ps[:, 4 + 2 * t + q, k * P:(k + 1) * P], merged[:, t, 4 * q + k:D:KT], ident)
                    last.then_inc(s_mT_p.sem, 1)
            pe.wait_ge(s_mT.sem, s_mT.at(L, 4))
            for f in range(2):
                need(J_WO0 + f)
                for t in range(T):
                    token_major(J_WO0 + f, t, 2 * f + t, 0, 512).then_inc((s_wo, s_static_used)[t].sem, 1)
            transpose_h(1)
            pe.wait_ge(s_hT.sem, s_hT.at(L, 8))
            need(J_ROUTER)
            for t in range(T):
                last = token_major(J_ROUTER, t, 6, 0, 36, at=64 * t)
            last.then_inc(s_static_used.sem, 1)
            pe.wait_ge(s_ch.sem, L + 1)
            mm(ps[:, 7, 0:E], table("before"), chosen[:, 0, :], start=True, stop=True)
            mm(ps[:, 7, E:2 * E], table("before"), chosen[:, 1, :], start=True, stop=False)
            mm(ps[:, 7, E:2 * E], table("ones"), chosen[:, 0, :], start=False, stop=True)
            mm(ps[:, 7, 2 * E:3 * E], table("ones"), chosen[:, 0, :], start=True, stop=False)
            mm(ps[:, 7, 2 * E:3 * E], table("ones"), chosen[:, 1, :], start=False, stop=True).then_inc(s_pos_p.sem, 1)

            def gather():
                for k in range(KT):
                    for t in range(T):
                        last = mm(ps[:, 4 + k // 4, (k % 4) * P:(k % 4 + 1) * P], h[:, t, k:D:KT],
                                  sel[:, t].rearrange("p j s -> p (j s)"), start=(t == 0), stop=(t == T - 1))
                last.then_inc(s_ga.sem, 1)

            def scatter(first=False):
                for t in range(T):
                    for f in range(2):
                        last = mm(ps[:, 2 * t + f, :], selwT[:, t * P:(t + 1) * P], ye[:, f * 512:(f + 1) * 512],
                                  start=first, stop=first, skip_group_check=True)
                return last

            pe.wait_ge(s_init.sem, L + 1)
            scatter(first=True)
            pe.drain()
            base = plan(pe, L, 48, 0, 4096)
            n_rounds = plan(pe, L, 49, PAIRS, ROUNDS_LIMIT)
            pe.wait_ge(s_sel.sem, base + L + 1)
            gather()
            with pe.Fori(0, n_rounds) as g:
                pair = plan(pe, L, g, 0, PAIRS - 1)
                gg = base + g
                pe.wait_ge(s_xg.sem, gg + L + 1)
                for c, bank, out in ((0, 6, s_gate), (2, 7, s_up)):
                    pe.wait_ge(s_slot[c].sem, pair_loaded(L, c, pair))
                    pe.wait_ge(s_slot[c + 1].sem, pair_loaded(L, c + 1, pair))
                    if c == 0:
                        pe.wait_ge(s_swT.sem, gg + 1)
                    else:
                        pe.wait_ge(s_hg.sem, gg + 1)
                    for k in range(KT):
                        for j in range(2):
                            last = mm(ps[CAP * j:CAP * (j + 1), bank, :], xgT[:, k, CAP * j:CAP * (j + 1)],
                                      ring[:, c + j, k * 512:(k + 1) * 512], start=(k == 0), stop=(k == KT - 1))
                    last.then_inc(out.sem, 1)
                pe.wait_ge(s_ye.sem, gg + 1)
                scatter().then_inc(s_scat.sem, 1)
                pe.wait_ge(s_sel.sem, gg + L + 2)
                gather()
                pe.wait_ge(s_selw.sem, gg + 1)
                pe.wait_ge(s_act.sem, gg + 1)
                for t in range(T):
                    last = tr(ps[:, 6, t * P:(t + 1) * P], selw[:, t].rearrange("p j s -> p (j s)"), ident)
                last.then_inc(s_swT_p.sem, 1)
                for k in range(FT):
                    last = tr(ps[:, 7, k * P:(k + 1) * P], act_h[:, k:FF:FT], ident)
                last.then_inc(s_hg_p.sem, 1)
                pe.wait_ge(s_slot[4].sem, pair_loaded(L, 4, pair))
                pe.wait_ge(s_slot[5].sem, pair_loaded(L, 5, pair))
                pe.wait_ge(s_hg.sem, gg + 2)
                pe.wait_ge(s_xg.sem, gg + L + 2)
                for f in range(2):
                    for k in range(FT):
                        for j in range(2):
                            last = mm(ps[CAP * j:CAP * (j + 1), 4 + f, :], hgT[:, k, CAP * j:CAP * (j + 1)],
                                      ring[:, 4 + j, k * D + f * 512:k * D + (f + 1) * 512],
                                      start=(k == 0), stop=(k == FT - 1))
                last.then_inc(s_down.sem, 1)
            pe.wait_ge(s_ye.sem, base + n_rounds + 1)
            scatter().then_inc(s_acc.sem, 1)

            transpose_h(2)
            pe.wait_ge(s_pin.sem, 16 * (L + 1))
            for k in range(2):
                for t in range(T):
                    last = tr(ps[:, 6, (2 * k + t) * P:(2 * k + t + 1) * P], pin[:, t, k:PLE:2], ident)
            last.then_inc(s_pl_p.sem, 1)
            pe.wait_ge(s_hT.sem, s_hT.at(L, 12))
            pe.wait_ge(s_pl.sem, L + 1)
            need(J_PLE)
            w = slot_view(J_PLE)
            for f in range(2):
                need(J_PG0 + f)
                for t in range(T):
                    i = 2 * f + t
                    b = 2 * (i % 2)
                    if i >= 2:
                        pe.wait_ge(s_pg.sem, s_pg.at(L, i + 3))
                    last = token_major(J_PG0 + f, t, b, 0, 512)
                    if t == 1:
                        last.then_inc(s_static_used.sem, 1)
                    for k in range(2):
                        last = mm(ps[:, b + 1, :], pinT[:, k, t * P:(t + 1) * P], w[:, k, f * 512:(f + 1) * 512],
                                  start=(k == 0), stop=(k == 1))
                    last.then_inc((s_pg_p if i < 3 else s_static_used).sem, 1)

    @block.scalar
    def _(act):
        def fn(*args, **kw):
            return nc.scalar.activation(*args, **kw)

        eps, one = table("eps"), table("one")
        act.wait_ge(s_trig.sem, 1)
        fn(cossin[:, :, :, :], cossin[:, :, :, :], ACT.Sin).then_inc(s_trigd.sem, 1)
        act.sem_inc(s_swT.sem, 1)
        act.sem_inc(s_hg.sem, 1)
        act.sem_inc(s_ye.sem, 1)
        act.wait_ge(s_x0.sem, 16)
        with act.Fori(0, L_N) as L:
            def rstd_of_x(n):
                for t in range(T):
                    fn(h[:, t, :], x[:, t, :], ACT.Square, accum_out=ss[:, t:t + 1])
                act.drain()
                fn(ss, ss, ACT.Ln, scale=1.0 / D, bias=eps)
                act.drain()
                fn(rstd, ss, ACT.Exp, scale=-0.5).then_inc(s_ss.sem, 1)

            act.wait_ge(s_pg.sem, 4 * (L + 1))
            rstd_of_x(0)
            act.wait_ge(s_par.sem, 48 * (L + 1))
            fn(nea, row("a_log"), ACT.Exp)
            for g in range(3):
                act.wait_ge(s_conv_y.sem, s_conv_y.at(L, g + 1))
                fn(conv_e, conv_y, ACT.Tanh, scale=0.5).then_inc(s_conv_e.sem, 1)
                if g == 2:
                    act.wait_ge(s_static_used.sem, chunk_used(L, J_CG))
                    fn(ba.rearrange("p t n -> p (t n)"), ps[:, 6, 0:16], ACT.Copy).then_inc(s_beta_e.sem, 1)
                    fn(cg, ps[:, 4:6, :], ACT.Tanh, scale=0.5).then_inc(s_gexp.sem, 1)
                    act.drain()
                    fn(beta, ba[:, :, 0:4], ACT.Tanh, scale=0.5).then_inc(s_beta_e.sem, 1)
                act.wait_ge(s_ct_p.sem, s_ct_p.at(L, g + 1))
                fn(ct[:, :, g * 512:(g + 1) * 512], ps[:, 2:4, :], ACT.Copy, scale=0.5
                   ).then_inc(s_ct.sem, 1)
            act.wait_ge(s_static_used.sem, chunk_used(L, J_BVT))
            act.wait_ge(s_zero.sem, 1)
            fn(blrT[0:RANK, :], ps[0:RANK, 7, 0:SEQ], ACT.Copy)
            fn(bt[:, :, 768:1024], ps[:, 0:2, 0:256], ACT.Copy).then_inc(s_pj_act.sem, 1)
            act.wait_ge(s_g.sem, s_g.at(L, 1))
            fn(gabs, gabs, ACT.Exp, scale=-1.0)
            act.drain()
            fn(gabs, gabs, ACT.Ln, bias=one).then_inc(s_beta_e.sem, 1)
            act.wait_ge(s_nsq.sem, L + 1)
            fn(ssq, ssq, ACT.Ln, bias=eps)
            act.drain()
            fn(ssq, ssq, ACT.Exp, scale=-0.5).then_inc(s_nr.sem, 1)
            act.wait_ge(s_G_p.sem, L + 1)
            fn(expG.rearrange("p t a h -> p (t a h)"), ps[:, 6, 64:96], ACT.Exp).then_inc(s_G.sem, 1)
            fn(negG, ps[:, 6, 64:96].rearrange("p (t a) -> p t a", t=T)[:, :, 0:4], ACT.Copy, scale=-1.0
               ).then_inc(s_G.sem, 1)
            act.wait_ge(s_static_used.sem, chunk_used(L, J_BR))
            fn(br, ps[:, 4:6, :], ACT.Tanh, scale=0.5).then_inc(s_gexp.sem, 1)
            def take_c(i, dst, b):
                act.wait_ge(s_trc_p.sem, s_trc_p.at(L, i + 1))
                for t in range(T):
                    last = fn(dst[:, :, t * P:(t + 1) * P], ps[:, b + t, :].rearrange("p (h n) -> p h n", h=H),
                              ACT.Copy)
                last.then_inc(s_trc.sem, 1)
            take_c(0, kT_c, 6)
            act.drain()
            for t in range(T):
                act.wait_ge(s_dm.sem, s_dm.at(L, t + 1))
                for hh in range(H):
                    last = fn(decT[:, t, hh, :], decT[:, t, hh, :], ACT.Exp, bias=negG[:, t, hh:hh + 1])
                last.then_inc(s_dec.sem, 1)
            act.wait_ge(s_static_used.sem, chunk_used(L, J_AKV))
            fn(aq[:, :, 512:768], ps[:, 0:2, 0:256], ACT.Copy)
            fn(bt[:, :, 0:256], ps[:, 0:2, 256:512], ACT.Copy).then_inc(s_pj_act.sem, 1)
            take_c(1, kbT_c, 4)
            take_c(2, qT_c, 6)
            take_c(3, qdT_c, 6)

            for l in range(LEVELS):
                for t in range(T):
                    act.wait_ge(s_P_p.sem, s_P_p.at(L, 2 * l + t + 1))
                    if l:
                        act.wait_ge(s_D_p.sem, s_D_p.at(L, 2 * (l - 1) + t + 1))
                    fn(Pm[:, t], ps[:, 2 + t, :].rearrange("p (h n) -> p h n", h=H), ACT.Copy).then_inc(s_P.sem, 1)
                if l in (1, 3):
                    act.wait_ge(s_static_used.sem, chunk_used(L, J_BK + l // 2))
                    if l == 1:
                        last = fn(bt[:, :, 256:768], ps[:, 0:2, :], ACT.Copy)
                    else:
                        last = fn(aq[:, :, 0:512], ps[:, 0:2, :], ACT.Copy)
                    last.then_inc(s_pj_act.sem, 1)
            act.wait_ge(s_z.sem, s_z.at(L, 2))
            fn(zab, zab, ACT.Exp, scale=-1.0)
            act.drain()
            fn(zab, zab, ACT.Ln, bias=one).then_inc(s_la.sem, 1)
            for t in range(T):
                act.wait_ge(s_wu_p.sem, s_wu_p.at(L, t + 1))
                act.wait_ge(s_trc.sem, s_trc.at(L, 4))
                fn(wT[:, :, t * P:(t + 1) * P], ps[:, 2 + t, :].rearrange("p (h n) -> p h n", h=H), ACT.Copy)
                fn(u[:, t, :], ps[:, 4 + t, :], ACT.Copy).then_inc(s_wu.sem, 1)

            act.wait_ge(s_b_p.sem, L + 1)
            fn(eb.rearrange("p t n -> p (t n)"), ps[:, 0, :], ACT.Exp)
            fn(enb.rearrange("p t n -> p (t n)"), ps[:, 0, :], ACT.Exp, scale=-1.0)
            fn(ea.rearrange("p t n -> p (t n)"), ps[:, 1, :], ACT.Exp)
            fn(decB.rearrange("p g t n -> p (g t n)"), ps[:, 4, 0:8], ACT.Exp).then_inc(s_b.sem, 1)
            act.wait_ge(s_trb_p.sem, L + 1)
            fn(qeT.rearrange("p g n -> p (g n)"), ps[:, 4, :], ACT.Copy)
            fn(keT.rearrange("p g n -> p (g n)"), ps[:, 5, :], ACT.Copy).then_inc(s_trb.sem, 1)

            def o_norm(n):
                act.wait_ge(s_on.sem, s_on.at(L, n + 1))
                fn(sso, sso, ACT.Ln, scale=4.0 / P, bias=table("eps4"))
                act.drain()
                fn(sso, sso, ACT.Exp, scale=-0.5).then_inc(s_onr.sem, 1)

            o_norm(0)
            o_norm(1)
            act.wait_ge(s_asq.sem, L + 1)
            fn(ssa, ssa, ACT.Ln, scale=1.0 / HD_A, bias=eps)
            act.drain()
            fn(ssa, ssa, ACT.Exp, scale=-0.5).then_inc(s_ar.sem, 1)
            def take_yT(n):
                act.wait_ge(s_yT_p.sem, s_yT_p.at(L, n + 1))
                for t in range(T):
                    last = fn(yT[:, :, t * P:(t + 1) * P], ps[:, 6 + t, :].rearrange("p (k n) -> p k n", k=4), ACT.Copy)
                last.then_inc(s_yT.sem, 1)

            def gate(i):
                if i % 4 < 3:
                    act.wait_ge(s_gt_p.sem, s_gt_p.at(L, 3 * (i // 4) + i % 4 + 1))
                else:
                    act.wait_ge(s_static_used.sem, chunk_used(L, J_GC1 + 3 * (i // 4)))
                if i >= 2:
                    act.wait_ge(s_mg.sem, s_mg.at(L, i - 1))
                fn(tmpA[:, i % 2, :], ps[:, i % 2, :], ACT.Tanh, scale=0.5).then_inc(s_gt_e.sem, 1)

            take_yT(0)
            for i in range(4):
                gate(i)
            act.wait_ge(s_tra_p.sem, L + 1)
            for t in range(T):
                fn(qT_a[:, :, t * P:(t + 1) * P], ps[:, 4 + t, :].rearrange("p (g n) -> p g n", g=4), ACT.Copy)
            fn(kTa, ps[:, 6, 0:256], ACT.Copy)
            fn(kTb, ps[:, 6, 256:512], ACT.Copy).then_inc(s_tra.sem, 1)
            take_yT(1)
            gate(4)
            gate(5)
            act.wait_ge(s_sx.sem, L + 1)
            fn(esink, esink, ACT.Exp)
            fn(scores, scores, ACT.Exp).then_inc(s_pe.sem, 1)
            gate(6)
            gate(7)
            for i in range(6):
                act.wait_ge(s_pt_p.sem, s_pt_p.at(L, i + 1))
                fn(pT[:, 4 * i:4 * i + 4, :], ps[:, 4 + i % 4, :].rearrange("p (k n) -> p k n", k=4), ACT.Copy
                   ).then_inc(s_pt.sem, 1)
            take_yT(2)
            for i in range(8, 12):
                gate(i)
            for q in range(4):
                act.wait_ge(s_mT_p.sem, s_mT_p.at(L, q + 1))
                t, half = divmod(q, 2)
                fn(hT[:, 4 * half:4 * half + 4, t * P:(t + 1) * P],
                   ps[:, 4 + q, :].rearrange("p (k n) -> p k n", k=4), ACT.Copy, scale=0.5).then_inc(s_mT.sem, 1)
            act.wait_ge(s_x.sem, s_x.at(L, 1))
            rstd_of_x(1)
            for i in range(2):
                act.wait_ge(s_rt.sem, s_rt.at(L, i + 1))
                if i == 0:
                    last = fn(lg[:, :, 0:GROUPS], lg[:, :, 0:GROUPS], ACT.Exp)
                else:
                    last = fn(e2, e2, ACT.Exp)
                last.then_inc(s_rte.sem, 1)
            act.wait_ge(s_tbl.sem, L + 1)
            base = plan(act, L, 48, 0, 4096)
            n_rounds = plan(act, L, 49, PAIRS, ROUNDS_LIMIT)
            act.wait_ge(s_init.sem, L + 1)
            with act.Fori(0, n_rounds) as g:
                gg = base + g
                act.wait_ge(s_gate.sem, gg + 1)
                fn(sig, ps[:, 6, :], ACT.Tanh, scale=0.5).then_inc(s_sig.sem, 1)
                act.wait_ge(s_scat.sem, gg + 1)
                act.wait_ge(s_swT_p.sem, gg + 2)
                fn(selwT, ps[:, 6, 0:256], ACT.Copy).then_inc(s_swT.sem, 1)
                act.wait_ge(s_hg_p.sem, gg + 1)
                fn(hgT.rearrange("p k n -> p (k n)"), ps[:, 7, :], ACT.Copy).then_inc(s_hg.sem, 1)
                act.wait_ge(s_down.sem, gg + 1)
                fn(ye.rearrange("p (f n) -> p f n", f=2), ps[:, 4:6, :], ACT.Copy).then_inc(s_ye.sem, 1)
            act.wait_ge(s_x.sem, s_x.at(L, 2))
            rstd_of_x(2)
            act.wait_ge(s_pl_p.sem, L + 1)
            fn(pinT.rearrange("p k n -> p (k n)"), ps[:, 6, :], ACT.Copy).then_inc(s_pl.sem, 1)
            for i in range(4):
                if i < 3:
                    act.wait_ge(s_pg_p.sem, s_pg_p.at(L, i + 1))
                else:
                    act.wait_ge(s_static_used.sem, chunk_used(L, J_PLE))
                fn(gtmp[:, i % 2, :], ps[:, 2 * (i % 2), :], ACT.Tanh, scale=0.5).then_inc(s_pg_e.sem, 1)

    @block.vector
    def _(dve):
        v = nc.vector
        tt, ts, stt = v.tensor_tensor, v.tensor_scalar, v.scalar_tensor_tensor

        def over(ap, shape):
            return ap.broadcast_to(shape)

        dve.sem_inc(s_par_used.sem, 1)
        for _i in range(4):
            dve.sem_inc(s_pg.sem, 1)
        dve.wait_ge(s_tab.sem, 32)
        trig = so2[:, :, :, :, :].rearrange("p a t h n -> p (a t h n)")
        n_trig = 2 * T * HALF
        posf, kf2, ang2 = trig[:, 0:T], trig[:, 16:16 + n_trig], trig[:, 64:64 + n_trig]
        kf = kf2.rearrange("p (w t n) -> p w t n", w=2, t=T)
        ang = ang2.rearrange("p (w t n) -> p w t n", w=2, t=T)
        v.tensor_copy(posf, posi[:, :])
        dve.drain()
        for w in range(2):
            tt(ang[:, w], over(posf.unsqueeze(2), [P, T, HALF]), over(table("inv_freq").unsqueeze(1), [P, T, HALF]),
               ALU.mult)
        dve.drain()
        for w in range(2):
            ts(kf[:, w], ang[:, w], float(1 / (2 * np.pi)), 0.25 if w == 0 else 0.0, ALU.mult, ALU.add)
        dve.drain()
        magic = float(1.5 * 2 ** 23)
        ts(kf, kf, magic, None, ALU.add)
        dve.drain()
        ts(kf, kf, magic, None, ALU.subtract)
        dve.drain()
        c1 = 6.28125
        c2 = float(np.float32(np.round((2 * np.pi - c1) * 2 ** 20) / 2 ** 20))
        c3 = float(2 * np.pi - c1 - c2)
        for c in (c1, c2, c3):
            stt(out=ang2, in0=kf2, scalar=-c, in1=ang2, op0=ALU.mult, op1=ALU.add)
            dve.drain()
        ts(ang[:, 0], ang[:, 0], float(np.pi / 2), None, ALU.add)
        dve.drain()
        ts(cossin[:, :, :, :], ang, 3.1415925, -3.1415925, ALU.min, ALU.max).then_inc(s_trig.sem, 1)
        v.memset(base_f[:, :], 0.0)
        dve.wait_ge(s_x0.sem, 16)
        dve.wait_ge(s_trigd.sem, 1)
        with dve.Fori(0, L_N) as L:
            def normed(n, gain):
                dve.wait_ge(s_ss.sem, s_ss.at(L, n + 1))
                for t in range(T):
                    ts(h[:, t, :], x[:, t, :], rstd[:, t:t + 1], None, ALU.mult).then_inc(s_h.sem, 1)
                if n == 0:
                    dve.wait_ge(s_par.sem, 48 * (L + 1))
                for q in range(4):
                    t, half = divmod(q, 2)
                    dve.wait_ge(s_hTp.sem, s_hTp.at(L, 4 * n + q + 1))
                    tt(hT[:, 4 * half:4 * half + 4, t * P:(t + 1) * P],
                       ps[:, 2 + q, :].rearrange("p (k n) -> p k n", k=4),
                       over(col(gain)[:, 4 * half:4 * half + 4].unsqueeze(2), [P, 4, P]), ALU.mult
                       ).then_inc(s_hT.sem, 1)

            def twice_gated(out, half_tanh, gated):
                return stt(out=out, in0=half_tanh, scalar=1.0, in1=gated, op0=ALU.add, op1=ALU.mult)

            normed(0, "attn_norm")
            taps = col("conv").rearrange("p (m j) -> p m j", j=4)

            def conv(g):
                b = 0 if g % 2 == 0 else 6
                dve.wait_ge(s_static_used.sem, chunk_used(L, J_CQ + g))
                if g:
                    dve.wait_ge(s_ct_p.sem, s_ct_p.at(L, g))
                src = ps[:, b:b + 2, :].rearrange("p a (m n) -> p (a m) n", m=2)
                for d in range(4):
                    for m in range(4):
                        w = taps[:, 4 * g + m, 3 - d:4 - d]
                        if d == 0:
                            last = ts(conv_y[:, m, :], src[:, m, :], w, None, ALU.mult)
                        else:
                            last = stt(out=conv_y[:, m, d:], in0=src[:, m, 0:SEQ - d], scalar=w,
                                       in1=conv_y[:, m, d:], op0=ALU.mult, op1=ALU.add)
                    if d < 3:
                        dve.drain()
                last.then_inc(s_conv_y.sem, 1)
                dve.wait_ge(s_conv_e.sem, s_conv_e.at(L, g + 1))
                twice_gated(conv_y, conv_e, conv_y).then_inc(s_conv_s.sem, 1)

            conv(0)
            conv(1)
            conv(2)
            dve.wait_ge(s_gexp.sem, s_gexp.at(L, 1))
            twice_gated(cg, cg, ps[:, 4:6, :]).then_inc(s_pj_dve.sem, 1)
            dve.wait_ge(s_beta_e.sem, s_beta_e.at(L, 2))
            tt(gdec, ba[:, :, 4:8], over(row("dt_bias").unsqueeze(1), [P, T, H]), ALU.add)
            ts(beta, beta, 1.0, 0.5, ALU.add, ALU.mult)
            dve.drain()
            stt(out=gabs, in0=gdec, scalar=-1.0, in1=gdec, op0=ALU.mult, op1=ALU.max).then_inc(s_g.sem, 1)
            dve.wait_ge(s_beta_e.sem, s_beta_e.at(L, 3))
            stt(out=gdec, in0=gdec, scalar=0.0, in1=gabs, op0=ALU.max, op1=ALU.add).then_inc(s_g.sem, 1)
            dve.wait_ge(s_g.sem, s_g.at(L, 2))
            stt(out=gdec, in0=gdec, scalar=-1.0, in1=over(nea.unsqueeze(1), [P, T, H]), op0=ALU.mult,
                op1=ALU.mult).then_inc(s_g.sem, 1)
            dve.wait_ge(s_g.sem, s_g.at(L, 3))
            v.tensor_copy(tmpA.rearrange("p t (h s) -> p t h s", h=H), over(gdec.unsqueeze(3), [P, T, H, P])
                          ).then_inc(s_g.sem, 1)

            def heads(ap):
                return ap.rearrange("p t (h n) -> p t h n", n=P)
            dve.wait_ge(s_ct.sem, s_ct.at(L, 3))
            for i in range(2):
                tt(kg, ct[:, :, i * 512:(i + 1) * 512], ct[:, :, i * 512:(i + 1) * 512], ALU.mult)
                dve.drain()
                last = v.tensor_reduce(ssq[:, :, 4 * i:4 * i + 4], heads(kg), AX.X, ALU.add)
                if i == 0:
                    dve.drain()
            last.then_inc(s_nsq.sem, 1)
            dve.wait_ge(s_nr.sem, L + 1)
            ts(ssq[:, :, 0:4], ssq[:, :, 0:4], float(128 ** -0.5), None, ALU.mult)
            dve.drain()
            qc, kc, vc = ct[:, :, 0:512], ct[:, :, 512:1024], ct[:, :, 1024:1536]

            def by_head(out, in0, scale, **kw):
                return tt(heads(out), heads(in0), over(scale.unsqueeze(3), [P, T, H, P]), ALU.mult)
            by_head(kc, kc, ssq[:, :, 4:8])
            by_head(qc, qc, ssq[:, :, 0:4]).then_inc(s_kqn.sem, 1)
            dve.drain()
            by_head(tmpk, kc, beta).then_inc(s_kb.sem, 1)
            by_head(vc, vc, beta)
            dve.wait_ge(s_gexp.sem, s_gexp.at(L, 2))
            twice_gated(br, br, ps[:, 4:6, :]).then_inc(s_pj_dve.sem, 1)
            dve.wait_ge(s_G.sem, s_G.at(L, 2))
            tt(betaG, beta, expG[:, :, 0, :], ALU.mult)
            dve.drain()
            by_head(kg, kc, betaG)
            by_head(kd, kc, expG[:, :, 1, :])
            for t in range(T):
                dve.wait_ge(s_Gr_p.sem, s_Gr_p.at(L, t + 1))
                tt(decT[:, t], ps[:, 2 + t, :].rearrange("p (h n) -> p h n", h=H),
                   over(table("not_causal_big").unsqueeze(1), [P, 4, P]), ALU.subtract).then_inc(s_dm.sem, 1)
            for t in range(T):
                dve.wait_ge(s_dec.sem, s_dec.at(L, t + 1))
                dve.wait_ge(s_A_p.sem, s_A_p.at(L, t + 1))
                tt(AT[:, t], ps[:, 2 + t, :].rearrange("p (h n) -> p h n", h=H), decT[:, t], ALU.mult
                   ).then_inc(s_A.sem, 1)
            for t in range(T):
                dve.wait_ge(s_at_p.sem, s_at_p.at(L, t + 1))
                tt(attG[:, t], ps[:, 4 + t, :].rearrange("p (h n) -> p h n", h=H), decT[:, t], ALU.mult
                   ).then_inc(s_at.sem, 1)
            dve.wait_ge(s_trc_p.sem, s_trc_p.at(L, 3))
            by_head(qc, qc, expG[:, :, 0, :]).then_inc(s_qd.sem, 1)
            for l in range(LEVELS):
                for t in range(T):
                    dve.wait_ge(s_D_p.sem, s_D_p.at(L, 2 * l + t + 1))
                    idb = over(ident.unsqueeze(1), [P, 4, P])
                    if l < LEVELS - 1:
                        tt(X[:, t], X[:, t] if l else idb, ps[:, 6 + t, :].rearrange("p (h n) -> p h n", h=H),
                           ALU.subtract)
                    tt(XT[:, t], XT[:, t] if l else idb, ps[:, 4 + t, :].rearrange("p (h n) -> p h n", h=H),
                       ALU.subtract).then_inc(s_X.sem, 1)
                dve.drain()
            def scan_v(n):
                t, r = n // 2, CHUNK * (n % 2)
                rs = slice(r, r + CHUNK)
                if n == 0:
                    dve.wait_ge(s_wu.sem, s_wu.at(L, 2))
                    v.tensor_copy(vnew[rs, t, :], u[rs, t, :]).then_inc(s_vn.sem, 1)
                else:
                    dve.wait_ge(s_ws.sem, s_ws.at(L, n))
                    tt(vnew[rs, t, :], u[rs, t, :], ps[rs, 6, :], ALU.subtract).then_inc(s_vn.sem, 1)

            def scan_S(n):
                t = n // 2
                dve.wait_ge(s_ds.sem, s_ds.at(L, n + 1))
                new = ps[:, 7, :].rearrange("p (h n) -> p h n", h=H)
                if n == 0:
                    v.tensor_copy(Sc, new).then_inc(s_S.sem, 1)
                else:
                    tt(Sc, Sc, over(expG[:, t, 2 + n % 2, :].unsqueeze(2), [P, H, P]), ALU.mult)
                    dve.drain()
                    tt(Sc, Sc, new, ALU.add).then_inc(s_S.sem, 1)
                dve.drain()

            diag = over(table("pair_diag").unsqueeze(1), [P, 2, 256])

            def gla_state(n):
                t = n // 2
                dve.wait_ge(s_du_p.sem, s_du_p.at(L, n + 1))
                new = ps[:, 1 - n % 2, :].rearrange("p (g n) -> p g n", g=2)
                if n == 0:
                    tt(Sb[:, 0], new, diag, ALU.mult).then_inc(s_Sb.sem, 1)
                else:
                    tt(dum, new, diag, ALU.mult)
                    dve.drain()
                    for g in range(2):
                        last = stt(out=Sb[:, n, g, :], in0=Sb[:, n - 1, g, :], scalar=decB[:, g, t, n % 2:n % 2 + 1],
                                   in1=dum[:, g, :], op0=ALU.mult, op1=ALU.add)
                    last.then_inc(s_Sb.sem, 1)
                dve.drain()

            dve.wait_ge(s_z.sem, s_z.at(L, 1))
            v.tensor_copy(la.rearrange("p t n -> p (t n)"), ps[:, 0, :])
            dve.drain()
            stt(out=zab, in0=la, scalar=-1.0, in1=la, op0=ALU.mult, op1=ALU.max).then_inc(s_z.sem, 1)
            scan_v(0)
            dve.wait_ge(s_la.sem, s_la.at(L, 1))
            stt(out=la, in0=la, scalar=0.0, in1=zab, op0=ALU.min, op1=ALU.subtract).then_inc(s_la.sem, 1)
            dve.wait_ge(s_la.sem, s_la.at(L, 2))
            ts(la, la, 1.0 / 16.0, None, ALU.mult).then_inc(s_lar.sem, 1)
            scan_S(0)
            scan_v(1)
            scan_S(1)
            dve.wait_ge(s_b.sem, L + 1)
            stt(out=qe, in0=bt[:, :, 0:256], scalar=float(DK_B ** -0.5), in1=eb, op0=ALU.mult, op1=ALU.mult)
            tt(ke, bt[:, :, 256:512], enb, ALU.mult)
            tt(kdb, bt[:, :, 256:512], ea, ALU.mult).then_inc(s_qke.sem, 1)
            gla_state(0)
            scan_v(2)
            scan_S(2)
            gla_state(1)
            for odd in range(2):
                dve.wait_ge(s_ab_p.sem, s_ab_p.at(L, odd + 1))
                tt(attB.rearrange("p t (g e) n -> p t g e n", e=2)[:, :, :, odd, :],
                   ps[:, 4 + odd, :].rearrange("p (t g n) -> p t g n", t=T, g=2),
                   over(causal.unsqueeze(1).unsqueeze(1), [P, T, 2, P]), ALU.mult).then_inc(s_ab.sem, 1)
            gla_state(2)
            scan_v(3)

            def head_norm(n, bank, gate, gain):
                y, sq = y_of[n], sq_of[n]
                for t in range(T):
                    dve.wait_ge(s_oc.sem, s_oc.at(L, 2 * n + t + 1))
                    v.tensor_copy(y[:, t, :], ps[:, bank + t, :]).then_inc(s_ot.sem, 1)
                dve.drain()
                tt(sq, y, y, ALU.mult)
                dve.drain()
                v.tensor_reduce(sso, heads(sq), AX.X, ALU.add).then_inc(s_on.sem, 1)
                tt(heads(gate), heads(gate), over(row(gain).unsqueeze(1).unsqueeze(1), [P, T, H, P]), ALU.mult)
                dve.wait_ge(s_onr.sem, s_onr.at(L, n + 1))
                by_head(y, y, sso)
                dve.drain()
                tt(y, y, gate, ALU.mult).then_inc(s_y.sem, 1)

            def merge(i):
                f, t = (i % 4) // 2, i % 2
                e = tmpA[:, t, :]
                dve.wait_ge(s_gt_e.sem, s_gt_e.at(L, i + 1))
                dst = merged[:, t, f * 512:(f + 1) * 512]
                if i < 4:
                    twice_gated(dst, e, ps[:, 2 + t, :]).then_inc(s_mg.sem, 1)
                else:
                    twice_gated(e, e, ps[:, 2 + t, :])
                    dve.drain()
                    tt(dst, dst, e, ALU.add).then_inc(s_mg.sem, 1)

            head_norm(0, 2, cg, "gdn_norm")
            head_norm(1, 4, br, "gla_norm")
            qk = aq[:, :, 0:QK_A].rearrange("p t (h n) -> p t h n", n=HD_A)
            sq = scores.rearrange("p h n -> p (h n)")[:, 0:T * QK_A].rearrange("p (t h n) -> p t h n", t=T, n=HD_A)
            tt(sq, qk, qk, ALU.mult)
            dve.drain()
            v.tensor_reduce(ssa, sq, AX.X, ALU.add).then_inc(s_asq.sem, 1)
            dve.wait_ge(s_ar.sem, L + 1)
            tt(qk, qk, over(ssa.unsqueeze(3), [P, T, 10, HD_A]), ALU.mult)
            dve.drain()
            tt(aq[:, :, 0:QK_A], aq[:, :, 0:QK_A], over(row("qk_gain").unsqueeze(1), [P, T, QK_A]), ALU.mult)
            dve.drain()
            cos = over(cossin[:, 0].unsqueeze(2), [P, T, 10, HALF])
            sin = over(cossin[:, 1].unsqueeze(2), [P, T, 10, HALF])
            x1, x2 = qk[:, :, :, 0:HALF], qk[:, :, :, HALF:ROT]
            tt(so2[:, 0], x1, cos, ALU.mult)
            tt(so2[:, 1], x2, sin, ALU.mult)
            tt(so2[:, 2], x2, cos, ALU.mult)
            tt(ra, x1, sin, ALU.mult)
            dve.drain()
            tt(x1, so2[:, 0], so2[:, 1], ALU.subtract)
            tt(x2, so2[:, 2], ra, ALU.add)
            dve.drain()
            v.tensor_copy(kswap[:, :, 0:64], aq[:, :, 576:640])
            v.tensor_copy(kswap[:, :, 64:128], aq[:, :, 512:576]).then_inc(s_ak.sem, 1)
            for i in range(4):
                merge(i)
            sc = float(HD_A ** -0.5)
            dve.wait_ge(s_sc_p.sem, s_sc_p.at(L, 1))
            for odd in range(2):
                last = stt(out=scores[:, odd:HEADS_A:2, 0:P], in0=ps[:, 4 + odd, :].rearrange("p (h n) -> p h n", n=P),
                           scalar=sc, in1=over(table("swa0").unsqueeze(1), [P, 4, P]), op0=ALU.mult, op1=ALU.add)
            last.then_inc(s_sc.sem, 1)
            merge(4)
            merge(5)
            dve.wait_ge(s_sc_p.sem, s_sc_p.at(L, 2))
            for odd, b in enumerate((6, 4)):
                last = stt(out=scores[:, odd:HEADS_A:2, P:3 * P],
                           in0=ps[:, b:b + 2, :].rearrange("p a (h n) -> p (a h) n", n=SEQ), scalar=sc,
                           in1=over(table("swa1").unsqueeze(1), [P, 4, SEQ]), op0=ALU.mult, op1=ALU.add)
            last.then_inc(s_sc.sem, 1)
            dve.drain()
            v.tensor_reduce(mx[:, 0, :], scores[:, :, 0:P], AX.X, ALU.max)
            v.tensor_reduce(mx[:, 1, :], scores[:, :, P:3 * P], AX.X, ALU.max)
            dve.drain()
            sink = over(row("sinks").unsqueeze(1), [P, T, HEADS_A])
            tt(mx, mx, sink, ALU.max)
            dve.drain()
            tt(esink, sink, mx, ALU.subtract)
            tt(scores[:, :, 0:P], scores[:, :, 0:P], over(mx[:, 0, :].unsqueeze(2), [P, 8, P]), ALU.subtract)
            tt(scores[:, :, P:3 * P], scores[:, :, P:3 * P], over(mx[:, 1, :].unsqueeze(2), [P, 8, SEQ]),
               ALU.subtract).then_inc(s_sx.sem, 1)
            merge(6)
            dve.wait_ge(s_pe.sem, L + 1)
            v.tensor_reduce(den[:, 0, :], scores[:, :, 0:P], AX.X, ALU.add)
            v.tensor_reduce(den[:, 1, :], scores[:, :, P:3 * P], AX.X, ALU.add)
            dve.drain()
            tt(den, den, esink, ALU.add)
            dve.drain()
            v.reciprocal(den, den)
            dve.drain()
            merge(7)
            for t in range(T):
                dve.wait_ge(s_pv.sem, s_pv.at(L, t + 1))
                for kv in range(KV_A):
                    last = tt(y_of[2][:, t, kv * 256:(kv + 1) * 256].rearrange("p (h n) -> p h n", n=HD_A),
                              ps[:, 4 + 2 * t + kv, :].rearrange("p (h n) -> p h n", n=P)[:, :, kv * HD_A:(kv + 1) * HD_A],
                              over(den[:, t, 4 * kv:4 * kv + 4].unsqueeze(2), [P, 4, HD_A]), ALU.mult)
            last.then_inc(s_y.sem, 1)
            for i in range(8, 12):
                merge(i)
            dve.drain()
            for i in range(4):
                f, t = divmod(i, 2)
                if t == 0:
                    dve.wait_ge(s_wo.sem, s_wo.at(L, f + 1))
                else:
                    dve.wait_ge(s_static_used.sem, chunk_used(L, J_WO0 + f))
                last = tt(x[:, t, f * 512:(f + 1) * 512], x[:, t, f * 512:(f + 1) * 512], ps[:, i, :], ALU.add)
            last.then_inc(s_x.sem, 1)
            normed(1, "ffn_norm")
            dve.wait_ge(s_static_used.sem, chunk_used(L, J_ROUTER))
            tt(lg, ps[:, 6, 0:128].rearrange("p (t n) -> p t n", t=T)[:, :, 0:36],
               over(row("b_router").unsqueeze(1), [P, T, 36]), ALU.add)
            dve.drain()
            gl = lg[:, :, 0:GROUPS]
            v.tensor_reduce(gmx, gl, AX.X, ALU.max)
            dve.drain()
            tt(gl, gl, over(gmx.unsqueeze(2), [P, T, GROUPS]), ALU.subtract)
            dve.drain()

            def first_max(dst, vals, top, desc, n):
                tt(dst, vals, top, ALU.is_equal)
                dve.drain()
                tt(dst, dst, over(desc.unsqueeze(1), [P, T, n]), ALU.mult)
                dve.drain()
                v.tensor_reduce(pk, dst, AX.X, ALU.max)
                dve.drain()
                tt(dst, dst, over(pk.unsqueeze(2), [P, T, n]), ALU.is_equal)
                dve.drain()
            ts(oh_g, gl, 0.0, None, ALU.is_equal)
            dve.drain()
            tt(oh_g, oh_g, over(table("desc4").unsqueeze(1), [P, T, GROUPS]), ALU.mult).then_inc(s_rt.sem, 1)
            dve.drain()
            v.tensor_reduce(pk, oh_g, AX.X, ALU.max)
            dve.drain()
            tt(oh_g, oh_g, over(pk.unsqueeze(2), [P, T, GROUPS]), ALU.is_equal)
            dve.drain()
            ts(msk_g, oh_g, BIG, -BIG, ALU.mult, ALU.add)
            fine = lg[:, :, GROUPS:36].rearrange("p t (g n) -> p t g n", g=GROUPS)
            fm4 = fm.rearrange("p t (g n) -> p t g n", g=GROUPS)
            tt(fm4, fine, over(oh_g.unsqueeze(3), [P, T, GROUPS, PER_GROUP]), ALU.mult)
            dve.drain()
            tt(fm4, fm4, over(msk_g.unsqueeze(3), [P, T, GROUPS, PER_GROUP]), ALU.add)
            dve.drain()
            v.tensor_reduce(m1, fm, AX.X, ALU.max)
            dve.drain()
            first_max(oh1, fm, over(m1.unsqueeze(2), [P, T, E]), table("desc32"), E)
            stt(out=fm, in0=oh1, scalar=-2 * BIG, in1=fm, op0=ALU.mult, op1=ALU.add)
            dve.drain()
            v.tensor_reduce(m2, fm, AX.X, ALU.max)
            dve.drain()
            tt(e2, m2, m1, ALU.subtract).then_inc(s_rt.sem, 1)
            first_max(oh2, fm, over(m2.unsqueeze(2), [P, T, E]), table("desc32"), E)
            tt(chosen, oh1, oh2, ALU.add).then_inc(s_ch.sem, 1)
            dve.wait_ge(s_rte.sem, s_rte.at(L, 2))
            v.tensor_reduce(gsum, gl, AX.X, ALU.add)
            ts(w1, e2, 1.0, None, ALU.add)
            dve.drain()
            tt(w1, w1, gsum, ALU.mult)
            dve.drain()
            v.reciprocal(w1, w1)
            dve.drain()
            tt(w2, w1, e2, ALU.mult)
            tt(wts, oh1, over(w1.unsqueeze(2), [P, T, E]), ALU.mult)
            dve.drain()
            tt(tmpe, oh2, over(w2.unsqueeze(2), [P, T, E]), ALU.mult)
            dve.drain()
            tt(wts, wts, tmpe, ALU.add)
            dve.wait_ge(s_pos_p.sem, L + 1)
            away = 10000.0
            stt(out=posm, in0=ps[:, 7, 0:2 * E].rearrange("p (t n) -> p t n", t=T), scalar=away, in1=chosen,
                op0=ALU.add, op1=ALU.mult)
            v.tensor_copy(counts, ps[:, 7, 2 * E:3 * E])
            dve.drain()
            ts(posm, posm, away, None, ALU.subtract)
            c2v = counts.rearrange("p (a j) -> p a j", j=2)
            tt(rtmp, c2v[:, :, 0], c2v[:, :, 1], ALU.max)
            v.memset(rounds, 1.0)
            dve.drain()
            for lim in range(CAP, SEQ, CAP):
                stt(out=rounds, in0=rtmp, scalar=float(lim), in1=rounds, op0=ALU.is_gt, op1=ALU.add)
                dve.drain()
            v.tensor_copy(cum, rounds)
            dve.drain()
            for sft in (1, 2, 4, 8):
                v.tensor_copy(rtmp, cum)
                dve.drain()
                tt(cum[:, sft:], rtmp[:, sft:], rtmp[:, 0:PAIRS - sft], ALU.add)
                dve.drain()
            tt(cmp3, over(table("iota32").unsqueeze(2), [P, ROUNDS_MAX, PAIRS]),
               over(cum.unsqueeze(1), [P, ROUNDS_MAX, PAIRS]), ALU.is_ge)
            dve.drain()
            v.tensor_reduce(pair_f, cmp3, AX.X, ALU.add)
            dve.drain()
            tt(cmp3, cmp3, over(rounds.unsqueeze(1), [P, ROUNDS_MAX, PAIRS]), ALU.mult)
            ts(pair_f, pair_f, float(PAIRS - 1), None, ALU.min)
            dve.drain()
            v.tensor_reduce(off_f, cmp3, AX.X, ALU.add)
            dve.drain()
            tt(off_f, table("iota32"), off_f, ALU.subtract)
            dve.drain()
            ts(off_f, off_f, float(CAP), None, ALU.mult)
            v.tensor_copy(row_f[:, 0:32], pair_f)
            ts(row_f[:, 32:48], cum, base_f[:, 0:1], None, ALU.add)
            v.tensor_copy(row_f[:, 48:49], base_f[:, :])
            v.tensor_copy(row_f[:, 49:50], cum[:, PAIRS - 1:PAIRS])
            dve.drain()
            v.tensor_copy(tbl[0:1, bass.ds(L * 64, 50)], row_f[0:1, 0:50])
            tt(base_f[:, :], base_f[:, :], cum[:, PAIRS - 1:PAIRS], ALU.add)
            dve.drain().then_inc(s_tbl.sem, 1)
            dve.wait_ge(s_tbl.sem, L + 1)
            base = plan(dve, L, 48, 0, 4096)
            n_rounds = plan(dve, L, 49, PAIRS, ROUNDS_LIMIT)

            def select(dst, pair, g):
                for t in range(T):
                    last = stt(out=dst[:, t], in0=over(posm[:, t, bass.ds(pair * 2, 2)].unsqueeze(2), [P, 2, CAP]),
                               scalar=off_f[:, bass.ds(g, 1)],
                               in1=over(table("iota64").unsqueeze(1), [P, 2, CAP]),
                               op0=ALU.subtract, op1=ALU.is_equal)
                return last

            def take_gathered():
                for half in range(2):
                    last = tt(xgT[:, 4 * half:4 * half + 4, :], ps[:, 4 + half, :].rearrange("p (k n) -> p k n", k=4),
                              over(col("ffn_norm")[:, 4 * half:4 * half + 4].unsqueeze(2), [P, 4, P]), ALU.mult)
                last.then_inc(s_xg.sem, 1)

            select(sel, 0, 0).then_inc(s_sel.sem, 1)
            dve.wait_ge(s_ga.sem, base + L + 1)
            take_gathered()
            with dve.Fori(0, n_rounds) as g:
                gg = base + g
                dve.drain()
                pair = plan(dve, L, g, 0, PAIRS - 1)
                nxt = plan(dve, L, g + 1, 0, PAIRS - 1)
                dve.wait_ge(s_swT_p.sem, gg + 1)
                select(selw, pair, g)
                dve.wait_ge(s_ga.sem, gg + L + 1)
                select(sel, nxt, g + 1).then_inc(s_sel.sem, 1)
                dve.drain()
                tt(selw, selw, over(wts[:, :, bass.ds(pair * 2, 2)].unsqueeze(3), [P, T, 2, CAP]), ALU.mult
                   ).then_inc(s_selw.sem, 1)
                dve.wait_ge(s_sig.sem, gg + 1)
                twice_gated(act_h, sig, ps[:, 6, :])
                dve.drain()
                dve.wait_ge(s_up.sem, gg + 1)
                stt(out=act_h, in0=act_h, scalar=0.5, in1=ps[:, 7, :], op0=ALU.mult, op1=ALU.mult
                    ).then_inc(s_act.sem, 1)
                dve.wait_ge(s_ga.sem, gg + L + 2)
                take_gathered()
            dve.wait_ge(s_acc.sem, L + 1)
            for t in range(T):
                last = tt(x[:, t, :].rearrange("p (f n) -> p f n", f=2), x[:, t, :].rearrange("p (f n) -> p f n", f=2),
                          ps[:, 2 * t:2 * t + 2, :], ALU.add)
            last.then_inc(s_x.sem, 1)
            normed(2, "ple_norm")
            dve.drain().then_inc(s_par_used.sem, 1)
            for i in range(4):
                f, t = divmod(i, 2)
                e = gtmp[:, i % 2, :]
                dve.wait_ge(s_pg_e.sem, s_pg_e.at(L, i + 1))
                twice_gated(e, e, ps[:, 2 * (i % 2) + 1, :])
                dve.drain()
                xs = x[:, t, f * 512:(f + 1) * 512]
                stt(out=xs, in0=e, scalar=0.5, in1=xs, op0=ALU.mult, op1=ALU.add).then_inc(s_pg.sem, 1)


def kernel(**inputs):
    import concourse.bacc as bacc
    from concourse.bass_utils import run_bass_kernel_spmd

    i = {k: np.asarray(v) for k, v in inputs.items()}
    L = i["w_in"].shape[0]

    def by_feature(g):
        return g.reshape(L, P, -1)

    conv = i["gdn_conv"].transpose(0, 2, 1).reshape(L, 12, P, 4).transpose(0, 2, 1, 3).reshape(L, P, 48)
    arrays = {
        "x": i["x"].reshape(SEQ, D),
        "p": i["p"].reshape(L, SEQ, PLE),
        "positions": i["positions"].reshape(SEQ),
        "tables": TABLES,
        "cols": np.concatenate([by_feature(i["attn_norm"]), by_feature(i["ffn_norm"]), by_feature(i["ple_norm"]),
                                conv], -1),
        "rows": np.concatenate([np.tile(i["q_norm"], (1, HEADS_A)), np.tile(i["k_norm"], (1, KV_A)), i["gla_norm"],
                                i["gdn_norm"], i["sinks"], i["gdn_dt_bias"], i["gdn_a_log"], i["b_coarse"],
                                i["b_fine"]], -1),
        "wa2": np.concatenate([i["gla_wa2"], i["gla_ba"][:, None, :]], 1),
        "w_router": np.concatenate([i["w_coarse"], i["w_fine"]], -1),
    }
    for name in ("w_in", "w_br_a", "w_br_b", "w_br_c", "w_o", "w_gate_e", "w_up_e", "w_down_e", "w_ple_gate",
                 "w_ple"):
        arrays[name] = i[name]
    nc = bacc.Bacc("TRN2", target_bir_lowering=False, num_devices=1)
    a = {"x_layers": L}
    feed = {}
    for name, v in arrays.items():
        v = np.ascontiguousarray(v)
        feed[f"in_{name}"] = v
        a[name] = nc.dram_tensor(f"in_{name}", v.shape, mybir.dt.from_np(v.dtype), kind="ExternalInput").ap()
    a["out"] = nc.dram_tensor("out_x", (SEQ, D), F32, kind="ExternalOutput").ap()
    build(nc, a)
    r = run_bass_kernel_spmd(nc, [feed], core_ids=[0])
    return r.results[0]["out_x"].reshape(inputs["x"].shape)
```

```python
from contextlib import ExitStack

import numpy as np
import concourse.bass as bass
from concourse import mybir

F32 = mybir.dt.float32
I32 = mybir.dt.int32
ALU = mybir.AluOpType
ACT = mybir.ActivationFunctionType
AX = mybir.AxisListType

P = 128
D = 1024
SEQ = 256
T = SEQ // P
KT = D // P
EPS = 1e-6
BIG = 1e30
HEADS_A, KV_A, HD_A = 8, 2, 64
QK_A = (HEADS_A + KV_A) * HD_A
ROT = HD_A // 4
HALF = ROT // 2
H = 4
DK_B = 64
CHUNK = 64
RANK = 16
E = 32
GROUPS = 4
PER_GROUP = E // GROUPS
PAIRS = E // 2
FF = 512
FT = FF // P
CAP = 64
ROUNDS_MAX = 32
ROUNDS_LIMIT = PAIRS + 2 * SEQ // (CAP + 1)
PLE = 256
SLOT = 8 * 520

C_AQ, C_AK, C_BQ, C_BK, C_BV, C_LR, C_BR = 0, 512, 768, 1024, 1280, 1792, 1808
C_CQKV, C_BETA, C_CG, C_GATE = 2320, 3856, 3864, 4376

STATIC = [
    ("w_in", C_CQKV, 512), ("w_in", C_CQKV + 512, 512), ("w_in", C_CQKV + 1024, 512),
    ("w_in", C_BETA, 520), ("w_in", C_BV + 256, 272), ("w_in", C_BR, 512),
    ("w_in", C_AK, 512), ("w_in", C_BK, 512), ("w_in", C_AQ, 512),
    ("w_in", C_GATE + 2048, 512), ("w_br_c", 0, 1024), ("w_in", C_GATE + 2560, 512),
    ("w_in", C_GATE + 1024, 512), ("w_br_b", 0, 1024), ("w_in", C_GATE + 1536, 512),
    ("w_in", C_GATE, 512), ("w_br_a", 0, 1024), ("w_in", C_GATE + 512, 512),
    ("w_o", 0, 512), ("w_o", 512, 512), ("w_router", 0, 36),
    ("w_ple_gate", 0, 512), ("w_ple_gate", 512, 512), ("w_ple", 0, 1024),
]
(J_CQ, J_CK, J_CV, J_CG, J_BVT, J_BR, J_AKV, J_BK, J_AQ, J_GC0, J_WC, J_GC1, J_GB0, J_WB, J_GB1,
 J_GA0, J_WA, J_GA1, J_WO0, J_WO1, J_ROUTER, J_PG0, J_PG1, J_PLE) = range(24)
BEFORE_MOE = J_ROUTER + 1
NS = len(STATIC)

_s = np.arange(P)[:, None]
_c = np.arange(P)[None, :]
_same = _s // CHUNK == _c // CHUNK
LEVELS = 6


FIRST_TABLES = ("ident", "eps", "eps4", "one")


def _tables():
    t = {}
    t["ident"] = _s == _c
    t["causal"] = (_s <= _c) & _same
    t["after"] = (_s > _c) & _same
    t["chunk0"] = np.broadcast_to(_s < CHUNK, (P, P))
    t["chunk1"] = np.broadcast_to(_s >= CHUNK, (P, P))
    t["not_causal_big"] = np.where((_s <= _c) & _same, 0.0, BIG)
    for l in range(LEVELS):
        b = 1 << l
        t[f"level{l}"] = (_s // (2 * b) == _c // (2 * b)) & (_s // b % 2 == 0) & (_c // b % 2 == 1)
    t["ones"] = np.ones((P, P))
    t["before"] = _s < _c
    t["swa0"] = np.where(_c <= _s, 0.0, -BIG)
    k = np.arange(2 * P)[None, :]
    t["swa1"] = np.where((k > _s) & (k <= _s + P), 0.0, -BIG)
    t["pair_diag"] = (_s // DK_B) == (k // P)
    up_to = np.arange(PAIRS)[None, :] <= np.arange(PAIRS)[:, None]
    t["up_to"] = np.broadcast_to(up_to.reshape(-1), (P, PAIRS * PAIRS))
    t["iota64"] = np.broadcast_to(np.arange(CAP), (P, CAP))
    t["iota32"] = np.broadcast_to(np.arange(ROUNDS_MAX), (P, ROUNDS_MAX))
    t["desc32"] = np.broadcast_to(E - np.arange(E), (P, E))
    t["desc4"] = np.broadcast_to(GROUPS - np.arange(GROUPS), (P, GROUPS))
    t["eps"] = np.full((P, 1), EPS)
    t["eps4"] = np.full((P, 1), 4 * EPS)
    t["one"] = np.ones((P, 1))
    at, off, parts = {}, 0, []
    for name, a in sorted(t.items(), key=lambda item: item[0] not in FIRST_TABLES):
        at[name] = (off, a.shape[1])
        off += a.shape[1]
        parts.append(np.asarray(a, np.float32))
    return at, np.concatenate(parts, 1)


TABLE_AT, TABLES = _tables()
FIRST_N = sum(TABLE_AT[name][1] for name in FIRST_TABLES)
INV_FREQ = np.float32(1.0) / np.float32(500000.0) ** (np.arange(0, ROT, 2, dtype=np.float32) / np.float32(ROT))

ROWS = {"qk_gain": QK_A, "gla_norm": 128, "gdn_norm": 128, "sinks": HEADS_A, "dt_bias": H, "a_log": H,
        "b_router": 36}
ROW_AT, _o = {}, 0
for _n, _w in ROWS.items():
    ROW_AT[_n] = (_o, _w)
    _o += _w
ROW_N = _o
COLS = {"attn_norm": KT, "ffn_norm": KT, "ple_norm": KT, "conv": 48}
COL_AT, _o = {}, 0
for _n, _w in COLS.items():
    COL_AT[_n] = (_o, _w)
    _o += _w
COL_N = _o


class Signal:

    def __init__(self, sem, per):
        self.sem, self.per = sem, per

    def at(self, layer, k):
        return layer * self.per + k


def build(nc, a):
    with ExitStack() as ctx:
        _build(nc, a, ctx)


def _build(nc, a, ctx):
    L_N = a["x_layers"]

    def sb(name, shape, dt=F32):
        return ctx.enter_context(nc.sbuf_tensor(name, shape, dt))

    def signal(name, per=1):
        return Signal(ctx.enter_context(nc.semaphore(name)), per)

    ring = sb("ring", [P, 6, SLOT])
    tab = sb("tab", [P, TABLES.shape[1]])
    rows = sb("rows", [P, ROW_N])
    cols = sb("cols", [P, COL_N])
    wa2 = sb("wa2", [RANK + 1, 256])
    blrT = sb("blrT", [RANK + 1, SEQ])
    x = sb("x", [P, T, D])
    h = sb("h", [P, T, D])
    hT = sb("hT", [P, KT, SEQ])
    cossin = sb("cossin", [P, 2, T, HALF])
    posi = sb("posi", [P, T], I32)
    small = sb("small", [P, 512])
    big_a = sb("big_a", [P, 16384])
    ps = ctx.enter_context(nc.psum_tensor("ps", [P, 8, 512], F32))

    class Arena:
        def __init__(self, ap):
            self.ap, self.off, self.size = ap, 0, ap.shape[1]

        def take(self, *dims, at=None):
            n = int(np.prod(dims))
            off = self.off if at is None else at
            if at is None:
                self.off += n
            assert off + n <= self.size, (off + n, self.size)
            v = self.ap[:, off:off + n]
            if len(dims) == 2:
                return v.rearrange("p (a b) -> p a b", a=dims[0])
            if len(dims) == 3:
                return v.rearrange("p (a b c) -> p a b c", a=dims[0], b=dims[1])
            return v

    A = Arena(big_a[:, :])
    scratch = Arena(ring[:, 3:6, :].rearrange("p s n -> p (s n)"))

    def table(name):
        o, n = TABLE_AT[name]
        return tab[:, o:o + n]

    def row(name):
        o, n = ROW_AT[name]
        return rows[:, o:o + n]

    def col(name):
        o, n = COL_AT[name]
        return cols[:, o:o + n]

    ident = table("ident")
    causal, after = table("causal"), table("after")

    ct = A.take(T, 1536)
    kT_c = A.take(4, SEQ)
    kbT_c = A.take(4, SEQ)
    qT_c = A.take(4, SEQ)
    qdT_c = A.take(4, SEQ)
    cg = A.take(T, 512)
    br = A.take(T, 512)
    bt = A.take(T, 1024)
    aq = A.take(T, 768)
    yT = A.take(4, SEQ)
    tmpA = A.take(T, 512)
    tmpk = scratch.take(T, 512)
    kg = scratch.take(T, 512)
    kd = scratch.take(T, 512)
    decT = scratch.take(T, 4, P)
    AT = scratch.take(T, 4, P)
    lower = scratch.take(T, 4, P)
    X = scratch.take(T, 4, P)
    XT = scratch.take(T, 4, P)
    Pm = scratch.take(T, 4, P)
    attG = scratch.take(T, 4, P)
    vnew = scratch.take(T, 512)
    Sc = scratch.take(4, P)
    conv_y = scratch.take(4, SEQ, at=3 * 1024)
    conv_e = scratch.take(4, SEQ, at=4 * 1024)
    wT, u = kbT_c, qT_c.rearrange("p h c -> p (h c)").rearrange("p (t n) -> p t n", t=T)
    la = scratch.take(T, 256, at=3 * 1024)
    zab = scratch.take(T, 256, at=3 * 1024 + 512)
    h_flat = h.rearrange("p t d -> p (t d)")

    def in_h(i):
        return h_flat[:, 512 * i:512 * (i + 1)].rearrange("p (t n) -> p t n", t=T)
    eb, enb, ea = in_h(0), in_h(1), in_h(2)
    qe, ke, kdb = eb, enb, ea
    Sb = scratch.take(3, 2, 256, at=4 * 1024)
    dum = scratch.take(2, 256, at=4 * 1024 + 1536)
    qeT = scratch.take(2, SEQ, at=6 * 1024)
    keT = scratch.take(2, SEQ, at=6 * 1024 + 512)
    attB = scratch.take(T, 4, P, at=8 * 1024)
    y_of = [scratch.take(T, 512, at=at) for at in (0, 7 * 1024, 0)]
    sq_of = [scratch.take(T, 512, at=at) for at in (1024, 2 * 1024)]
    merged = scratch.take(T, D, at=9 * 1024)
    kswap = scratch.take(T, P, at=11 * 1024)
    kTa = scratch.take(SEQ, at=11 * 1024 + 256)
    kTb = scratch.take(SEQ, at=11 * 1024 + 512)
    scores = A.take(HEADS_A, 3 * P, at=0)
    pT = A.take(24, P, at=3072)
    qT_a = qdT_c
    M = Arena(big_a[:, :])
    sel = M.take(T, 2, CAP)
    selw = M.take(T, 2, CAP)
    selwT = M.take(SEQ)
    xgT = M.take(KT, P)
    sig = M.take(FF)
    act_h = M.take(FF)
    hgT = M.take(FT, P)
    ye = M.take(D)
    lg = M.take(T, 36)
    oh_g = M.take(T, GROUPS)
    msk_g = M.take(T, GROUPS)
    fm = M.take(T, E)
    tmpe = M.take(T, E)
    oh1 = M.take(T, E)
    oh2 = M.take(T, E)
    wts = M.take(T, E)
    chosen = M.take(T, E)
    posm = M.take(T, E)
    counts = M.take(E)
    rounds = M.take(PAIRS)
    rtmp = M.take(PAIRS)
    cum = M.take(PAIRS)
    cmp3 = M.take(ROUNDS_MAX, PAIRS)
    pair_f = M.take(ROUNDS_MAX)
    off_f = M.take(ROUNDS_MAX)
    row_f = M.take(64)
    pin = M.take(T, PLE)
    pinT = act_h.rearrange("p (k n) -> p k n", k=2)
    gtmp = xgT.rearrange("p k n -> p (k n)").rearrange("p (t n) -> p t n", t=T)
    even_gates = M.take(2, KT * 512)
    even_up = (hT.rearrange("p k n -> p (k n)"), M.take(KT * 512 // 2))
    tbl = sb("tbl", [1, L_N * 64], I32)
    base_f = sb("base_f", [P, 1])

    so = [0]

    def sm(*dims):
        n = int(np.prod(dims))
        v = small[:, so[0]:so[0] + n]
        so[0] += n
        assert so[0] <= 512
        if len(dims) == 2:
            return v.rearrange("p (a b) -> p a b", a=dims[0])
        if len(dims) == 3:
            return v.rearrange("p (a b c) -> p a b c", a=dims[0], b=dims[1])
        return v

    warm = sm(2)
    ss = sm(T)
    rms = sm(T)
    rstd = sm(T)
    ba = sm(T, 8)
    beta = sm(T, H)
    gdec = sm(T, H)
    gabs = sm(T, H)
    nea = sm(H)
    expG = sm(T, 4, H)
    negG = sm(T, H)
    betaG = sm(T, H)
    ssq = sm(T, 8)
    decB = sm(2, T, 2)
    ssa = sm(T, 10)
    mx = sm(T, HEADS_A)
    den = sm(T, HEADS_A)
    esink = sm(T, HEADS_A)
    ra = [sm(T, 10, HALF) for _ in range(1)][0]
    inv_freq = sb("inv_freq", [P, HALF])
    so2 = sb("rope_tmp", [P, 3, T, 10, HALF])
    sso = sm(2, T, H)
    rmso = sm(2, T, H)
    gmx = sm(T)
    m1 = sm(T)
    m2 = sm(T)
    gsum = sm(T)
    e2 = sm(T)
    w1 = sm(T)
    w2 = sm(T)
    pk = sm(T)

    s_tab0 = signal("first_tables_loaded")
    s_tab = signal("tables_loaded")
    s_x0 = signal("x_loaded")
    s_posi = signal("positions_loaded")
    s_par = signal("params_loaded", 3)
    s_par_used = signal("params_used")
    s_pin = signal("ple_input_loaded")
    s_slot = [signal(f"slot{i}_loaded") for i in range(6)]
    s_static_used = signal("static_chunk_used", NS)
    s_trig = signal("trig_args_ready")
    s_trigd = signal("trig_done")
    s_zero = signal("zeros_ready")
    s_ss = signal("rms_ready", 3 * T)
    s_h = signal("h_normed")
    s_rs = signal("ple_rstd_ready")
    s_hTp = signal("h_transposed", 3 * 4)
    s_hT = signal("hT_ready", 3 * 4)
    s_conv_y = signal("conv_out_ready", 3)
    s_conv_e = signal("conv_exp_ready", 3)
    s_conv_s = signal("conv_silu_ready", 3)
    s_ct_p = signal("conv_transposed", 3)
    s_ct = signal("ct_ready", 3)
    s_pj_dve = signal("output_gate_taken", 2)
    s_pj_act = signal("projection_taken", 4)
    s_gexp = signal("gate_tanh_ready", 2)
    s_nsq = signal("head_squares_ready")
    s_nr = signal("head_norms_ready")
    s_beta_e = signal("beta_exp_ready", 3)
    s_g = signal("g_ready", 4)
    s_G_p = signal("G_summed")
    s_G = signal("G_exps_ready", 2)
    s_Gr_p = signal("G_rows_ready", T)
    s_dm = signal("decay_args_ready", T)
    s_dec = signal("decay_ready", T)
    s_kqn = signal("k_q_normed")
    s_kb = signal("k_beta_ready")
    s_trc_p = signal("c_transposed", 4)
    s_trc = signal("c_transposed_taken", 4)
    s_qd = signal("q_decayed")
    s_A_p = signal("kk_products", T)
    s_A = signal("AT_ready", T)
    s_at_p = signal("qk_products", T)
    s_at = signal("attG_ready", T)
    s_lv = signal("level_blocks_ready", LEVELS * T)
    s_P_p = signal("level_P", LEVELS * T)
    s_P = signal("level_P_taken", (LEVELS - 1) * T)
    s_D_p = signal("level_D", (LEVELS - 1) * T)
    s_X = signal("inverse_updated", LEVELS * T)
    s_wu_p = signal("w_u_products", T)
    s_wu = signal("w_u_ready", T)
    s_ws = signal("w_state", 3)
    s_vn = signal("v_new_ready", 4)
    s_ds = signal("state_product", 3)
    s_S = signal("state_ready", 3)
    s_oc = signal("o_products", 2 * T)
    s_onr = signal("o_norm_ready", 2)
    s_y = signal("y_ready", 3)
    s_yT_p = signal("y_transposed", 3)
    s_yT = signal("yT_ready", 3)
    s_gt_p = signal("merge_products", 9)
    s_gt_e = signal("merge_gate_tanhs", 12)
    s_mg = signal("merge_added", 12)
    s_z = signal("z_ready", 2)
    s_la = signal("log_a_exp", 2)
    s_lar = signal("log_a_ready")
    s_b_p = signal("b_summed")
    s_b = signal("b_exps_ready")
    s_qke = signal("gla_operands_ready")
    s_trb_p = signal("gla_transposed")
    s_trb = signal("gla_transposed_taken")
    s_ab_p = signal("gla_products", T)
    s_ab = signal("gla_att_ready", T)
    s_du_p = signal("gla_state_products", 3)
    s_Sb = signal("gla_states_ready", 3)
    s_asq = signal("swa_squares_ready")
    s_ar = signal("swa_rms_ready")
    s_ak = signal("swa_roped")
    s_tra_p = signal("swa_transposed")
    s_tra = signal("swa_transposed_taken")
    s_sc_p = signal("scores_products", T)
    s_sc = signal("scores_masked", T)
    s_sx = signal("scores_centered")
    s_pe = signal("probs_ready")
    s_pt_p = signal("probs_transposed", 6)
    s_pt = signal("probs_taken", 6)
    s_pv = signal("pv_products", T)
    s_mT_p = signal("merged_transposed", 4)
    s_mT = signal("merged_taken", 4)
    s_wo = signal("wo_products", 2)
    s_x = signal("x_updated", 2 * T)
    s_rt = signal("router_exp_args", 2)
    s_rte = signal("router_exps", 2)
    s_ch = signal("chosen_ready")
    s_pos_p = signal("positions_summed")
    s_tbl = signal("rounds_planned")
    s_pairs = signal("pairs_of_rounds_planned")
    s_init = signal("moe_zeroed")
    s_sel0 = signal("first_selection_ready")
    s_ga0 = signal("first_gathered")
    s_even = [signal(f"even_gate_{j}_loaded") for j in range(2)]
    s_even_up = signal("even_up_loaded")
    s_sel = signal("selection_ready")
    s_selw = signal("weighted_selection_ready")
    s_ga = signal("gathered")
    s_xg = signal("gathered_taken")
    s_gate = signal("gate_done")
    s_up = signal("up_done")
    s_down = signal("down_done")
    s_sig = signal("silu_tanh_ready")
    s_act = signal("act_ready")
    s_swT_p = signal("weighted_selection_transposed")
    s_swT = signal("weighted_selection_taken")
    s_hg_p = signal("act_transposed")
    s_hg = signal("act_taken")
    s_ye = signal("expert_out_taken")
    s_scat = signal("scattered")
    s_acc = signal("moe_done")
    s_pl_p = signal("ple_transposed")
    s_pl = signal("ple_taken")
    s_pg_p = signal("ple_products", 3)
    s_pg_e = signal("ple_gate_tanhs", 4)
    s_pg = signal("ple_added", 4)
    s_out = signal("out_stored")

    BEFORE, ROUNDS_AT = ROUNDS_MAX, ROUNDS_MAX + PAIRS + 1

    def plan(eng, L, at, lo, hi):
        return eng.value_load(tbl[0:1, bass.ds(L * 64 + at, 1)], min_val=lo, max_val=hi)

    block = ctx.enter_context(nc.Block())

    def slot_view(j):
        name, c0, n = STATIC[j]
        kt = {"w_br_a": 4, "w_br_b": 4, "w_br_c": 4, "w_ple": 2}.get(name, KT)
        return ring[:, j % 3, 0:kt * n].rearrange("p (k n) -> p k n", k=kt)

    def chunk_used(L, j):
        return L * NS + 3 + j + 1

    def pair_loads(c):
        return PAIRS // 2 if c < 3 else PAIRS

    def loads_before(L, c):
        return L * ((NS // 3 if c < 3 else 0) + pair_loads(c))

    def slot_loaded(L, j):
        c = j % 3
        return 16 * (loads_before(L, c) + j // 3 + 1 + (pair_loads(c) if j >= BEFORE_MOE else 0))

    def pair_loaded(L, c, n):
        return 16 * (loads_before(L, c) + (BEFORE_MOE // 3 if c < 3 else 0) + n + 1)

    @block.sync
    def _(sp):
        sp.dma_start(posi[:, :], a["positions"].rearrange("(t p) -> p t", p=P),
                     allow_slow_non_contiguous=True).then_inc(s_posi.sem, 16)
        sp.dma_start(x[:, :, :], a["x"].rearrange("(t p) d -> p t d", p=P)).then_inc(s_x0.sem, 16)
        sp.dma_start(tab[:, 0:FIRST_N], a["tables"][:, 0:FIRST_N]).then_inc(s_tab0.sem, 16)
        moe = {"w_gate_e": a["w_gate_e"].rearrange("l e (p k) n -> (l e) p (k n)", k=KT),
               "w_up_e": a["w_up_e"].rearrange("l e (p k) n -> (l e) p (k n)", k=KT),
               "w_down_e": a["w_down_e"].rearrange("l e (p k) n -> (l e) p (k n)", k=FT)}

        def one(ap, i):
            return ap[bass.ds(i, 1)]

        with sp.Fori(0, L_N) as L:
            sp.wait_ge(s_par_used.sem, s_par_used.at(L, 1))
            sp.dma_start(cols[:, :], one(a["cols"], L).rearrange("l p n -> (l p) n")).then_inc(s_par.sem, 16)
            sp.dma_start(rows[:, :], one(a["rows"], L).rearrange("l n -> (l n)").partition_broadcast(P)
                         ).then_inc(s_par.sem, 16)
            sp.dma_start(wa2[:, :], one(a["wa2"], L).rearrange("l k n -> (l k) n")).then_inc(s_par.sem, 16)

            def load_static(j):
                name, c0, n = STATIC[j]
                kt = slot_view(j).shape[1]
                src = one(a[name], L)[:, :, c0:c0 + n].rearrange("l (p k) n -> (l p) k n", k=kt)
                sp.dma_start(slot_view(j), src).then_inc(s_slot[j % 3].sem, 16)

            for j in range(BEFORE_MOE):
                if j != J_AQ:
                    sp.wait_ge(s_static_used.sem, chunk_used(L, j - 2 if j == J_BK else j - 3))
                load_static(j)

            def load_matrix(i, c, place, signal_):
                name = ("w_gate_e", "w_up_e", "w_down_e")[c // 2]
                sp.dma_start(place, one(moe[name], L * E + 2 * i + c % 2).rearrange("l p n -> (l p) n")
                             ).then_inc(signal_.sem, 16)

            def load_pair(i, c):
                load_matrix(i, c, ring[:, c, 0:4096], s_slot[c])

            def load_even_gates(i):
                for j in range(2):
                    load_matrix(i, j, even_gates[:, j, :], s_even[j])

            def load_even_up(i):
                src = one(moe["w_up_e"], L * E + 2 * i).rearrange("l p n -> (l p) n")
                for half in range(2):
                    sp.dma_start(even_up[half], src[:, half * 2048:(half + 1) * 2048]).then_inc(s_even_up.sem, 16)

            sp.wait_ge(s_mT.sem, s_mT.at(L, 4))
            load_even_gates(0)
            for c in range(3, 6):
                load_pair(0, c)
            for c in range(3):
                sp.wait_ge(s_static_used.sem, chunk_used(L, BEFORE_MOE + c - 3))
                load_pair(1, c)
            load_even_up(0)
            sp.wait_ge(s_tbl.sem, L + 1)
            total = plan(sp, L, BEFORE + PAIRS, 1, 4096)

            def behind(signal_, i):
                done = plan(sp, L, BEFORE + i, 1, 4096)
                sp.wait_ge(signal_.sem, done)

            def load_up_down(i, next_up):
                behind(s_up, i)
                load_pair(i, 3)
                next_up()
                behind(s_down, i)
                load_pair(i, 4)
                load_pair(i, 5)

            def load_odd_gates(i):
                load_pair(i, 0)
                load_pair(i, 1)

            behind(s_gate, 1)
            load_even_gates(2)
            with sp.Fori(0, PAIRS // 2 - 2) as ii:
                odd = 2 * ii + 1
                load_up_down(odd, lambda: load_even_up(odd + 1))
                behind(s_gate, odd + 1)
                load_odd_gates(odd + 2)
                load_up_down(odd + 1, lambda: load_pair(odd + 2, 2))
                behind(s_gate, odd + 2)
                load_even_gates(odd + 3)
            load_up_down(PAIRS - 3, lambda: load_even_up(PAIRS - 2))
            load_up_down(PAIRS - 2, lambda: load_pair(PAIRS - 1, 0))
            load_pair(PAIRS - 1, 1)
            load_pair(PAIRS - 1, 2)
            load_up_down(PAIRS - 1, lambda: None)
            sp.wait_ge(s_gate.sem, total)
            load_static(J_PG0)
            load_static(J_PG1)
            sp.wait_ge(s_up.sem, total)
            load_static(J_PLE)
        for t in range(T):
            sp.wait_ge(s_pg.sem, 4 * L_N + (3 if t == 0 else 4))
            sp.dma_start(a["out"].rearrange("(t p) d -> p t d", p=P)[:, t, :], x[:, t, :]).then_inc(s_out.sem, 16)
        sp.wait_ge(s_out.sem, 16 * T)

    @block.gpsimd
    def _(pool):
        pool.memset(blrT[:, :], 1.0).then_inc(s_zero.sem, 1)
        pool.wait_ge(s_slot[0].sem, 16)
        pool.dma_start(tab[:, FIRST_N:], a["tables"][:, FIRST_N:]).then_inc(s_tab.sem, 16)
        pool.wait_ge(s_tab.sem, 16)
        with pool.Fori(0, L_N) as L:
            for l in range(LEVELS):
                for t in range(T):
                    if l == 0:
                        pool.wait_ge(s_A.sem, s_A.at(L, t + 1))
                    elif l == 1:
                        pool.wait_ge(s_X.sem, s_X.at(L, t + 1))
                    else:
                        pool.wait_ge(s_P_p.sem, s_P_p.at(L, 2 * (l - 1) + t + 1))
                    pool.tensor_tensor(lower[:, t], AT[:, t],
                                       table(f"level{l}").unsqueeze(1).broadcast_to([P, 4, P]),
                                       ALU.mult).then_inc(s_lv.sem, 1)
            pool.wait_ge(s_wo.sem, s_wo.at(L, 1))
            pool.dma_start(pin, a["p"][bass.ds(L, 1)].rearrange("l (t p) n -> p (l t) n", p=P)
                           ).then_inc(s_pin.sem, 16)
            pool.memset(ye, 0.0)
            pool.memset(selwT, 0.0).then_inc(s_init.sem, 1)

    @block.tensor
    def _(pe):
        mm = nc.tensor.matmul
        tr = nc.tensor.transpose
        for c in range(3):
            pe.sem_inc(s_static_used.sem, 1)
        pe.sem_inc(s_swT_p.sem, 1)
        pe.sem_inc(s_ga.sem, 1)
        pe.wait_ge(s_tab0.sem, 16)
        with pe.Fori(0, L_N) as L:
            def transpose_tile(n, src, t):
                for q in range(2):
                    for k in range(4):
                        last = tr(ps[:, 4 + 2 * t + q, k * P:(k + 1) * P], src[:, t, 4 * q + k:D:KT], ident)
                    last.then_inc(s_hTp.sem, 1)

            def token_major(j, t, bank, c0, n, at=0):
                w = slot_view(j)
                for k in range(w.shape[1]):
                    last = mm(ps[:, bank, at:at + n], hT[:, k, t * P:(t + 1) * P], w[:, k, c0:c0 + n],
                              start=(k == 0), stop=(k == w.shape[1] - 1))
                return last

            def need(j):
                pe.wait_ge(s_slot[j % 3].sem, slot_loaded(L, j))

            for t in range(T):
                pe.wait_ge(s_h.sem, L * T + t + 1)
                transpose_tile(0, h, t)
            pe.wait_ge(s_hT.sem, s_hT.at(L, 4))

            def channel_group(g):
                need(J_CQ + g)
                w = slot_view(J_CQ + g)
                if g == 2:
                    pe.wait_ge(s_conv_y.sem, s_conv_y.at(L, 1))
                for m in range(4):
                    b = (0 if g % 2 == 0 else 6) + m // 2
                    for k in range(KT):
                        last = mm(ps[:, b, (m % 2) * SEQ:(m % 2 + 1) * SEQ], w[:, k, m * P:(m + 1) * P],
                                  hT[:, k, :], start=(k == 0), stop=(k == KT - 1))
                last.then_inc(s_static_used.sem, 1)

            def conv_transposes(g):
                pe.wait_ge(s_conv_s.sem, s_conv_s.at(L, g + 1))
                if g:
                    pe.wait_ge(s_ct.sem, s_ct.at(L, g))
                for t in range(T):
                    for m in range(4):
                        last = tr(ps[:, 2 + t, m * P:(m + 1) * P], conv_y[:, m, t * P:(t + 1) * P], ident)
                last.then_inc(s_ct_p.sem, 1)

            channel_group(0)
            channel_group(1)
            conv_transposes(0)
            channel_group(2)
            conv_transposes(1)
            need(J_CG)
            pe.wait_ge(s_conv_y.sem, s_conv_y.at(L, 2))
            for t in range(T):
                token_major(J_CG, t, 6, 0, 8, at=8 * t)
            for t in range(T):
                last = token_major(J_CG, t, 4 + t, 8, 512)
            last.then_inc(s_static_used.sem, 1)
            conv_transposes(2)
            need(J_BVT)
            pe.wait_ge(s_conv_y.sem, s_conv_y.at(L, 3))
            w = slot_view(J_BVT)
            for k in range(KT):
                mm(ps[0:RANK, 7, 0:SEQ], w[:, k, 256:256 + RANK], hT[:, k, :], start=(k == 0), stop=(k == KT - 1))
            for t in range(T):
                last = token_major(J_BVT, t, t, 0, 256)
            last.then_inc(s_static_used.sem, 1)
            need(J_BR)
            pe.wait_ge(s_pj_dve.sem, s_pj_dve.at(L, 1))
            for t in range(T):
                last = token_major(J_BR, t, 4 + t, 0, 512)
            last.then_inc(s_static_used.sem, 1)
            pe.wait_ge(s_tab.sem, 16)
            pe.wait_ge(s_g.sem, s_g.at(L, 3))
            for t in range(T):
                for i, m in enumerate((causal, after, table("chunk0"), table("chunk1"))):
                    last = mm(ps[:, 6, 64 + 16 * t + 4 * i:68 + 16 * t + 4 * i], m, gdec[:, t, :], start=True, stop=True)
            last.then_inc(s_G_p.sem, 1)
            pe.wait_ge(s_g.sem, s_g.at(L, 4))
            pe.wait_ge(s_ct.sem, s_ct.at(L, 3))
            gB = tmpA.rearrange("p t (h s) -> p t h s", h=H)
            for t in range(T):
                for hh in range(H):
                    last = mm(ps[:, 2 + t, hh * P:(hh + 1) * P], gB[:, t, hh, :], causal, start=True, stop=True)
                last.then_inc(s_Gr_p.sem, 1)

            def c_transposes(i, src, b, ready):
                ready()
                for t in range(T):
                    for hh in range(H):
                        last = tr(ps[:, b + t, hh * P:(hh + 1) * P], src[:, t, hh * P:(hh + 1) * P], ident)
                last.then_inc(s_trc_p.sem, 1)

            def k_ready():
                pe.wait_ge(s_kqn.sem, L + 1)
                pe.wait_ge(s_pj_act.sem, s_pj_act.at(L, 1))
                pe.wait_ge(s_G.sem, s_G.at(L, 2))
            c_transposes(0, ct[:, :, 512:1024], 6, k_ready)

            def kb_ready():
                pe.wait_ge(s_kb.sem, L + 1)
                pe.wait_ge(s_pj_dve.sem, s_pj_dve.at(L, 2))
            c_transposes(1, tmpk, 4, kb_ready)
            need(J_AKV)
            pe.wait_ge(s_pj_act.sem, s_pj_act.at(L, 1))
            token_major(J_AKV, 0, 0, 0, 512)

            def q_ready():
                pe.wait_ge(s_trc.sem, s_trc.at(L, 1))
            c_transposes(2, ct[:, :, 0:512], 6, q_ready)
            token_major(J_AKV, 1, 1, 0, 512).then_inc(s_static_used.sem, 1)
            for t in range(T):
                pe.wait_ge(s_trc.sem, s_trc.at(L, 2))
                pe.wait_ge(s_dm.sem, s_dm.at(L, t + 1))
                for hh in range(H):
                    last = mm(ps[:, 2 + t, hh * P:(hh + 1) * P], kT_c[:, hh, t * P:(t + 1) * P],
                              kbT_c[:, hh, t * P:(t + 1) * P], start=True, stop=True)
                last.then_inc(s_A_p.sem, 1)
            for t in range(T):
                pe.wait_ge(s_trc.sem, s_trc.at(L, 3))
                for hh in range(H):
                    last = mm(ps[:, 4 + t, hh * P:(hh + 1) * P], kT_c[:, hh, t * P:(t + 1) * P],
                              qT_c[:, hh, t * P:(t + 1) * P], start=True, stop=True)
                last.then_inc(s_at_p.sem, 1)

            def qd_ready():
                pe.wait_ge(s_qd.sem, L + 1)
            c_transposes(3, ct[:, :, 0:512], 6, qd_ready)

            units = [(J_BK, 0), (J_BK, 1), (J_AQ, 0), (J_AQ, 1)]

            def unit(i):
                j, t = units[i]
                if t == 0:
                    need(j)
                    pe.wait_ge(s_pj_act.sem, s_pj_act.at(L, 2 + i // 2))
                last = token_major(j, t, t, 0, 512)
                if t == 1:
                    last.then_inc(s_static_used.sem, 1)

            def level(l):
                for t in range(T):
                    pe.wait_ge(s_lv.sem, s_lv.at(L, 2 * l + t + 1))
                    if l:
                        pe.wait_ge(s_X.sem, s_X.at(L, 2 * (l - 1) + t + 1))
                    for hh in range(H):
                        last = mm(ps[:, 2 + t, hh * P:(hh + 1) * P], lower[:, t, hh, :],
                                  X[:, t, hh, :] if l else ident, start=True, stop=True)
                    last.then_inc(s_P_p.sem, 1)
                if l == 0:
                    return
                for t in range(T):
                    pe.wait_ge(s_P.sem, s_P.at(L, 2 * (l - 1) + t + 1))
                    if l == 1:
                        pe.wait_ge(s_at.sem, s_at.at(L, t + 1))
                        pe.wait_ge(s_trc.sem, s_trc.at(L, 4))
                    for hh in range(H):
                        last = mm(ps[:, 4 + t, hh * P:(hh + 1) * P], Pm[:, t, hh, :],
                                  XT[:, t, hh, :], start=True, stop=True)
                    if l < LEVELS - 1:
                        for hh in range(H):
                            last = mm(ps[:, 6 + t, hh * P:(hh + 1) * P], XT[:, t, hh, :],
                                      Pm[:, t, hh, :], start=True, stop=True)
                    last.then_inc(s_D_p.sem, 1)

            for l in range(LEVELS):
                level(l)
                if l < 4:
                    unit(l)
                elif l == 4:
                    pe.wait_ge(s_pj_act.sem, s_pj_act.at(L, 4))
                    for t in range(T):
                        last = mm(ps[:, 0, t * 256:(t + 1) * 256], blrT[:, t * P:(t + 1) * P], wa2[:, :],
                                  start=True, stop=True)
                    last.then_inc(s_z.sem, 1)
            for t in range(T):
                pe.wait_ge(s_X.sem, s_X.at(L, 2 * (LEVELS - 1) + t + 1))
                for hh in range(H):
                    mm(ps[:, 2 + t, hh * P:(hh + 1) * P], kg[:, t, hh * P:(hh + 1) * P], XT[:, t, hh, :],
                       start=True, stop=True)
                for hh in range(H):
                    last = mm(ps[:, 4 + t, hh * P:(hh + 1) * P], XT[:, t, hh, :],
                              ct[:, t, 1024 + hh * P:1024 + (hh + 1) * P], start=True, stop=True)
                last.then_inc(s_wu_p.sem, 1)
            def scan(n, meanwhile=lambda: None):
                t, r = n // 2, CHUNK * (n % 2)
                if n:
                    pe.wait_ge(s_S.sem, s_S.at(L, n))
                    m = CHUNK if r == 0 else P
                    for hh in range(H):
                        last = mm(ps[0:m, 6, hh * P:(hh + 1) * P], wT[:, hh, t * P:t * P + m], Sc[:, hh, :],
                                  start=True, stop=True)
                    last.then_inc(s_ws.sem, 1)
                if n:
                    for hh in range(H):
                        mm(ps[r:r + CHUNK, 2 + t, hh * P:(hh + 1) * P], qdT_c[:, hh, t * P + r:t * P + r + CHUNK],
                           Sc[:, hh, :], start=(hh == 0), stop=(hh == H - 1), skip_group_check=True)
                meanwhile()
                pe.wait_ge(s_vn.sem, s_vn.at(L, n + 1))
                if n < 3:
                    for hh in range(H):
                        last = mm(ps[:, 7, hh * P:(hh + 1) * P], kd[r:r + CHUNK, t, hh * P:(hh + 1) * P],
                                  vnew[r:r + CHUNK, t, hh * P:(hh + 1) * P], start=True, stop=True)
                    last.then_inc(s_ds.sem, 1)
                if r:
                    for half in range(2):
                        o = CHUNK * half
                        for hh in range(H):
                            last = mm(ps[o:o + CHUNK, 2 + t, hh * P:(hh + 1) * P], attG[:, t, hh, o:o + CHUNK],
                                      vnew[:, t, hh * P:(hh + 1) * P],
                                      start=(t == 0 and half == 0 and hh == 0), stop=(hh == H - 1), skip_group_check=True)
                    last.then_inc(s_oc.sem, 1)

            def gla_state_product(n):
                t, r = n // 2, CHUNK * (n % 2)
                b = 1 - n % 2
                if n == 2:
                    pe.wait_ge(s_Sb.sem, s_Sb.at(L, 1))
                for g in range(2):
                    last = mm(ps[:, b, g * 256:(g + 1) * 256], kdb[r:r + CHUNK, t, g * P:(g + 1) * P],
                              bt[r:r + CHUNK, t, 512 + g * 256:512 + (g + 1) * 256], start=True, stop=True)
                last.then_inc(s_du_p.sem, 1)

            scan(0)
            pe.wait_ge(s_wu.sem, s_wu.at(L, 2))
            pe.wait_ge(s_lar.sem, L + 1)
            for t in range(T):
                mm(ps[:, 0, t * 256:(t + 1) * 256], causal, la[:, t, :], start=True, stop=True)
            for t in range(T):
                mm(ps[:, 1, t * 256:(t + 1) * 256], after, la[:, t, :], start=True, stop=True)
            for t in range(T):
                for g in range(2):
                    for n in range(2):
                        o = 4 * g + 2 * t + n
                        last = mm(ps[:, 4, o:o + 1], la[:, t, g * P:(g + 1) * P],
                                  table("chunk0" if n == 0 else "chunk1")[:, 0:1], start=True, stop=True)
            last.then_inc(s_b_p.sem, 1)
            scan(1)
            pe.wait_ge(s_qke.sem, L + 1)
            for i, src in enumerate((qe, ke)):
                for g in range(2):
                    for t in range(T):
                        last = tr(ps[:, 4 + i, (2 * g + t) * P:(2 * g + t + 1) * P], src[:, t, g * P:(g + 1) * P], ident)
            last.then_inc(s_trb_p.sem, 1)
            gla_state_product(0)
            scan(2)
            gla_state_product(1)

            def gla_products():
                pe.wait_ge(s_trb.sem, L + 1)
                for odd in range(2):
                    for t in range(T):
                        for g in range(2):
                            r = DK_B * odd
                            last = mm(ps[:, 4 + odd, (2 * t + g) * P:(2 * t + g + 1) * P],
                                      keT[r:r + DK_B, g, t * P:(t + 1) * P], qeT[r:r + DK_B, g, t * P:(t + 1) * P],
                                      start=True, stop=True)
                    last.then_inc(s_ab_p.sem, 1)
                gla_state_product(2)
            scan(3, gla_products)
            for t in range(T):
                pe.wait_ge(s_ab.sem, s_ab.at(L, 2))
                for half in range(2):
                    r, n = CHUNK * half, 2 * t + half
                    if n:
                        pe.wait_ge(s_Sb.sem, s_Sb.at(L, n))
                    out = ps[r:r + CHUNK, 4 + t, :]
                    for hh in range(H):
                        last = mm(out[:, hh * P:(hh + 1) * P], attB[:, t, hh, r:r + CHUNK],
                                  bt[:, t, 512 + hh * P:512 + (hh + 1) * P], start=(hh == 0), stop=(n == 0),
                                  skip_group_check=True)
                    if n:
                        for g in range(2):
                            last = mm(out[:, g * 256:(g + 1) * 256], qeT[:, g, t * P + r:t * P + r + CHUNK],
                                      Sb[:, n - 1, g, :], start=False, stop=(g == 1), skip_group_check=True)
                last.then_inc(s_oc.sem, 1)

            def y_transposes(n):
                pe.wait_ge(s_y.sem, s_y.at(L, n + 1))
                for t in range(T):
                    for k in range(4):
                        last = tr(ps[:, 6 + t, k * P:(k + 1) * P], y_of[n][:, t, k:512:4], ident)
                last.then_inc(s_yT_p.sem, 1)

            def merge_gate(n, jg, t):
                if t == 0:
                    need(jg)
                if n:
                    pe.wait_ge(s_mg.sem, s_mg.at(L, 4 * n + t - 1))
                last = token_major(jg, t, t, 0, 512)
                if t == T - 1:
                    last.then_inc(s_static_used.sem, 1)

            def branch_product(t, f, jg):
                w = slot_view(jg + 1)
                for k in range(4):
                    last = mm(ps[:, 2 + t, :], yT[:, k, t * P:(t + 1) * P], w[:, k, f * 512:(f + 1) * 512],
                              start=(k == 0), stop=(k == 3))
                return last

            def merge_first(n, jg):
                need(jg + 1)
                pe.wait_ge(s_yT.sem, s_yT.at(L, n + 1))
                for t in range(T):
                    branch_product(t, 0, jg).then_inc(s_gt_p.sem, 1)

            def merge_second(n, jg):
                need(jg + 2)
                pe.wait_ge(s_mg.sem, s_mg.at(L, 4 * n + 1))
                token_major(jg + 2, 0, 0, 0, 512)
                branch_product(0, 1, jg).then_inc(s_gt_p.sem, 1)
                pe.wait_ge(s_mg.sem, s_mg.at(L, 4 * n + 2))
                branch_product(1, 1, jg).then_inc(s_static_used.sem, 1)
                token_major(jg + 2, 1, 1, 0, 512).then_inc(s_static_used.sem, 1)

            merge_gate(0, J_GC0, 0)
            merge_gate(0, J_GC0, 1)
            y_transposes(0)
            merge_first(0, J_GC0)
            merge_second(0, J_GC0)
            pe.wait_ge(s_ak.sem, L + 1)
            for t in range(T):
                for g in range(4):
                    tr(ps[:, 4 + t, g * P:(g + 1) * P], aq[:, t, g * P:(g + 1) * P], ident)
                tr(ps[:, 6, t * P:(t + 1) * P], aq[:, t, 512:640], ident)
                last = tr(ps[:, 6, 256 + t * P:256 + (t + 1) * P], kswap[:, t, :], ident)
            last.then_inc(s_tra_p.sem, 1)
            merge_gate(1, J_GB0, 0)
            merge_gate(1, J_GB0, 1)

            def score(hh, t, out):
                r = HD_A * (hh % 2)
                kv = hh // (HEADS_A // KV_A)
                keys = (kTa if kv == hh % 2 else kTb)[r:r + HD_A, 0:P * (t + 1)]
                return mm(out, qT_a[r:r + HD_A, hh // 2, t * P:(t + 1) * P], keys, start=True, stop=True)
            pe.wait_ge(s_tra.sem, L + 1)
            y_transposes(1)
            for hh in range(HEADS_A):
                last = score(hh, 0, ps[:, 4 + hh % 2, (hh // 2) * P:(hh // 2 + 1) * P])
            last.then_inc(s_sc_p.sem, 1)
            merge_first(1, J_GB0)
            pe.wait_ge(s_sc.sem, s_sc.at(L, 1))
            for hh in range(HEADS_A):
                b = (6, 4)[hh % 2] + hh // 4
                last = score(hh, 1, ps[:, b, (hh // 2 % 2) * SEQ:(hh // 2 % 2 + 1) * SEQ])
            last.then_inc(s_sc_p.sem, 1)
            merge_second(1, J_GB0)
            merge_gate(2, J_GA0, 0)
            pe.wait_ge(s_pe.sem, L + 1)
            for i in range(6):
                if i >= 4:
                    pe.wait_ge(s_pt.sem, s_pt.at(L, i - 3))
                for k in range(4):
                    hh, b = divmod(4 * i + k, 3)
                    last = tr(ps[:, 4 + i % 4, k * P:(k + 1) * P], scores[:, hh, b * P:(b + 1) * P], ident)
                last.then_inc(s_pt_p.sem, 1)
            pe.wait_ge(s_pt.sem, s_pt.at(L, 6))
            for t in range(T):
                for hh in range(HEADS_A):
                    out = ps[:, 4 + 2 * t + hh // 4, (hh % 4) * P:(hh % 4 + 1) * P]
                    for kb in range(t + 1):
                        last = mm(out, pT[:, 3 * hh + (kb + 1 if t else 0), :], aq[:, kb, 640:768],
                                  start=(kb == 0), stop=(kb == t))
                last.then_inc(s_pv.sem, 1)
            y_transposes(2)
            merge_gate(2, J_GA0, 1)
            merge_first(2, J_GA0)
            merge_second(2, J_GA0)
            for t in range(T):
                pe.wait_ge(s_mg.sem, s_mg.at(L, 11 + t))
                for q in range(2):
                    for k in range(4):
                        last = tr(ps[:, 4 + 2 * t + q, k * P:(k + 1) * P], merged[:, t, 4 * q + k:D:KT], ident)
                    last.then_inc(s_mT_p.sem, 1)
            for f in range(2):
                need(J_WO0 + f)
                for t in range(T):
                    if f == 0:
                        pe.wait_ge(s_mT.sem, s_mT.at(L, 2 * t + 2))
                    token_major(J_WO0 + f, t, 2 * f + t, 0, 512).then_inc((s_wo, s_static_used)[t].sem, 1)
            for t in range(T):
                pe.wait_ge(s_x.sem, s_x.at(L, t + 1))
                transpose_tile(1, x, t)
            pe.wait_ge(s_hT.sem, s_hT.at(L, 8))
            need(J_ROUTER)
            for t in range(T):
                last = token_major(J_ROUTER, t, 6, 0, 36, at=64 * t)
            last.then_inc(s_static_used.sem, 1)
            pe.wait_ge(s_init.sem, L + 1)
            for t in range(T):
                for f in range(2):
                    mm(ps[:, 2 * t + f, :], selwT[:, t * P:(t + 1) * P], ye[:, f * 512:(f + 1) * 512],
                       start=True, stop=True)
            pe.wait_ge(s_ch.sem, L + 1)
            mm(ps[:, 7, 0:E], table("before"), chosen[:, 0, :], start=True, stop=True)
            mm(ps[:, 7, E:2 * E], table("before"), chosen[:, 1, :], start=True, stop=False)
            mm(ps[:, 7, E:2 * E], table("ones"), chosen[:, 0, :], start=False, stop=True)
            mm(ps[:, 7, 2 * E:3 * E], table("ones"), chosen[:, 0, :], start=True, stop=False)
            mm(ps[:, 7, 2 * E:3 * E], table("ones"), chosen[:, 1, :], start=False, stop=True).then_inc(s_pos_p.sem, 1)

            def gather():
                for k in range(KT):
                    for t in range(T):
                        last = mm(ps[:, 4 + k // 4, (k % 4) * P:(k % 4 + 1) * P], h[:, t, k:D:KT],
                                  sel[:, t].rearrange("p j s -> p (j s)"), start=(t == 0), stop=(t == T - 1))
                return last

            def scatter():
                for t in range(T):
                    for f in range(2):
                        last = mm(ps[:, 2 * t + f, :], selwT[:, t * P:(t + 1) * P], ye[:, f * 512:(f + 1) * 512],
                                  start=False, stop=False, skip_group_check=True)
                return last

            def ring_matrix(c):
                return lambda k: ring[:, c, k * 512:(k + 1) * 512]

            def even_gate(j):
                return lambda k: even_gates[:, j, k * 512:(k + 1) * 512]

            def even_up_matrix(k):
                return even_up[k // 4][:, (k % 4) * 512:(k % 4 + 1) * 512]

            def expert_in(bank, first, second, out):
                for k in range(KT):
                    for j, matrix in enumerate((first, second)):
                        last = mm(ps[CAP * j:CAP * (j + 1), bank, :], xgT[:, k, CAP * j:CAP * (j + 1)],
                                  matrix(k), start=(k == 0), stop=(k == KT - 1))
                last.then_inc(out.sem, 1)

            def moe_round(gg, pair, gates, up_loaded, up):
                pe.wait_ge(s_xg.sem, gg + L + 1)
                pe.wait_ge(s_swT.sem, gg + 1)
                expert_in(6, *gates, s_gate)
                up_loaded()
                pe.wait_ge(s_slot[3].sem, pair_loaded(L, 3, pair))
                pe.wait_ge(s_hg.sem, gg + 1)
                expert_in(7, up, ring_matrix(3), s_up)
                pe.wait_ge(s_ye.sem, gg + 1)
                scatter().then_inc(s_scat.sem, 1)
                pe.wait_ge(s_sel.sem, gg + 1)
                gather().then_inc(s_ga.sem, 1)
                pe.wait_ge(s_selw.sem, gg + 1)
                pe.wait_ge(s_act.sem, gg + 1)
                for t in range(T):
                    last = tr(ps[:, 6, t * P:(t + 1) * P], selw[:, t].rearrange("p j s -> p (j s)"), ident)
                last.then_inc(s_swT_p.sem, 1)
                for k in range(FT):
                    last = tr(ps[:, 7, k * P:(k + 1) * P], act_h[:, k:FF:FT], ident)
                last.then_inc(s_hg_p.sem, 1)
                pe.wait_ge(s_slot[4].sem, pair_loaded(L, 4, pair))
                pe.wait_ge(s_slot[5].sem, pair_loaded(L, 5, pair))
                pe.wait_ge(s_hg.sem, gg + 2)
                pe.wait_ge(s_xg.sem, gg + L + 2)
                for f in range(2):
                    for k in range(FT):
                        for j in range(2):
                            last = mm(ps[CAP * j:CAP * (j + 1), 4 + f, :], hgT[:, k, CAP * j:CAP * (j + 1)],
                                      ring[:, 4 + j, k * D + f * 512:k * D + (f + 1) * 512],
                                      start=(k == 0), stop=(k == FT - 1))
                last.then_inc(s_down.sem, 1)

            pe.wait_ge(s_sel0.sem, L + 1)
            gather().then_inc(s_ga0.sem, 1)
            pe.wait_ge(s_tbl.sem, L + 1)
            total = plan(pe, L, BEFORE + PAIRS, 0, 4096)
            with pe.Fori(0, PAIRS // 2) as ii:
                first = plan(pe, L, BEFORE + 2 * ii, 0, 4096)
                middle = plan(pe, L, BEFORE + 2 * ii + 1, 1, 4096)
                end = plan(pe, L, BEFORE + 2 * ii + 2, 1, 4096)
                with pe.Fori(first, middle) as gg:
                    for j in range(2):
                        pe.wait_ge(s_even[j].sem, 16 * (L * (PAIRS // 2) + ii + 1))

                    def even_up_loaded():
                        pe.wait_ge(s_even_up.sem, 32 * (L * (PAIRS // 2) + ii + 1))
                    moe_round(gg, 2 * ii, (even_gate(0), even_gate(1)), even_up_loaded, even_up_matrix)
                with pe.Fori(middle, end) as gg:
                    for j in range(2):
                        pe.wait_ge(s_slot[j].sem, pair_loaded(L, j, ii))

                    def odd_up_loaded():
                        pe.wait_ge(s_slot[2].sem, pair_loaded(L, 2, ii))
                    moe_round(gg, 2 * ii + 1, (ring_matrix(0), ring_matrix(1)), odd_up_loaded, ring_matrix(2))
            pe.wait_ge(s_pin.sem, 16 * (L + 1))
            for k in range(2):
                for t in range(T):
                    last = tr(ps[:, 6, (2 * k + t) * P:(2 * k + t + 1) * P], pin[:, t, k:PLE:2], ident)
            last.then_inc(s_pl_p.sem, 1)
            pe.wait_ge(s_ye.sem, total + 1)
            scatter().then_inc(s_acc.sem, 1)

            for t in range(T):
                pe.wait_ge(s_x.sem, s_x.at(L, T + t + 1))
                if t == 1:
                    pe.wait_ge(s_pl.sem, L + 1)
                transpose_tile(2, x, t)
            pe.wait_ge(s_hT.sem, s_hT.at(L, 12))
            need(J_PLE)
            w = slot_view(J_PLE)
            for f in range(2):
                need(J_PG0 + f)
                for t in range(T):
                    i = 2 * f + t
                    b = 2 * (i % 2)
                    if i >= 2:
                        pe.wait_ge(s_pg.sem, s_pg.at(L, i + 3))
                    last = token_major(J_PG0 + f, t, b, 0, 512)
                    if t == 1:
                        last.then_inc(s_static_used.sem, 1)
                    for k in range(2):
                        last = mm(ps[:, b + 1, :], pinT[:, k, t * P:(t + 1) * P], w[:, k, f * 512:(f + 1) * 512],
                                  start=(k == 0), stop=(k == 1))
                    last.then_inc((s_pg_p if i < 3 else s_static_used).sem, 1)

    @block.scalar
    def _(act):
        def fn(*args, **kw):
            return nc.scalar.activation(*args, **kw)

        eps, one = table("eps"), table("one")

        def table_of(function):
            fn(warm[:, 0:1], one, function)

        act.wait_ge(s_trig.sem, 1)
        fn(cossin[:, :, :, :], cossin[:, :, :, :], ACT.Sin).then_inc(s_trigd.sem, 1)
        act.sem_inc(s_swT.sem, 1)
        act.sem_inc(s_hg.sem, 1)
        act.sem_inc(s_ye.sem, 1)
        act.wait_ge(s_tab0.sem, 16)
        act.wait_ge(s_x0.sem, 16)
        with act.Fori(0, L_N) as L:
            def rms_of_x(n):
                for t in range(T):
                    if n == 0:
                        act.wait_ge(s_pg.sem, 4 * L + 3 + t)
                    else:
                        act.wait_ge(s_x.sem, s_x.at(L, (n - 1) * T + t + 1))
                    fn(h[:, t, :], x[:, t, :], ACT.Square, accum_out=ss[:, t:t + 1])
                    act.drain()
                    if n < 2:
                        fn(rms[:, t:t + 1], ss[:, t:t + 1], ACT.Sqrt, scale=1.0 / D, bias=eps).then_inc(s_ss.sem, 1)
                    else:
                        fn(rms[:, t:t + 1], ss[:, t:t + 1], ACT.Sqrt, scale=4.0 / D, bias=table("eps4")
                           ).then_inc(s_ss.sem, 1)

            table_of(ACT.Sqrt)
            rms_of_x(0)
            table_of(ACT.Tanh)
            act.wait_ge(s_par.sem, 48 * (L + 1))
            fn(nea, row("a_log"), ACT.Exp)
            for g in range(3):
                act.wait_ge(s_conv_y.sem, s_conv_y.at(L, g + 1))
                fn(conv_e, conv_y, ACT.Tanh, scale=0.5).then_inc(s_conv_e.sem, 1)
                if g == 2:
                    act.wait_ge(s_static_used.sem, chunk_used(L, J_CG))
                    fn(ba.rearrange("p t n -> p (t n)"), ps[:, 6, 0:16], ACT.Copy).then_inc(s_beta_e.sem, 1)
                    fn(cg, ps[:, 4:6, :], ACT.Tanh, scale=0.5).then_inc(s_gexp.sem, 1)
                    act.drain()
                    fn(beta, ba[:, :, 0:4], ACT.Tanh, scale=0.5).then_inc(s_beta_e.sem, 1)
                act.wait_ge(s_ct_p.sem, s_ct_p.at(L, g + 1))
                fn(ct[:, :, g * 512:(g + 1) * 512], ps[:, 2:4, :], ACT.Copy, scale=0.5
                   ).then_inc(s_ct.sem, 1)
            act.wait_ge(s_static_used.sem, chunk_used(L, J_BVT))
            act.wait_ge(s_zero.sem, 1)
            fn(blrT[0:RANK, :], ps[0:RANK, 7, 0:SEQ], ACT.Copy)
            fn(bt[:, :, 768:1024], ps[:, 0:2, 0:256], ACT.Copy).then_inc(s_pj_act.sem, 1)
            act.wait_ge(s_g.sem, s_g.at(L, 1))
            fn(gabs, gabs, ACT.Exp, scale=-1.0)
            act.drain()
            fn(gabs, gabs, ACT.Ln, bias=one).then_inc(s_beta_e.sem, 1)
            act.wait_ge(s_nsq.sem, L + 1)
            fn(ssq, ssq, ACT.Sqrt, bias=eps).then_inc(s_nr.sem, 1)
            act.wait_ge(s_G_p.sem, L + 1)
            fn(expG.rearrange("p t a h -> p (t a h)"), ps[:, 6, 64:96], ACT.Exp).then_inc(s_G.sem, 1)
            fn(negG, ps[:, 6, 64:96].rearrange("p (t a) -> p t a", t=T)[:, :, 0:4], ACT.Copy, scale=-1.0
               ).then_inc(s_G.sem, 1)
            act.wait_ge(s_static_used.sem, chunk_used(L, J_BR))
            fn(br, ps[:, 4:6, :], ACT.Tanh, scale=0.5).then_inc(s_gexp.sem, 1)
            def take_c(i, dst, b):
                act.wait_ge(s_trc_p.sem, s_trc_p.at(L, i + 1))
                for t in range(T):
                    last = fn(dst[:, :, t * P:(t + 1) * P], ps[:, b + t, :].rearrange("p (h n) -> p h n", h=H),
                              ACT.Copy)
                last.then_inc(s_trc.sem, 1)
            take_c(0, kT_c, 6)
            take_c(1, kbT_c, 4)
            act.drain()
            for t in range(T):
                act.wait_ge(s_dm.sem, s_dm.at(L, t + 1))
                for hh in range(H):
                    last = fn(decT[:, t, hh, :], decT[:, t, hh, :], ACT.Exp, bias=negG[:, t, hh:hh + 1])
                last.then_inc(s_dec.sem, 1)
            take_c(2, qT_c, 6)
            act.wait_ge(s_static_used.sem, chunk_used(L, J_AKV))
            fn(aq[:, :, 512:768], ps[:, 0:2, 0:256], ACT.Copy)
            fn(bt[:, :, 0:256], ps[:, 0:2, 256:512], ACT.Copy).then_inc(s_pj_act.sem, 1)
            take_c(3, qdT_c, 6)

            for l in range(1, LEVELS):
                for t in range(T):
                    act.wait_ge(s_P_p.sem, s_P_p.at(L, 2 * l + t + 1))
                    if l > 1:
                        act.wait_ge(s_D_p.sem, s_D_p.at(L, 2 * (l - 2) + t + 1))
                    fn(Pm[:, t], ps[:, 2 + t, :].rearrange("p (h n) -> p h n", h=H), ACT.Copy).then_inc(s_P.sem, 1)
                if l in (1, 3):
                    act.wait_ge(s_static_used.sem, chunk_used(L, J_BK + l // 2))
                    if l == 1:
                        last = fn(bt[:, :, 256:768], ps[:, 0:2, :], ACT.Copy)
                    else:
                        last = fn(aq[:, :, 0:512], ps[:, 0:2, :], ACT.Copy)
                    last.then_inc(s_pj_act.sem, 1)
            act.wait_ge(s_z.sem, s_z.at(L, 2))
            fn(zab, zab, ACT.Exp, scale=-1.0)
            act.drain()
            fn(zab, zab, ACT.Ln, bias=one).then_inc(s_la.sem, 1)
            for t in range(T):
                act.wait_ge(s_wu_p.sem, s_wu_p.at(L, t + 1))
                act.wait_ge(s_trc.sem, s_trc.at(L, 4))
                fn(wT[:, :, t * P:(t + 1) * P], ps[:, 2 + t, :].rearrange("p (h n) -> p h n", h=H), ACT.Copy)
                if t == 0:
                    act.wait_ge(s_vn.sem, s_vn.at(L, 1))
                fn(u[:, t, :], ps[:, 4 + t, :], ACT.Copy).then_inc(s_wu.sem, 1)

            act.wait_ge(s_b_p.sem, L + 1)
            fn(eb.rearrange("p t n -> p (t n)"), ps[:, 0, :], ACT.Exp)
            fn(enb.rearrange("p t n -> p (t n)"), ps[:, 0, :], ACT.Exp, scale=-1.0)
            fn(ea.rearrange("p t n -> p (t n)"), ps[:, 1, :], ACT.Exp)
            fn(decB.rearrange("p g t n -> p (g t n)"), ps[:, 4, 0:8], ACT.Exp).then_inc(s_b.sem, 1)
            act.wait_ge(s_trb_p.sem, L + 1)
            fn(qeT.rearrange("p g n -> p (g n)"), ps[:, 4, :], ACT.Copy)
            fn(keT.rearrange("p g n -> p (g n)"), ps[:, 5, :], ACT.Copy).then_inc(s_trb.sem, 1)

            def take_yT(n):
                act.wait_ge(s_yT_p.sem, s_yT_p.at(L, n + 1))
                for t in range(T):
                    last = fn(yT[:, :, t * P:(t + 1) * P], ps[:, 6 + t, :].rearrange("p (k n) -> p k n", k=4), ACT.Copy)
                last.then_inc(s_yT.sem, 1)

            def o_norm(n):
                for t in range(T):
                    act.wait_ge(s_oc.sem, s_oc.at(L, 2 * n + t + 1))
                    for hh in range(H):
                        fn(sq_of[n][:, t, hh * P:(hh + 1) * P], ps[:, 2 + 2 * n + t, hh * P:(hh + 1) * P], ACT.Square,
                           accum_out=sso[:, n, t, hh:hh + 1])
                act.drain()
                fn(rmso[:, n], sso[:, n], ACT.Sqrt, scale=4.0 / P, bias=table("eps4")).then_inc(s_onr.sem, 1)

            table_of(ACT.Sqrt)
            o_norm(0)
            o_norm(1)
            take_yT(0)
            act.wait_ge(s_asq.sem, L + 1)
            fn(ssa, ssa, ACT.Sqrt, scale=1.0 / HD_A, bias=eps).then_inc(s_ar.sem, 1)
            def gate(i):
                if i % 4 < 3:
                    act.wait_ge(s_gt_p.sem, s_gt_p.at(L, 3 * (i // 4) + i % 4 + 1))
                else:
                    act.wait_ge(s_static_used.sem, chunk_used(L, J_GC1 + 3 * (i // 4)))
                if i >= 2:
                    act.wait_ge(s_mg.sem, s_mg.at(L, i - 1))
                fn(tmpA[:, i % 2, :], ps[:, i % 2, :], ACT.Tanh, scale=0.5).then_inc(s_gt_e.sem, 1)

            table_of(ACT.Tanh)
            for i in range(4):
                gate(i)
            act.wait_ge(s_tra_p.sem, L + 1)
            for t in range(T):
                fn(qT_a[:, :, t * P:(t + 1) * P], ps[:, 4 + t, :].rearrange("p (g n) -> p g n", g=4), ACT.Copy)
            fn(kTa, ps[:, 6, 0:256], ACT.Copy)
            fn(kTb, ps[:, 6, 256:512], ACT.Copy).then_inc(s_tra.sem, 1)
            take_yT(1)
            gate(4)
            gate(5)
            act.wait_ge(s_sx.sem, L + 1)
            fn(esink, esink, ACT.Exp)
            fn(scores, scores, ACT.Exp).then_inc(s_pe.sem, 1)
            gate(6)
            gate(7)
            for i in range(6):
                act.wait_ge(s_pt_p.sem, s_pt_p.at(L, i + 1))
                fn(pT[:, 4 * i:4 * i + 4, :], ps[:, 4 + i % 4, :].rearrange("p (k n) -> p k n", k=4), ACT.Copy
                   ).then_inc(s_pt.sem, 1)
            take_yT(2)
            for i in range(8, 12):
                gate(i)
            table_of(ACT.Sqrt)
            for q in range(4):
                act.wait_ge(s_mT_p.sem, s_mT_p.at(L, q + 1))
                t, half = divmod(q, 2)
                fn(hT[:, 4 * half:4 * half + 4, t * P:(t + 1) * P],
                   ps[:, 4 + q, :].rearrange("p (k n) -> p k n", k=4), ACT.Copy, scale=0.5).then_inc(s_mT.sem, 1)
            rms_of_x(1)
            for i in range(2):
                act.wait_ge(s_rt.sem, s_rt.at(L, i + 1))
                if i == 0:
                    last = fn(lg[:, :, 0:GROUPS], lg[:, :, 0:GROUPS], ACT.Exp)
                else:
                    last = fn(e2, e2, ACT.Exp)
                last.then_inc(s_rte.sem, 1)
            act.wait_ge(s_tbl.sem, L + 1)
            base = plan(act, L, BEFORE, 0, 4096)
            n_rounds = plan(act, L, ROUNDS_AT, PAIRS, ROUNDS_LIMIT)
            table_of(ACT.Tanh)
            act.wait_ge(s_init.sem, L + 1)
            with act.Fori(0, n_rounds) as g:
                gg = base + g
                act.wait_ge(s_gate.sem, gg + 1)
                fn(sig, ps[:, 6, :], ACT.Tanh, scale=0.5).then_inc(s_sig.sem, 1)
                act.wait_ge(s_scat.sem, gg + 1)
                act.wait_ge(s_swT_p.sem, gg + 2)
                fn(selwT, ps[:, 6, 0:256], ACT.Copy).then_inc(s_swT.sem, 1)
                act.wait_ge(s_hg_p.sem, gg + 1)
                fn(hgT.rearrange("p k n -> p (k n)"), ps[:, 7, :], ACT.Copy).then_inc(s_hg.sem, 1)
                act.wait_ge(s_down.sem, gg + 1)
                fn(ye.rearrange("p (f n) -> p f n", f=2), ps[:, 4:6, :], ACT.Copy).then_inc(s_ye.sem, 1)
            table_of(ACT.Sqrt)
            act.wait_ge(s_pl_p.sem, L + 1)
            fn(pinT.rearrange("p k n -> p (k n)"), ps[:, 6, :], ACT.Copy).then_inc(s_pl.sem, 1)
            rms_of_x(2)
            table_of(ACT.Tanh)
            act.wait_ge(s_rs.sem, L + 1)
            for i in range(4):
                if i < 3:
                    act.wait_ge(s_pg_p.sem, s_pg_p.at(L, i + 1))
                else:
                    act.wait_ge(s_static_used.sem, chunk_used(L, J_PLE))
                fn(gtmp[:, i % 2, :], ps[:, 2 * (i % 2), :], ACT.Tanh, scale=rstd[:, i % 2:i % 2 + 1]
                   ).then_inc(s_pg_e.sem, 1)

    @block.vector
    def _(dve):
        v = nc.vector
        tt, ts, stt = v.tensor_tensor, v.tensor_scalar, v.scalar_tensor_tensor

        def over(ap, shape):
            return ap.broadcast_to(shape)

        dve.sem_inc(s_par_used.sem, 1)
        for _i in range(4):
            dve.sem_inc(s_pg.sem, 1)
        for n in range(HALF):
            v.memset(inv_freq[:, n:n + 1], float(INV_FREQ[n]))
        dve.wait_ge(s_posi.sem, 16)
        trig = so2[:, :, :, :, :].rearrange("p a t h n -> p (a t h n)")
        n_trig = 2 * T * HALF
        posf, kf2, ang2 = trig[:, 0:T], trig[:, 16:16 + n_trig], trig[:, 64:64 + n_trig]
        kf = kf2.rearrange("p (w t n) -> p w t n", w=2, t=T)
        ang = ang2.rearrange("p (w t n) -> p w t n", w=2, t=T)
        v.tensor_copy(posf, posi[:, :])
        dve.drain()
        for w in range(2):
            tt(ang[:, w], over(posf.unsqueeze(2), [P, T, HALF]), over(inv_freq[:, :].unsqueeze(1), [P, T, HALF]),
               ALU.mult)
        dve.drain()
        for w in range(2):
            ts(kf[:, w], ang[:, w], float(1 / (2 * np.pi)), 0.25 if w == 0 else 0.0, ALU.mult, ALU.add)
        dve.drain()
        magic = float(1.5 * 2 ** 23)
        ts(kf, kf, magic, None, ALU.add)
        dve.drain()
        ts(kf, kf, magic, None, ALU.subtract)
        dve.drain()
        c1 = 6.28125
        c2 = float(np.float32(np.round((2 * np.pi - c1) * 2 ** 20) / 2 ** 20))
        c3 = float(2 * np.pi - c1 - c2)
        for c in (c1, c2, c3):
            stt(out=ang2, in0=kf2, scalar=-c, in1=ang2, op0=ALU.mult, op1=ALU.add)
            dve.drain()
        ts(ang[:, 0], ang[:, 0], float(np.pi / 2), None, ALU.add)
        dve.drain()
        ts(cossin[:, :, :, :], ang, 3.1415925, -3.1415925, ALU.min, ALU.max).then_inc(s_trig.sem, 1)
        v.memset(base_f[:, :], 0.0)
        dve.wait_ge(s_x0.sem, 16)
        dve.wait_ge(s_trigd.sem, 1)
        dve.wait_ge(s_tab0.sem, 16)
        with dve.Fori(0, L_N) as L:
            def reciprocal_rms(n):
                dve.wait_ge(s_ss.sem, s_ss.at(L, n * T + T))
                return v.reciprocal(rstd, rms)

            def normed(n, t):
                dve.wait_ge(s_ss.sem, s_ss.at(L, n * T + t + 1))
                v.reciprocal(rstd[:, t:t + 1], rms[:, t:t + 1])
                dve.drain()
                return ts(h[:, t, :], x[:, t, :], rstd[:, t:t + 1], None, ALU.mult)

            def take_hT(n, gain):
                if n == 0:
                    dve.wait_ge(s_par.sem, 48 * (L + 1))
                for q in range(4):
                    t, half = divmod(q, 2)
                    dve.wait_ge(s_hTp.sem, s_hTp.at(L, 4 * n + q + 1))
                    tt(hT[:, 4 * half:4 * half + 4, t * P:(t + 1) * P],
                       ps[:, 4 + q, :].rearrange("p (k n) -> p k n", k=4),
                       over(col(gain)[:, 4 * half:4 * half + 4].unsqueeze(2), [P, 4, P]), ALU.mult
                       ).then_inc(s_hT.sem, 1)

            def twice_gated(out, half_tanh, gated):
                return stt(out=out, in0=half_tanh, scalar=1.0, in1=gated, op0=ALU.add, op1=ALU.mult)

            for t in range(T):
                normed(0, t).then_inc(s_h.sem, 1)
            take_hT(0, "attn_norm")
            taps = col("conv").rearrange("p (m j) -> p m j", j=4)

            def conv(g):
                b = 0 if g % 2 == 0 else 6
                dve.wait_ge(s_static_used.sem, chunk_used(L, J_CQ + g))
                if g:
                    dve.wait_ge(s_ct_p.sem, s_ct_p.at(L, g))
                src = ps[:, b:b + 2, :].rearrange("p a (m n) -> p (a m) n", m=2)
                for d in range(4):
                    for m in range(4):
                        w = taps[:, 4 * g + m, 3 - d:4 - d]
                        if d == 0:
                            last = ts(conv_y[:, m, :], src[:, m, :], w, None, ALU.mult)
                        else:
                            last = stt(out=conv_y[:, m, d:], in0=src[:, m, 0:SEQ - d], scalar=w,
                                       in1=conv_y[:, m, d:], op0=ALU.mult, op1=ALU.add)
                    if d < 3:
                        dve.drain()
                last.then_inc(s_conv_y.sem, 1)
                dve.wait_ge(s_conv_e.sem, s_conv_e.at(L, g + 1))
                twice_gated(conv_y, conv_e, conv_y).then_inc(s_conv_s.sem, 1)

            conv(0)
            conv(1)
            conv(2)
            dve.wait_ge(s_gexp.sem, s_gexp.at(L, 1))
            twice_gated(cg, cg, ps[:, 4:6, :]).then_inc(s_pj_dve.sem, 1)
            dve.wait_ge(s_beta_e.sem, s_beta_e.at(L, 2))
            tt(gdec, ba[:, :, 4:8], over(row("dt_bias").unsqueeze(1), [P, T, H]), ALU.add)
            ts(beta, beta, 1.0, 0.5, ALU.add, ALU.mult)
            dve.drain()
            stt(out=gabs, in0=gdec, scalar=-1.0, in1=gdec, op0=ALU.mult, op1=ALU.max).then_inc(s_g.sem, 1)
            dve.wait_ge(s_beta_e.sem, s_beta_e.at(L, 3))
            stt(out=gdec, in0=gdec, scalar=0.0, in1=gabs, op0=ALU.max, op1=ALU.add).then_inc(s_g.sem, 1)
            dve.wait_ge(s_g.sem, s_g.at(L, 2))
            stt(out=gdec, in0=gdec, scalar=-1.0, in1=over(nea.unsqueeze(1), [P, T, H]), op0=ALU.mult,
                op1=ALU.mult).then_inc(s_g.sem, 1)
            dve.wait_ge(s_g.sem, s_g.at(L, 3))
            v.tensor_copy(tmpA.rearrange("p t (h s) -> p t h s", h=H), over(gdec.unsqueeze(3), [P, T, H, P])
                          ).then_inc(s_g.sem, 1)

            def heads(ap):
                return ap.rearrange("p t (h n) -> p t h n", n=P)
            dve.wait_ge(s_ct.sem, s_ct.at(L, 3))
            for i in range(2):
                tt(kg, ct[:, :, i * 512:(i + 1) * 512], ct[:, :, i * 512:(i + 1) * 512], ALU.mult)
                dve.drain()
                last = v.tensor_reduce(ssq[:, :, 4 * i:4 * i + 4], heads(kg), AX.X, ALU.add)
                if i == 0:
                    dve.drain()
            last.then_inc(s_nsq.sem, 1)
            dve.wait_ge(s_nr.sem, L + 1)
            v.reciprocal(ssq, ssq)
            dve.drain()
            ts(ssq[:, :, 0:4], ssq[:, :, 0:4], float(128 ** -0.5), None, ALU.mult)
            dve.drain()
            qc, kc, vc = ct[:, :, 0:512], ct[:, :, 512:1024], ct[:, :, 1024:1536]

            def by_head(out, in0, scale, **kw):
                return tt(heads(out), heads(in0), over(scale.unsqueeze(3), [P, T, H, P]), ALU.mult)
            by_head(kc, kc, ssq[:, :, 4:8])
            by_head(qc, qc, ssq[:, :, 0:4]).then_inc(s_kqn.sem, 1)
            dve.drain()
            by_head(tmpk, kc, beta).then_inc(s_kb.sem, 1)
            by_head(vc, vc, beta)
            dve.wait_ge(s_gexp.sem, s_gexp.at(L, 2))
            twice_gated(br, br, ps[:, 4:6, :]).then_inc(s_pj_dve.sem, 1)
            dve.wait_ge(s_G.sem, s_G.at(L, 2))
            dve.wait_ge(s_tab.sem, 16)
            for t in range(T):
                dve.wait_ge(s_Gr_p.sem, s_Gr_p.at(L, t + 1))
                tt(decT[:, t], ps[:, 2 + t, :].rearrange("p (h n) -> p h n", h=H),
                   over(table("not_causal_big").unsqueeze(1), [P, 4, P]), ALU.subtract).then_inc(s_dm.sem, 1)
            tt(betaG, beta, expG[:, :, 0, :], ALU.mult)
            dve.drain()
            by_head(kg, kc, betaG)
            by_head(kd, kc, expG[:, :, 1, :])
            for t in range(T):
                dve.wait_ge(s_dec.sem, s_dec.at(L, t + 1))
                dve.wait_ge(s_A_p.sem, s_A_p.at(L, t + 1))
                tt(AT[:, t], ps[:, 2 + t, :].rearrange("p (h n) -> p h n", h=H), decT[:, t], ALU.mult
                   ).then_inc(s_A.sem, 1)
            dve.wait_ge(s_trc_p.sem, s_trc_p.at(L, 3))
            by_head(qc, qc, expG[:, :, 0, :]).then_inc(s_qd.sem, 1)
            for t in range(T):
                dve.wait_ge(s_at_p.sem, s_at_p.at(L, t + 1))
                tt(attG[:, t], ps[:, 4 + t, :].rearrange("p (h n) -> p h n", h=H), decT[:, t], ALU.mult
                   ).then_inc(s_at.sem, 1)
            def heads_of(bank):
                return ps[:, bank, :].rearrange("p (h n) -> p h n", h=H)

            def gla_log_a():
                dve.wait_ge(s_z.sem, s_z.at(L, 1))
                v.tensor_copy(la.rearrange("p t n -> p (t n)"), ps[:, 0, :])
                dve.drain()
                stt(out=zab, in0=la, scalar=-1.0, in1=la, op0=ALU.mult, op1=ALU.max).then_inc(s_z.sem, 1)

            for l in range(LEVELS):
                if l == LEVELS - 1:
                    gla_log_a()
                for t in range(T):
                    if l == 0:
                        idb = over(ident.unsqueeze(1), [P, 4, P])
                        dve.wait_ge(s_lv.sem, s_lv.at(L, t + 1))
                        tt(XT[:, t], idb, lower[:, t], ALU.subtract)
                        dve.wait_ge(s_P_p.sem, s_P_p.at(L, t + 1))
                        tt(X[:, t], idb, heads_of(2 + t), ALU.subtract).then_inc(s_X.sem, 1)
                        continue
                    dve.wait_ge(s_D_p.sem, s_D_p.at(L, 2 * (l - 1) + t + 1))
                    if l < LEVELS - 1:
                        tt(X[:, t], X[:, t], heads_of(6 + t), ALU.subtract)
                    tt(XT[:, t], XT[:, t], heads_of(4 + t), ALU.subtract).then_inc(s_X.sem, 1)
                dve.drain()
            def scan_v(n):
                t, r = n // 2, CHUNK * (n % 2)
                rs = slice(r, r + CHUNK)
                if n == 0:
                    dve.wait_ge(s_wu_p.sem, s_wu_p.at(L, 1))
                    v.tensor_copy(vnew[rs, t, :], ps[rs, 4, :]).then_inc(s_vn.sem, 1)
                else:
                    dve.wait_ge(s_ws.sem, s_ws.at(L, n))
                    tt(vnew[rs, t, :], u[rs, t, :], ps[rs, 6, :], ALU.subtract).then_inc(s_vn.sem, 1)

            def scan_S(n):
                t = n // 2
                dve.wait_ge(s_ds.sem, s_ds.at(L, n + 1))
                new = ps[:, 7, :].rearrange("p (h n) -> p h n", h=H)
                if n == 0:
                    v.tensor_copy(Sc, new).then_inc(s_S.sem, 1)
                else:
                    tt(Sc, Sc, over(expG[:, t, 2 + n % 2, :].unsqueeze(2), [P, H, P]), ALU.mult)
                    dve.drain()
                    tt(Sc, Sc, new, ALU.add).then_inc(s_S.sem, 1)
                dve.drain()

            diag = over(table("pair_diag").unsqueeze(1), [P, 2, 256])

            def gla_state(n):
                t = n // 2
                dve.wait_ge(s_du_p.sem, s_du_p.at(L, n + 1))
                new = ps[:, 1 - n % 2, :].rearrange("p (g n) -> p g n", g=2)
                if n == 0:
                    tt(Sb[:, 0], new, diag, ALU.mult).then_inc(s_Sb.sem, 1)
                else:
                    tt(dum, new, diag, ALU.mult)
                    dve.drain()
                    for g in range(2):
                        last = stt(out=Sb[:, n, g, :], in0=Sb[:, n - 1, g, :], scalar=decB[:, g, t, n % 2:n % 2 + 1],
                                   in1=dum[:, g, :], op0=ALU.mult, op1=ALU.add)
                    last.then_inc(s_Sb.sem, 1)
                dve.drain()

            scan_v(0)
            dve.wait_ge(s_la.sem, s_la.at(L, 1))
            stt(out=la, in0=la, scalar=0.0, in1=zab, op0=ALU.min, op1=ALU.subtract).then_inc(s_la.sem, 1)
            dve.wait_ge(s_la.sem, s_la.at(L, 2))
            ts(la, la, 1.0 / 16.0, None, ALU.mult).then_inc(s_lar.sem, 1)
            scan_S(0)
            scan_v(1)
            scan_S(1)
            dve.wait_ge(s_b.sem, L + 1)
            stt(out=qe, in0=bt[:, :, 0:256], scalar=float(DK_B ** -0.5), in1=eb, op0=ALU.mult, op1=ALU.mult)
            tt(ke, bt[:, :, 256:512], enb, ALU.mult)
            tt(kdb, bt[:, :, 256:512], ea, ALU.mult).then_inc(s_qke.sem, 1)
            gla_state(0)
            scan_v(2)
            scan_S(2)
            gla_state(1)
            scan_v(3)
            for odd in range(2):
                dve.wait_ge(s_ab_p.sem, s_ab_p.at(L, odd + 1))
                tt(attB.rearrange("p t (g e) n -> p t g e n", e=2)[:, :, :, odd, :],
                   ps[:, 4 + odd, :].rearrange("p (t g n) -> p t g n", t=T, g=2),
                   over(causal.unsqueeze(1).unsqueeze(1), [P, T, 2, P]), ALU.mult).then_inc(s_ab.sem, 1)
            gla_state(2)

            def head_norm(n, bank, gate, gain):
                y = y_of[n]
                tt(heads(gate), heads(gate), over(row(gain).unsqueeze(1).unsqueeze(1), [P, T, H, P]), ALU.mult)
                dve.wait_ge(s_onr.sem, s_onr.at(L, n + 1))
                v.reciprocal(rmso[:, n], rmso[:, n])
                dve.drain()
                by_head(y, ps[:, bank:bank + 2, :], rmso[:, n])
                dve.drain()
                tt(y, y, gate, ALU.mult).then_inc(s_y.sem, 1)

            def merge(i):
                f, t = (i % 4) // 2, i % 2
                e = tmpA[:, t, :]
                dve.wait_ge(s_gt_e.sem, s_gt_e.at(L, i + 1))
                dst = merged[:, t, f * 512:(f + 1) * 512]
                if i < 4:
                    twice_gated(dst, e, ps[:, 2 + t, :]).then_inc(s_mg.sem, 1)
                else:
                    twice_gated(e, e, ps[:, 2 + t, :])
                    dve.drain()
                    tt(dst, dst, e, ALU.add).then_inc(s_mg.sem, 1)

            head_norm(0, 2, cg, "gdn_norm")
            head_norm(1, 4, br, "gla_norm")
            qk = aq[:, :, 0:QK_A].rearrange("p t (h n) -> p t h n", n=HD_A)
            sq = scores.rearrange("p h n -> p (h n)")[:, 0:T * QK_A].rearrange("p (t h n) -> p t h n", t=T, n=HD_A)
            tt(sq, qk, qk, ALU.mult)
            dve.drain()
            v.tensor_reduce(ssa, sq, AX.X, ALU.add).then_inc(s_asq.sem, 1)
            dve.wait_ge(s_ar.sem, L + 1)
            v.reciprocal(ssa, ssa)
            dve.drain()
            tt(qk, qk, over(ssa.unsqueeze(3), [P, T, 10, HD_A]), ALU.mult)
            dve.drain()
            tt(aq[:, :, 0:QK_A], aq[:, :, 0:QK_A], over(row("qk_gain").unsqueeze(1), [P, T, QK_A]), ALU.mult)
            dve.drain()
            cos = over(cossin[:, 0].unsqueeze(2), [P, T, 10, HALF])
            sin = over(cossin[:, 1].unsqueeze(2), [P, T, 10, HALF])
            x1, x2 = qk[:, :, :, 0:HALF], qk[:, :, :, HALF:ROT]
            tt(so2[:, 0], x1, cos, ALU.mult)
            tt(so2[:, 1], x2, sin, ALU.mult)
            tt(so2[:, 2], x2, cos, ALU.mult)
            tt(ra, x1, sin, ALU.mult)
            dve.drain()
            tt(x1, so2[:, 0], so2[:, 1], ALU.subtract)
            tt(x2, so2[:, 2], ra, ALU.add)
            dve.drain()
            v.tensor_copy(kswap[:, :, 0:64], aq[:, :, 576:640])
            v.tensor_copy(kswap[:, :, 64:128], aq[:, :, 512:576]).then_inc(s_ak.sem, 1)
            for i in range(4):
                merge(i)
            sc = float(HD_A ** -0.5)
            dve.wait_ge(s_sc_p.sem, s_sc_p.at(L, 1))
            for odd in range(2):
                last = stt(out=scores[:, odd:HEADS_A:2, 0:P], in0=ps[:, 4 + odd, :].rearrange("p (h n) -> p h n", n=P),
                           scalar=sc, in1=over(table("swa0").unsqueeze(1), [P, 4, P]), op0=ALU.mult, op1=ALU.add)
            last.then_inc(s_sc.sem, 1)
            merge(4)
            merge(5)
            dve.wait_ge(s_sc_p.sem, s_sc_p.at(L, 2))
            for odd, b in enumerate((6, 4)):
                last = stt(out=scores[:, odd:HEADS_A:2, P:3 * P],
                           in0=ps[:, b:b + 2, :].rearrange("p a (h n) -> p (a h) n", n=SEQ), scalar=sc,
                           in1=over(table("swa1").unsqueeze(1), [P, 4, SEQ]), op0=ALU.mult, op1=ALU.add)
            last.then_inc(s_sc.sem, 1)
            dve.drain()
            v.tensor_reduce(mx[:, 0, :], scores[:, :, 0:P], AX.X, ALU.max)
            v.tensor_reduce(mx[:, 1, :], scores[:, :, P:3 * P], AX.X, ALU.max)
            dve.drain()
            sink = over(row("sinks").unsqueeze(1), [P, T, HEADS_A])
            tt(mx, mx, sink, ALU.max)
            dve.drain()
            tt(esink, sink, mx, ALU.subtract)
            tt(scores[:, :, 0:P], scores[:, :, 0:P], over(mx[:, 0, :].unsqueeze(2), [P, 8, P]), ALU.subtract)
            tt(scores[:, :, P:3 * P], scores[:, :, P:3 * P], over(mx[:, 1, :].unsqueeze(2), [P, 8, SEQ]),
               ALU.subtract).then_inc(s_sx.sem, 1)
            merge(6)
            dve.wait_ge(s_pe.sem, L + 1)
            v.tensor_reduce(den[:, 0, :], scores[:, :, 0:P], AX.X, ALU.add)
            v.tensor_reduce(den[:, 1, :], scores[:, :, P:3 * P], AX.X, ALU.add)
            dve.drain()
            tt(den, den, esink, ALU.add)
            dve.drain()
            v.reciprocal(den, den)
            dve.drain()
            merge(7)
            for t in range(T):
                dve.wait_ge(s_pv.sem, s_pv.at(L, t + 1))
                for kv in range(KV_A):
                    last = tt(y_of[2][:, t, kv * 256:(kv + 1) * 256].rearrange("p (h n) -> p h n", n=HD_A),
                              ps[:, 4 + 2 * t + kv, :].rearrange("p (h n) -> p h n", n=P)[:, :, kv * HD_A:(kv + 1) * HD_A],
                              over(den[:, t, 4 * kv:4 * kv + 4].unsqueeze(2), [P, 4, HD_A]), ALU.mult)
            last.then_inc(s_y.sem, 1)
            for i in range(8, 12):
                merge(i)
            dve.drain()
            for i in range(4):
                f, t = divmod(i, 2)
                if t == 0:
                    dve.wait_ge(s_wo.sem, s_wo.at(L, f + 1))
                else:
                    dve.wait_ge(s_static_used.sem, chunk_used(L, J_WO0 + f))
                last = tt(x[:, t, f * 512:(f + 1) * 512], x[:, t, f * 512:(f + 1) * 512], ps[:, i, :], ALU.add)
                if f == 1:
                    last.then_inc(s_x.sem, 1)
            take_hT(1, "ffn_norm")
            for t in range(T):
                normed(1, t)
            dve.wait_ge(s_static_used.sem, chunk_used(L, J_ROUTER))
            for t in range(T):
                stt(out=lg[:, t, :], in0=ps[:, 6, 64 * t:64 * t + 36], scalar=rstd[:, t:t + 1], in1=row("b_router"),
                    op0=ALU.mult, op1=ALU.add)
            dve.drain()
            gl = lg[:, :, 0:GROUPS]
            v.tensor_reduce(gmx, gl, AX.X, ALU.max)
            dve.drain()

            def first_max(dst, vals, top, desc):
                for t in range(T):
                    stt(out=dst[:, t, :], in0=vals[:, t, :], scalar=top[:, t:t + 1], in1=desc, op0=ALU.is_equal,
                        op1=ALU.mult)
                dve.drain()
                v.tensor_reduce(pk, dst, AX.X, ALU.max)
                dve.drain()
                tt(dst, dst, over(pk.unsqueeze(2), [P, T, E]), ALU.is_equal)
                dve.drain()
            for t in range(T):
                stt(out=oh_g[:, t, :], in0=gl[:, t, :], scalar=gmx[:, t:t + 1], in1=table("desc4"), op0=ALU.is_equal,
                    op1=ALU.mult)
            dve.drain()
            v.tensor_reduce(pk, oh_g, AX.X, ALU.max)
            tt(gl, gl, over(gmx.unsqueeze(2), [P, T, GROUPS]), ALU.subtract).then_inc(s_rt.sem, 1)
            dve.drain()
            tt(oh_g, oh_g, over(pk.unsqueeze(2), [P, T, GROUPS]), ALU.is_equal)
            dve.drain()
            ts(msk_g, oh_g, BIG, -BIG, ALU.mult, ALU.add)
            fine = lg[:, :, GROUPS:36].rearrange("p t (g n) -> p t g n", g=GROUPS)
            fm4 = fm.rearrange("p t (g n) -> p t g n", g=GROUPS)
            dve.drain()
            tt(fm4, fine, over(msk_g.unsqueeze(3), [P, T, GROUPS, PER_GROUP]), ALU.add)
            dve.drain()
            v.tensor_reduce(m1, fm, AX.X, ALU.max)
            dve.drain()
            first_max(oh1, fm, m1, table("desc32"))
            stt(out=fm, in0=oh1, scalar=-2 * BIG, in1=fm, op0=ALU.mult, op1=ALU.add)
            dve.drain()
            v.tensor_reduce(m2, fm, AX.X, ALU.max)
            dve.drain()
            tt(e2, m2, m1, ALU.subtract).then_inc(s_rt.sem, 1)
            first_max(oh2, fm, m2, table("desc32"))
            tt(chosen, oh1, oh2, ALU.add).then_inc(s_ch.sem, 1)
            dve.wait_ge(s_pos_p.sem, L + 1)
            away = 10000.0
            stt(out=posm, in0=ps[:, 7, 0:2 * E].rearrange("p (t n) -> p t n", t=T), scalar=away, in1=chosen,
                op0=ALU.add, op1=ALU.mult)
            v.tensor_copy(counts, ps[:, 7, 2 * E:3 * E])
            dve.drain()
            ts(posm, posm, away, None, ALU.subtract)
            c2v = counts.rearrange("p (a j) -> p a j", j=2)
            tt(rtmp, c2v[:, :, 0], c2v[:, :, 1], ALU.max)
            dve.drain()

            def select(dst, pair, offset):
                for t in range(T):
                    last = stt(out=dst[:, t], in0=over(posm[:, t, bass.ds(pair * 2, 2)].unsqueeze(2), [P, 2, CAP]),
                               scalar=offset, in1=over(table("iota64").unsqueeze(1), [P, 2, CAP]),
                               op0=ALU.subtract, op1=ALU.is_equal)
                return last
            select(sel, 0, 0.0).then_inc(s_sel0.sem, 1)
            more = cmp3.rearrange("p g i -> p (g i)")[:, 0:PAIRS * (SEQ // CAP - 1)].rearrange("p (a n) -> p a n", a=PAIRS)
            stt(out=more, in0=over(rtmp.unsqueeze(2), [P, PAIRS, SEQ // CAP - 1]), scalar=1.0 / CAP,
                in1=over(table("iota32")[:, 1:SEQ // CAP].unsqueeze(1), [P, PAIRS, SEQ // CAP - 1]),
                op0=ALU.mult, op1=ALU.is_gt)
            dve.drain()
            v.tensor_reduce(rtmp, more, AX.X, ALU.add)
            dve.drain()
            ts(rounds, rtmp, 1.0, None, ALU.add)
            up_to = cmp3[:, 0:PAIRS, :]
            stt(out=up_to, in0=over(rtmp.unsqueeze(1), [P, PAIRS, PAIRS]), scalar=1.0,
                in1=table("up_to").rearrange("p (a b) -> p a b", a=PAIRS), op0=ALU.add, op1=ALU.mult)
            dve.drain()
            v.tensor_reduce(cum, up_to, AX.X, ALU.add)
            dve.drain()
            ts(row_f[:, BEFORE + 1:BEFORE + PAIRS + 1], cum, base_f[:, 0:1], None, ALU.add)
            v.tensor_copy(row_f[:, BEFORE:BEFORE + 1], base_f[:, :])
            v.tensor_copy(row_f[:, ROUNDS_AT:ROUNDS_AT + 1], cum[:, PAIRS - 1:PAIRS])
            dve.drain()
            v.tensor_copy(tbl[0:1, bass.ds(L * 64 + BEFORE, PAIRS + 2)], row_f[0:1, BEFORE:BEFORE + PAIRS + 2])
            tt(base_f[:, :], base_f[:, :], cum[:, PAIRS - 1:PAIRS], ALU.add)
            dve.drain().then_inc(s_tbl.sem, 1)

            def take_gathered():
                for half in range(2):
                    last = tt(xgT[:, 4 * half:4 * half + 4, :], ps[:, 4 + half, :].rearrange("p (k n) -> p k n", k=4),
                              over(col("ffn_norm")[:, 4 * half:4 * half + 4].unsqueeze(2), [P, 4, P]), ALU.mult)
                last.then_inc(s_xg.sem, 1)

            dve.wait_ge(s_ga0.sem, L + 1)
            take_gathered()
            tt(cmp3, over(table("iota32").unsqueeze(2), [P, ROUNDS_MAX, PAIRS]),
               over(cum.unsqueeze(1), [P, ROUNDS_MAX, PAIRS]), ALU.is_ge)
            dve.drain()
            v.tensor_reduce(pair_f, cmp3, AX.X, ALU.add)
            dve.drain()
            tt(cmp3, cmp3, over(rounds.unsqueeze(1), [P, ROUNDS_MAX, PAIRS]), ALU.mult)
            ts(row_f[:, 0:ROUNDS_MAX], pair_f, float(PAIRS - 1), None, ALU.min)
            dve.drain()
            v.tensor_copy(tbl[0:1, bass.ds(L * 64, ROUNDS_MAX)], row_f[0:1, 0:ROUNDS_MAX])
            v.tensor_reduce(off_f, cmp3, AX.X, ALU.add)
            dve.drain()
            tt(off_f, table("iota32"), off_f, ALU.subtract)
            dve.drain()
            ts(off_f, off_f, float(CAP), None, ALU.mult)
            dve.wait_ge(s_rte.sem, s_rte.at(L, 2))
            v.tensor_reduce(gsum, gl, AX.X, ALU.add)
            ts(w1, e2, 1.0, None, ALU.add)
            dve.drain()
            tt(w1, w1, gsum, ALU.mult)
            dve.drain()
            v.reciprocal(w1, w1)
            dve.drain()
            tt(w2, w1, e2, ALU.mult)
            tt(wts, oh1, over(w1.unsqueeze(2), [P, T, E]), ALU.mult)
            dve.drain()
            tt(tmpe, oh2, over(w2.unsqueeze(2), [P, T, E]), ALU.mult)
            dve.drain()
            tt(wts, wts, tmpe, ALU.add)
            dve.drain().then_inc(s_pairs.sem, 1)
            dve.wait_ge(s_pairs.sem, L + 1)
            n_rounds = plan(dve, L, ROUNDS_AT, PAIRS, ROUNDS_LIMIT)
            base = plan(dve, L, BEFORE, 0, 4096)

            with dve.Fori(0, n_rounds) as g:
                gg = base + g
                dve.drain()
                pair = plan(dve, L, g, 0, PAIRS - 1)
                nxt = plan(dve, L, g + 1, 0, PAIRS - 1)
                dve.wait_ge(s_swT_p.sem, gg + 1)
                select(selw, pair, off_f[:, bass.ds(g, 1)])
                dve.wait_ge(s_ga.sem, gg + 1)
                select(sel, nxt, off_f[:, bass.ds(g + 1, 1)]).then_inc(s_sel.sem, 1)
                dve.drain()
                tt(selw, selw, over(wts[:, :, bass.ds(pair * 2, 2)].unsqueeze(3), [P, T, 2, CAP]), ALU.mult
                   ).then_inc(s_selw.sem, 1)
                dve.wait_ge(s_sig.sem, gg + 1)
                twice_gated(act_h, sig, ps[:, 6, :])
                dve.drain()
                dve.wait_ge(s_up.sem, gg + 1)
                stt(out=act_h, in0=act_h, scalar=0.5, in1=ps[:, 7, :], op0=ALU.mult, op1=ALU.mult
                    ).then_inc(s_act.sem, 1)
                dve.wait_ge(s_ga.sem, gg + 2)
                take_gathered()
            dve.wait_ge(s_acc.sem, L + 1)
            for t in range(T):
                tt(x[:, t, :].rearrange("p (f n) -> p f n", f=2), x[:, t, :].rearrange("p (f n) -> p f n", f=2),
                   ps[:, 2 * t:2 * t + 2, :], ALU.add).then_inc(s_x.sem, 1)
            take_hT(2, "ple_norm")
            reciprocal_rms(2).then_inc(s_rs.sem, 1)
            dve.drain().then_inc(s_par_used.sem, 1)
            for i in range(4):
                f, t = divmod(i, 2)
                e = gtmp[:, i % 2, :]
                dve.wait_ge(s_pg_e.sem, s_pg_e.at(L, i + 1))
                twice_gated(e, e, ps[:, 2 * (i % 2) + 1, :])
                dve.drain()
                xs = x[:, t, f * 512:(f + 1) * 512]
                stt(out=xs, in0=e, scalar=0.5, in1=xs, op0=ALU.mult, op1=ALU.add).then_inc(s_pg.sem, 1)


def kernel(**inputs):
    import concourse.bacc as bacc
    from concourse.bass_utils import run_bass_kernel_spmd

    i = {k: np.asarray(v) for k, v in inputs.items()}
    L = i["w_in"].shape[0]

    def by_feature(g):
        return g.reshape(L, P, -1)

    conv = i["gdn_conv"].transpose(0, 2, 1).reshape(L, 12, P, 4).transpose(0, 2, 1, 3).reshape(L, P, 48)
    arrays = {
        "x": i["x"].reshape(SEQ, D),
        "p": i["p"].reshape(L, SEQ, PLE),
        "positions": i["positions"].reshape(SEQ),
        "tables": TABLES,
        "cols": np.concatenate([by_feature(i["attn_norm"]), by_feature(i["ffn_norm"]), by_feature(i["ple_norm"]),
                                conv], -1),
        "rows": np.concatenate([np.tile(i["q_norm"], (1, HEADS_A)), np.tile(i["k_norm"], (1, KV_A)), i["gla_norm"],
                                i["gdn_norm"], i["sinks"], i["gdn_dt_bias"], i["gdn_a_log"], i["b_coarse"],
                                i["b_fine"]], -1),
        "wa2": np.concatenate([i["gla_wa2"], i["gla_ba"][:, None, :]], 1),
        "w_router": np.concatenate([i["w_coarse"], i["w_fine"]], -1),
    }
    for name in ("w_in", "w_br_a", "w_br_b", "w_br_c", "w_o", "w_gate_e", "w_up_e", "w_down_e", "w_ple_gate",
                 "w_ple"):
        arrays[name] = i[name]
    nc = bacc.Bacc("TRN2", target_bir_lowering=False, num_devices=1)
    a = {"x_layers": L}
    feed = {}
    for name, v in arrays.items():
        v = np.ascontiguousarray(v)
        feed[f"in_{name}"] = v
        a[name] = nc.dram_tensor(f"in_{name}", v.shape, mybir.dt.from_np(v.dtype), kind="ExternalInput").ap()
    a["out"] = nc.dram_tensor("out_x", (SEQ, D), F32, kind="ExternalOutput").ap()
    build(nc, a)
    r = run_bass_kernel_spmd(nc, [feed], core_ids=[0])
    return r.results[0]["out_x"].reshape(inputs["x"].shape)
```
